# Optimizing a Trainium2 kernel written in Bass

```python
import jax, jax.numpy as jnp
from jax import lax
import numpy as np

D_MODEL = 1024
BATCH = 1
SEQ = 256
DEPTH = 1

RET_HEADS = D_MODEL // 256
RET_QK_DIM = D_MODEL
RET_V_DIM = 2 * D_MODEL
RET_HEAD_QK = RET_QK_DIM // RET_HEADS
RET_HEAD_V = RET_V_DIM // RET_HEADS
RET_CHUNK = 128
ROPE_BASE = 10000.0
GN_EPS = 1e-5
CONV_DIM = D_MODEL
CONV_WIDTH = 31
LN_EPS = 1e-5
RMS_EPS = 1e-6
IN_SPLITS = (RET_QK_DIM, RET_QK_DIM, RET_V_DIM, RET_V_DIM, CONV_DIM, CONV_DIM, CONV_DIM, D_MODEL, D_MODEL)
IN_WIDTH = sum(IN_SPLITS)


def rmsnorm(x, g):
    xf = x.astype(jnp.float32)
    y = xf * lax.rsqrt(jnp.mean(xf * xf, axis=-1, keepdims=True) + RMS_EPS)
    return (y * g.astype(jnp.float32)).astype(x.dtype)

def layernorm(x, g, b):
    xf = x.astype(jnp.float32)
    mu = jnp.mean(xf, axis=-1, keepdims=True)
    var = jnp.mean(jnp.square(xf - mu), axis=-1, keepdims=True)
    y = (xf - mu) * lax.rsqrt(var + LN_EPS)
    return (y * g.astype(jnp.float32) + b.astype(jnp.float32)).astype(x.dtype)

def head_groupnorm(o):
    of = o.astype(jnp.float32)
    mu = jnp.mean(of, axis=-1, keepdims=True)
    var = jnp.mean(jnp.square(of - mu), axis=-1, keepdims=True)
    return (of - mu) * lax.rsqrt(var + GN_EPS)

def rotary(t, positions):
    dh = t.shape[-1]
    half = dh // 2
    inv_freq = ROPE_BASE ** (-jnp.arange(half, dtype=jnp.float32) / half)
    ang = positions.astype(jnp.float32)[..., None] * inv_freq
    cos = jnp.cos(ang)[:, :, None, :]
    sin = jnp.sin(ang)[:, :, None, :]
    t1, t2 = t[..., :half], t[..., half:]
    return jnp.concatenate([t1 * cos - t2 * sin, t1 * sin + t2 * cos], axis=-1)

def retention_chunkwise(q, k, v):
    B, S, H, dk = q.shape
    dv = v.shape[-1]
    C = RET_CHUNK
    N = S // C
    log_g = jnp.log1p(-jnp.exp2(-5.0 - jnp.arange(H, dtype=jnp.float32)))
    idx = jnp.arange(C, dtype=jnp.float32)
    diff = idx[:, None] - idx[None, :]
    causal = diff >= 0
    decay_mask = jnp.where(causal, jnp.exp(log_g[:, None, None] * jnp.where(causal, diff, 0.0)), 0.0)
    xi = jnp.exp(log_g[:, None] * (idx + 1.0))
    zeta = jnp.exp(log_g[:, None] * (C - 1.0 - idx))
    g_chunk = jnp.exp(log_g * C)

    def to_chunks(t):
        return t.reshape(B, N, C, H, t.shape[-1]).transpose(1, 0, 3, 2, 4)

    def step(state, inp):
        qc, kc, vc = inp
        scores = jnp.einsum('bhid,bhjd->bhij', qc, kc) * decay_mask[None]
        inner = jnp.einsum('bhij,bhje->bhie', scores, vc)
        cross = jnp.einsum('bhid,bhde->bhie', qc, state) * xi[None, :, :, None]
        new_state = state * g_chunk[None, :, None, None] + jnp.einsum(
            'bhjd,bhje->bhde', kc * zeta[None, :, :, None], vc)
        return new_state, inner + cross

    state0 = jnp.zeros((B, H, dk, dv), jnp.float32)
    _, o = lax.scan(step, state0, (to_chunks(q), to_chunks(k), to_chunks(v)))
    return o.transpose(1, 0, 3, 2, 4).reshape(B, S, H, dv)

def causal_depthwise_conv(u, w, b):
    out = lax.conv_general_dilated(
        u, w[:, None, :].astype(u.dtype), window_strides=(1,),
        padding=[(CONV_WIDTH - 1, 0)],
        dimension_numbers=('NWC', 'WIO', 'NWC'),
        feature_group_count=u.shape[-1])
    return out + b.astype(u.dtype)

def first_inputs(seed: int = 0) -> dict:
    key = jax.random.key(seed)
    ks = jax.random.split(key, 16)
    f32 = jnp.float32
    x = jax.random.normal(ks[0], (BATCH, SEQ, D_MODEL), f32)
    c = jax.random.normal(ks[1], (BATCH, D_MODEL), f32)
    offsets = jax.random.randint(ks[2], (BATCH, 1), 0, 4096, dtype=jnp.int32)
    positions = offsets + jnp.arange(SEQ, dtype=jnp.int32)[None, :]
    w_ada = jax.random.normal(ks[3], (DEPTH, D_MODEL, 3 * D_MODEL), f32) * (0.1 * D_MODEL ** -0.5)
    b_ada = jax.random.normal(ks[4], (DEPTH, 3 * D_MODEL), f32) * 0.02
    pre_norm_g = 1.0 + 0.05 * jax.random.normal(ks[5], (DEPTH, D_MODEL), f32)
    w_in = jax.random.normal(ks[6], (DEPTH, D_MODEL, IN_WIDTH), f32) * D_MODEL ** -0.5
    conv_w = jax.random.normal(ks[7], (DEPTH, CONV_WIDTH, CONV_DIM), f32) * CONV_WIDTH ** -0.5
    conv_b = jax.random.normal(ks[8], (DEPTH, CONV_DIM), f32) * 0.02
    conv_ln_g = 1.0 + 0.05 * jax.random.normal(ks[9], (DEPTH, CONV_DIM), f32)
    conv_ln_b = jax.random.normal(ks[10], (DEPTH, CONV_DIM), f32) * 0.02
    w_ret_out = jax.random.normal(ks[11], (DEPTH, RET_V_DIM, D_MODEL), f32) * RET_V_DIM ** -0.5
    w_conv_out = jax.random.normal(ks[12], (DEPTH, CONV_DIM, D_MODEL), f32) * CONV_DIM ** -0.5
    w_out = jax.random.normal(ks[13], (DEPTH, D_MODEL, D_MODEL), f32) * D_MODEL ** -0.5
    post_norm_g = 1.0 + 0.05 * jax.random.normal(ks[14], (DEPTH, D_MODEL), f32)
    return {"x": x, "c": c, "positions": positions, "w_ada": w_ada, "b_ada": b_ada,
            "pre_norm_g": pre_norm_g, "w_in": w_in, "conv_w": conv_w, "conv_b": conv_b,
            "conv_ln_g": conv_ln_g, "conv_ln_b": conv_ln_b, "w_ret_out": w_ret_out,
            "w_conv_out": w_conv_out, "w_out": w_out, "post_norm_g": post_norm_g}

def first_block(x, c, positions, w_ada, b_ada, pre_norm_g, w_in, conv_w, conv_b,
              conv_ln_g, conv_ln_b, w_ret_out, w_conv_out, w_out, post_norm_g):
    B, S, _ = x.shape
    split_at = [int(v) for v in np.cumsum(IN_SPLITS)[:-1]]
    for l in range(DEPTH):
        mod = c @ w_ada[l] + b_ada[l]
        shift, scale, gate = jnp.split(mod, 3, axis=-1)
        h = rmsnorm(x, pre_norm_g[l]) * (1.0 + scale[:, None, :]) + shift[:, None, :]

        proj = h @ w_in[l]
        q, k, v, z_ret, u_val, u_gate, z_conv, g_a, g_b = jnp.split(proj, split_at, axis=-1)

        qh = rotary(q.reshape(B, S, RET_HEADS, RET_HEAD_QK).astype(jnp.float32), positions)
        kh = rotary(k.reshape(B, S, RET_HEADS, RET_HEAD_QK).astype(jnp.float32), positions) * RET_HEAD_QK ** -0.5
        vh = v.reshape(B, S, RET_HEADS, RET_HEAD_V).astype(jnp.float32)
        ret = head_groupnorm(retention_chunkwise(qh, kh, vh)).reshape(B, S, RET_V_DIM).astype(x.dtype)
        y_a = (ret * jax.nn.silu(z_ret)) @ w_ret_out[l]

        a = u_val * jax.nn.sigmoid(u_gate)
        a = causal_depthwise_conv(a, conv_w[l], conv_b[l])
        a = jax.nn.silu(layernorm(a, conv_ln_g[l], conv_ln_b[l]))
        y_b = (a * jax.nn.silu(z_conv)) @ w_conv_out[l]

        merged = jax.nn.sigmoid(g_a) * y_a + jax.nn.sigmoid(g_b) * y_b
        y = merged @ w_out[l]

        x = x + gate[:, None, :] * rmsnorm(y, post_norm_g[l])
    return x


HG_WIDTH = D_MODEL // 2
HG_HEAD_DIM = 128
HG_HEADS = HG_WIDTH // HG_HEAD_DIM
ML_WIDTH = D_MODEL - HG_WIDTH
ML_V_DIM = 128
ML_HEADS = ML_WIDTH // ML_V_DIM
ML_QK_DIM = ML_V_DIM // 2
D_MIX = HG_WIDTH + ML_WIDTH
CONV_WIDTH_2 = 4
D_FF = 2816
CHUNK = 64
EPS = 1e-6
SPLIT_SIZES = (HG_WIDTH, HG_WIDTH, HG_WIDTH, HG_WIDTH,
               ML_HEADS * ML_QK_DIM, ML_HEADS * ML_QK_DIM,
               ML_WIDTH, ML_WIDTH,
               ML_HEADS, ML_HEADS)
D_IN = 4 * HG_WIDTH + 2 * ML_HEADS * ML_QK_DIM + 2 * ML_WIDTH + 2 * ML_HEADS


def rms_norm(x, g):
    xf = x.astype(jnp.float32)
    y = xf * lax.rsqrt(jnp.mean(xf * xf, axis=-1, keepdims=True) + EPS)
    return (y * g.astype(jnp.float32)).astype(x.dtype)

def swiglu_ffn(x, w_in, w_out):
    gate, up = jnp.split(x @ w_in, 2, axis=-1)
    return (jax.nn.silu(gate) * up) @ w_out

def split_cols(x, sizes):
    outs, start = [], 0
    for s in sizes:
        outs.append(x[..., start:start + s])
        start += s
    return outs

def causal_depthwise_conv_2(x, w, b):
    y = lax.conv_general_dilated(
        x, w[:, None, :].astype(x.dtype), window_strides=(1,),
        padding=[(CONV_WIDTH_2 - 1, 0)], dimension_numbers=("NWC", "WIO", "NWC"),
        feature_group_count=x.shape[-1])
    return y + b.astype(x.dtype)

def to_chunks(x):
    B, T, H, d = x.shape
    return x.reshape(B, T // CHUNK, CHUNK, H, d).transpose(1, 0, 3, 2, 4)

def scalar_to_chunks(x):
    B, T, H = x.shape
    return x.reshape(B, T // CHUNK, CHUNK, H).transpose(1, 0, 3, 2)

def from_chunks(y):
    NC, B, H, L, d = y.shape
    return y.transpose(1, 0, 3, 2, 4).reshape(B, NC * L, H, d)

def hgrn2_chunkwise(q, k, v, log_f):
    B, T, H, dk = q.shape
    dv = v.shape[-1]
    causal = jnp.tril(jnp.ones((CHUNK, CHUNK), dtype=bool))[:, :, None]

    def step(S, inp):
        qc, kc, vc, gc = inp
        G = jnp.cumsum(gc, axis=2)
        o_inter = jnp.einsum("bhtk,bhkv->bhtv", qc * jnp.exp(G), S)
        rel = G[:, :, :, None, :] - G[:, :, None, :, :]
        decay = jnp.exp(jnp.where(causal, rel, -jnp.inf))
        scores = jnp.sum(qc[:, :, :, None, :] * kc[:, :, None, :, :] * decay, axis=-1)
        o = o_inter + jnp.einsum("bhts,bhsv->bhtv", scores, vc)
        G_end = G[:, :, -1:, :]
        S_new = jnp.exp(G_end[:, :, 0, :])[..., None] * S + jnp.einsum(
            "bhsk,bhsv->bhkv", kc * jnp.exp(G_end - G), vc)
        return S_new, o

    S0 = jnp.zeros((B, H, dk, dv), jnp.float32)
    _, o = lax.scan(step, S0, (to_chunks(q), to_chunks(k), to_chunks(v), to_chunks(log_f)))
    return from_chunks(o)

def mlstm_chunkwise(q, k, v, log_i, log_f):
    B, T, H, dqk = q.shape
    dv = v.shape[-1]
    causal = jnp.tril(jnp.ones((CHUNK, CHUNK), dtype=bool))

    def step(carry, inp):
        C, n, m = carry
        qc, kc, vc, ic, fc = inp
        b = jnp.cumsum(fc, axis=-1)
        a = b + m[..., None]
        D = jnp.where(causal, b[..., :, None] - b[..., None, :] + ic[..., None, :], -jnp.inf)
        m_t = jnp.maximum(a, jnp.max(D, axis=-1))
        inter = jnp.exp(a - m_t)
        P = jnp.einsum("bhtd,bhsd->bhts", qc, kc) * jnp.exp(D - m_t[..., None])
        num = inter[..., None] * jnp.einsum("bhtd,bhdv->bhtv", qc, C) + jnp.einsum("bhts,bhsv->bhtv", P, vc)
        den = inter * jnp.einsum("bhtd,bhd->bht", qc, n) + jnp.sum(P, axis=-1)
        h = num / jnp.maximum(jnp.abs(den), jnp.exp(-m_t))[..., None]
        m_new = m_t[..., -1]
        w = jnp.exp(b[..., -1:] - b + ic - m_new[..., None])
        keep = inter[..., -1]
        C_new = keep[..., None, None] * C + jnp.einsum("bhs,bhsd,bhsv->bhdv", w, kc, vc)
        n_new = keep[..., None] * n + jnp.einsum("bhs,bhsd->bhd", w, kc)
        return (C_new, n_new, m_new), h

    init = (jnp.zeros((B, H, dqk, dv), jnp.float32), jnp.zeros((B, H, dqk), jnp.float32),
            jnp.zeros((B, H), jnp.float32))
    _, h = lax.scan(step, init, (to_chunks(q), to_chunks(k), to_chunks(v),
                                 scalar_to_chunks(log_i), scalar_to_chunks(log_f)))
    return from_chunks(h)

def token_mixer(h, w_in, conv_w, conv_b, gate_bias, lb, hg_norm, ml_norm, w_out):
    B, T, _ = h.shape
    f32 = jnp.float32
    hq, hf, hi, hgate, mq, mk, mv, mo, mig, mfg = split_cols(h @ w_in, SPLIT_SIZES)
    hs = (B, T, HG_HEADS, HG_HEAD_DIM)
    lbh = lb.reshape(HG_HEADS, HG_HEAD_DIM)
    forget = lbh + (1.0 - lbh) * jax.nn.sigmoid(hf.astype(f32).reshape(hs))
    hg_o = hgrn2_chunkwise(jax.nn.silu(hq.astype(f32)).reshape(hs), 1.0 - forget,
                           hi.astype(f32).reshape(hs), jnp.log(forget))
    hg_o = rms_norm(hg_o, hg_norm.reshape(HG_HEADS, HG_HEAD_DIM)).reshape(B, T, HG_WIDTH)
    hg_o = hg_o * jax.nn.silu(hgate.astype(f32))
    qk = jax.nn.silu(causal_depthwise_conv_2(jnp.concatenate([mq, mk], axis=-1), conv_w, conv_b))
    mq, mk = jnp.split(qk.astype(f32), 2, axis=-1)
    qs = (B, T, ML_HEADS, ML_QK_DIM)
    gates = (jnp.concatenate([mig, mfg], axis=-1) + gate_bias).astype(f32)
    log_i = gates[..., :ML_HEADS]
    log_f = jax.nn.log_sigmoid(gates[..., ML_HEADS:])
    ml_o = mlstm_chunkwise(mq.reshape(qs) * (ML_QK_DIM ** -0.5), mk.reshape(qs),
                           mv.astype(f32).reshape(B, T, ML_HEADS, ML_V_DIM), log_i, log_f)
    ml_o = rms_norm(ml_o, ml_norm.reshape(ML_HEADS, ML_V_DIM)).reshape(B, T, ML_WIDTH)
    ml_o = ml_o * jax.nn.sigmoid(mo.astype(f32))
    mix = jnp.concatenate([hg_o, ml_o], axis=-1).astype(h.dtype)
    return mix @ w_out

def second_inputs(seed: int = 0) -> dict:
    key = jax.random.key(seed)
    ks = jax.random.split(key, 16)
    nrm = jax.random.normal
    gate_bias = jnp.concatenate([
        0.1 * nrm(ks[8], (DEPTH, ML_HEADS)),
        jnp.linspace(3.0, 6.0, ML_HEADS)[None, :] + 0.1 * nrm(ks[9], (DEPTH, ML_HEADS))], axis=-1)
    return {
        "x": nrm(ks[0], (BATCH, SEQ, D_MODEL), jnp.float32),
        "norm_pre": 1.0 + 0.05 * nrm(ks[1], (DEPTH, 3, D_MODEL)),
        "norm_post": 1.0 + 0.05 * nrm(ks[2], (DEPTH, 3, D_MODEL)),
        "ffn1_w_in": nrm(ks[3], (DEPTH, D_MODEL, 2 * D_FF)) * D_MODEL ** -0.5,
        "ffn1_w_out": nrm(ks[4], (DEPTH, D_FF, D_MODEL)) * D_FF ** -0.5,
        "w_mix_in": nrm(ks[5], (DEPTH, D_MODEL, D_IN)) * D_MODEL ** -0.5,
        "conv_w": nrm(ks[6], (DEPTH, CONV_WIDTH_2, 2 * ML_HEADS * ML_QK_DIM)) * CONV_WIDTH_2 ** -0.5,
        "conv_b": 0.02 * nrm(ks[7], (DEPTH, 2 * ML_HEADS * ML_QK_DIM)),
        "mlstm_gate_bias": gate_bias,
        "hgrn_lb_logits": 0.5 * nrm(ks[10], (DEPTH + 1, HG_WIDTH)),
        "hgrn_norm": 1.0 + 0.05 * nrm(ks[11], (DEPTH, HG_WIDTH)),
        "mlstm_norm": 1.0 + 0.05 * nrm(ks[12], (DEPTH, ML_WIDTH)),
        "w_mix_out": nrm(ks[13], (DEPTH, D_MIX, D_MODEL)) * D_MIX ** -0.5,
        "ffn2_w_in": nrm(ks[14], (DEPTH, D_MODEL, 2 * D_FF)) * D_MODEL ** -0.5,
        "ffn2_w_out": nrm(ks[15], (DEPTH, D_FF, D_MODEL)) * D_FF ** -0.5,
    }

def second_block(x, norm_pre, norm_post, ffn1_w_in, ffn1_w_out, w_mix_in, conv_w, conv_b,
              mlstm_gate_bias, hgrn_lb_logits, hgrn_norm, mlstm_norm, w_mix_out,
              ffn2_w_in, ffn2_w_out):
    lower_bounds = jnp.cumsum(jax.nn.softmax(hgrn_lb_logits.astype(jnp.float32), axis=0), axis=0)
    for l in range(DEPTH):
        x = x + 0.5 * rms_norm(swiglu_ffn(rms_norm(x, norm_pre[l, 0]), ffn1_w_in[l], ffn1_w_out[l]),
                               norm_post[l, 0])
        mixed = token_mixer(rms_norm(x, norm_pre[l, 1]), w_mix_in[l], conv_w[l], conv_b[l],
                            mlstm_gate_bias[l], lower_bounds[l], hgrn_norm[l], mlstm_norm[l],
                            w_mix_out[l])
        x = x + rms_norm(mixed, norm_post[l, 1])
        x = x + 0.5 * rms_norm(swiglu_ffn(rms_norm(x, norm_pre[l, 2]), ffn2_w_in[l], ffn2_w_out[l]),
                               norm_post[l, 2])
    return x


def setup_inputs(seed=0):
    out = dict(first_inputs(seed))
    for name, value in second_inputs(seed + 1).items():
        if name != "x":
            out[name + "_2"] = value
    return out


def reference(
    x, c, positions, w_ada, b_ada, pre_norm_g, w_in, conv_w, conv_b, conv_ln_g, conv_ln_b,
    w_ret_out, w_conv_out, w_out, post_norm_g, norm_pre_2, norm_post_2, ffn1_w_in_2,
    ffn1_w_out_2, w_mix_in_2, conv_w_2, conv_b_2, mlstm_gate_bias_2, hgrn_lb_logits_2,
    hgrn_norm_2, mlstm_norm_2, w_mix_out_2, ffn2_w_in_2, ffn2_w_out_2,
):
    x = first_block(
        x, c, positions, w_ada, b_ada, pre_norm_g, w_in, conv_w, conv_b, conv_ln_g, conv_ln_b,
        w_ret_out, w_conv_out, w_out, post_norm_g,
    )
    return second_block(
        x, norm_pre_2, norm_post_2, ffn1_w_in_2, ffn1_w_out_2, w_mix_in_2, conv_w_2, conv_b_2,
        mlstm_gate_bias_2, hgrn_lb_logits_2, hgrn_norm_2, mlstm_norm_2, w_mix_out_2,
        ffn2_w_in_2, ffn2_w_out_2,
    )


_drawn_inputs = setup_inputs


def setup_inputs(seed=0):
    import zlib

    import numpy as np

    out = dict(_drawn_inputs(seed))
    spreads = {}
    factors = {'pre_norm_g': 3.318,
     'conv_b': 8.0,
     'conv_ln_g': 8.0,
     'conv_ln_b': 26.35,
     'post_norm_g': 7.477,
     'conv_b_2': 6.455}
    for name, (base, spread) in spreads.items():
        noise = np.random.default_rng([zlib.crc32(name.encode()), seed]).standard_normal(out[name].shape)
        drawn = base * np.exp(spread * noise) if base else spread * noise
        out[name] = __import__('jax').numpy.asarray(drawn.astype(out[name].dtype))
    for name, factor in factors.items():
        out[name] = (out[name] * factor).astype(out[name].dtype)
    return out
```

```python
from contextlib import ExitStack

import numpy as np

import concourse.bass as bass
from concourse import mybir

F32 = mybir.dt.float32
F32R = mybir.dt.float32r
U8 = mybir.dt.uint8
I32 = mybir.dt.int32
ALU = mybir.AluOpType
ACT = mybir.ActivationFunctionType
AX = mybir.AxisListType

P = 128
S = 256
NT = S // P
D = 1024
KD = D // P
CB = 512
UPG = 4
RH = 4
CW = 31
CW2 = 4
FF = 2816
FB = FF // 256
KF = FF // P
NH = 4
CHUNK = 64
QK = 64

STAGES = {}
_b = 0
_UNIT0 = [0]
for _name, _n, _k in (("u", 4, KD), ("qk", 4, KD), ("v", 4, KD), ("z", 4, KD), ("zc", 2, KD), ("g", 4, KD),
                      ("ret", 2, 2 * KD), ("conv", 2, KD), ("wout", 2, KD),
                      ("f1i", FB, KD), ("f1o", 2, KF), ("mixi", 7, KD), ("mixo", 2, KD),
                      ("f2i", FB, KD), ("f2o", 2, KF)):
    STAGES[_name] = (_b, _n, _k)
    for _ in range(_n):
        _UNIT0.append(_UNIT0[-1] + _k)
    _b += _n
BLOCKS = _b
UNITS = _UNIT0[-1]
GROUPS = UNITS // UPG
assert UNITS % UPG == 0
RAW = 2
RING = 4


def first(stage):
    return STAGES[stage][0]


def group_end(b):
    return -(-_UNIT0[b + 1] // UPG)


def split_to(b):
    return min(group_end(min(b + 1, BLOCKS - 1)), group_end(b) + 2)


COLS = {}
_c = 0
for _name, _n in (("c", 8), ("pre_g", 8), ("b_shift", 8), ("b_scale", 8), ("conv_b", 8), ("conv_w", 8 * CW),
                  ("pre2", 24), ("lb", 8), ("conv_w2", 4 * CW2), ("conv_b2", 4)):
    COLS[_name] = _c
    _c += _n
NCOLS = _c

ROWS = ["b_gate", "ln_g", "ln_b", "post_g", "post0", "mix_norm", "post1", "post2"]

SIDE = {}
_uses = {4: 0, 5: 0, 6: 0, 7: 0}


def _side(key, bank, times=1):
    SIDE[key] = (bank, _uses[bank] + 1)
    _uses[bank] += times


def _side4(key):
    for j in range(4):
        _side((key, j), 4 + j)


def _plan_side():
    _side("shift_scale", 4)
    _side(("gate", 0), 5)
    _side(("gate", 1), 6)
    _side4("pre0")
    _side4("aT")
    for m in range(6):
        if m >= 2:
            _side(("ro", m - 2, 0), 7)
            _side(("ro", m - 2, 1), 4)
        if 1 <= m <= 4:
            _side(("rs", m - 1), 6)
        if m <= 3:
            _side(("qT", m), 4)
            _side(("kT", m), 5)
    for j in range(8):
        _side(("retT", j), 4 + j % 4)
    for key in ("cvtok", "cvT", "mgT", "pre1"):
        _side4(key)
    _side(("ffT", 0, 0), 4, (FB + 1) // 2)
    _side(("ffT", 0, 1), 5, FB // 2)
    _side4("pre2")
    _side("gates", 7)
    _side(("hqT", 0), 4)
    _side(("hqT", 1), 5)
    _side(("hfT", 0), 6)
    _side(("hfT", 1), 7)
    _side("gatesT", 6)
    _side("umT", 6)
    _side(("mb", 0), 4)
    _side(("mb", 1), 5)
    for lv in range(8):
        for blk in range(NT):
            _side(("lv", lv, blk), 4 + 2 * (lv % 2) + blk)
        if lv == 1:
            _side(("cv2T", 0), 4)
            _side(("cv2T", 1), 5)
    for h in range(NH):
        _side(("ms", h), 4 + h)
    _side(("lv", 8, 0), 4)
    for t in range(NT):
        for j in range(2):
            _side(("mn", t, j), 4 + 2 * t + j)
    _side(("ho", 0), 6)
    _side(("ho", 1), 7)
    for key in ("mxT", "pre3"):
        _side4(key)
    _side(("ffT", 1, 0), 4, (FB + 1) // 2)
    _side(("ffT", 1, 1), 5, FB // 2)


_plan_side()

HI_BEFORE = {}
_n = 0
for _name, _k in (("pre0", 4), ("retT", 8), ("cvT", 4), ("mgT", 4), ("pre1", 8), (("ffT", 0), FB), ("pre2", 8),
                  ("mxT", 4), ("pre3", 8), (("ffT", 1), FB)):
    HI_BEFORE[_name] = _n
    _n += _k

NORMS = ["pre0", "post_w", "pre1", "post_f1", "pre2", "post_m", "pre3", "post_f2"]
SUMS_BEFORE = {}
_n = 0
for _name in NORMS:
    SUMS_BEFORE[_name] = _n
    _n += 2 if _name.startswith("pre") else 4

TWO_PI = 2 * np.pi
TWO_PI_1 = 6.28125
TWO_PI_2 = float(np.round((TWO_PI - TWO_PI_1) * 2**21) / 2**21)
TWO_PI_3 = float(TWO_PI - TWO_PI_1 - TWO_PI_2)
ROUND = 1.5 * 2**23
PI_INSIDE = 3.1415925


def build_program(nc, stream, ada, gates_w, cols, rows, gate_bias, x_in, pos_in,
                  ident_in, inv_freq_in, decay_in, level_in, causal_in, sel_in, out):
    ctx = ExitStack()
    with ctx:
        def sb(name, shape, dt=F32, stack=ctx):
            return stack.enter_context(nc.sbuf_tensor(name, shape, dt))

        def sem(name):
            return ctx.enter_context(nc.semaphore(name))

        raw_loaded = [sem(f"raw_loaded{n}") for n in range(RAW)]
        ada_loaded = [sem(f"ada_loaded{n}") for n in range(4)]
        row_loaded = {name: sem(f"{name}_loaded") for name in ROWS}
        pair_freed = [sem(f"pair_freed{n}") for n in range(2)]
        side_filled = [sem(f"side_filled{n}") for n in range(4, 8)]
        side_freed = [sem(f"side_freed{n}") for n in range(4, 8)]
        x_loaded = sem("x_loaded")
        col_loaded = sem("col_loaded")
        ident_loaded = sem("ident_loaded")
        pos_loaded = sem("pos_loaded")
        freq_loaded = sem("freq_loaded")
        ada_summed = sem("ada_summed")
        decay_loaded = sem("decay_loaded")
        w_lo_ready = sem("w_lo_ready")
        x_ready = sem("x_ready")
        out_written = sem("out_written")
        w_used = sem("w_used")
        normed = sem("normed")
        ones_ready = sem("ones_ready")
        act0_ready = sem("act0_ready")
        rotated = sem("rotated")
        ret_ready = sem("ret_ready")
        conv_step = sem("conv_step")
        conv_act_ready = sem("conv_act_ready")
        merged = sem("merged")
        gw_ready = sem("gw_ready")
        row_step = sem("row_step")
        sel_loaded = sem("sel_loaded")
        scaled_ready = sem("scaled_ready")
        hk_T_ready = sem("hk_T_ready")
        mqk_T_ready = sem("mqk_T_ready")
        mv_ones = sem("mv_ones")
        mixed = sem("mixed")
        w_hi_ready = sem("w_hi_ready")
        ss_ready = sem("ss_ready")
        act_hi_ready = sem("act_hi_ready")
        trig_step = sem("trig_step")
        trig_ready = sem("trig_ready")
        tanh_ready = sem("tanh_ready")
        pad_ready = sem("pad_ready")
        ln_step = sem("ln_step")
        conv_silu = sem("conv_silu")
        silu_ready = sem("silu_ready")
        gw_loaded = sem("gw_loaded")
        gw_hi_ready = sem("gw_hi_ready")
        lb_step = sem("lb_step")
        lb_exp = sem("lb_exp")
        log_f_ready = sem("log_f_ready")
        mw_exp = sem("mw_exp")
        diff_ready = sem("diff_ready")
        exp_ready = sem("exp_ready")
        mqk_pad_ready = sem("mqk_pad_ready")
        conv2_step = sem("conv2_step")
        mix_sq = sem("mix_sq")
        ss_whole = sem("ss_whole")
        var_ready = sem("var_ready")
        rstd_ready = sem("rstd_ready")
        half_ready = sem("half_ready")
        rot_step = sem("rot_step")
        head_var = sem("head_var")
        head_eps = sem("head_eps")
        head_rstd = sem("head_rstd")
        ln_var = sem("ln_var")
        ln_eps = sem("ln_eps")
        ln_rstd = sem("ln_rstd")
        x_again = sem("x_again")
        factor_ready = sem("factor_ready")
        gbias_loaded = sem("gbias_loaded")
        level_loaded = sem("level_loaded")
        causal_loaded = sem("causal_loaded")
        hsc_clear = sem("hsc_clear")
        level_ready = sem("level_ready")
        keep_step = sem("keep_step")
        mw_masked = sem("mw_masked")
        gates_scaled = sem("gates_scaled")
        mo_step = sem("mo_step")
        mix_ss = sem("mix_ss")
        mix_var = sem("mix_var")
        mix_rstd = sem("mix_rstd")
        mod_ready = sem("mod_ready")
        head_bn = sem("head_bn")
        ln_bn = sem("ln_bn")
        post_scaled = sem("post_scaled")
        cum_ready = sem("cum_ready")
        diff_part = sem("diff_part")
        mden_step = sem("mden_step")
        mix_scaled = sem("mix_scaled")

        raw = sb("raw", [P, RAW, UPG * CB])
        w_hi = sb("w_hi", [P, RING, UPG * CB], F32R)
        w_lo = sb("w_lo", [P, RING, UPG * CB], F32R)
        act_hi = sb("act_hi", [P, KD, S], F32R)
        act_lo = sb("act_lo", [P, KD, S], F32R)
        x = sb("x", [P, NT, D])
        tmp = sb("tmp", [P, NT, D])
        tmp_T = tmp[:].rearrange("p t d -> p (t d)").rearrange("p (k s) -> p k s", s=S)
        spread = sb("spread", [P, 2, D])
        gate_bc = sb("gate_bc", [P, D])
        ident = sb("ident", [P, P])
        col = sb("col", [P, NCOLS])
        half_power = sb("half_power", [P, 8])
        stat = sb("stat", [P, 8 * len(NORMS)])
        head_stat = sb("head_stat", [P, NT * RH, 10])
        ln_stat = sb("ln_stat", [P, NT, 16])
        junk = sb("junk", [P, D])
        bank = [ctx.enter_context(nc.psum_tensor(f"bank{i}", [P, CB], F32)) for i in range(8)]

        with ExitStack() as own:
            ada_w = sb("ada_w", [P, 4, 3 * D], stack=own)
            ada_acc = sb("ada_acc", [P, 3 * D], stack=own)
            mod_T = sb("mod_T", [P, 16], stack=own)
            h_T = sb("h_T", [P, KD, S], stack=own)
            ang = sb("ang", [P, NT, 2, P], stack=own)
            turns = sb("turns", [P, NT, 2, P], stack=own)
            part = sb("part", [P, NT, 2, P], stack=own)
            ones = sb("ones", [P, P], stack=own)
            inv_freq = sb("inv_freq", [P, P], stack=own)
            pos_i = sb("pos_i", [P, NT], I32, stack=own)
            pos_f = sb("pos_f", [P, NT], stack=own)
        with ExitStack() as own:
            qkv = sb("qkv", [P, 4, NT, D], stack=own)
            z = sb("z", [P, 2, NT, D], stack=own)
            g = sb("g", [P, 2, NT, D], stack=own)
            a_T = sb("a_T", [P, KD, S + CW - 1], stack=own)
            qk_T = sb("qk_T", [P, 2, 2, S], stack=own)
        with ExitStack() as own:
            sb("under_ret", [P, 2, NT, D], stack=own)
            ret_hi = sb("ret_hi", [P, 2 * KD, S], F32R, stack=own)
            ret_lo = sb("ret_lo", [P, 2 * KD, S], F32R, stack=own)
        flat = spread[:].rearrange("p a d -> p (a d)")
        trig = flat[:, 0:512].rearrange("p (t w f) -> p t w f", t=NT, w=2)
        decay = flat[:, 512:2048].rearrange("p (h c) -> p h c", h=RH)
        masked = junk[:, 0:768].rearrange("p (a c) -> p a c", a=2)
        odd_taps = junk[:, 768:1024]
        tanh_u = junk[:, 0:512].rearrange("p (t c) -> p t c", t=NT)
        rot = g[:, 0, 0, :].rearrange("p (a h f) -> p a h f", a=2, h=RH)
        with ExitStack() as own:
            ff_hi = sb("ff_hi", [P, FB, 2 * S], F32R, stack=own)
            ff_lo = sb("ff_lo", [P, FB, 2 * S], F32R, stack=own)
            silu_g = sb("silu_g", [P, NT, 256], stack=own)
            ff_tok = sb("ff_tok", [P, 2, NT, 256], stack=own)
        with ExitStack() as own:
            hv = sb("hv", [P, NT, CB], stack=own)
            hgate = sb("hgate", [P, NT, CB], stack=own)
            mo = sb("mo", [P, NT, CB], stack=own)
            mqk = sb("mqk", [P, NT, CB], stack=own)
            mv = sb("mv", [P, NT, NH, P + 2], stack=own)
            hq_T = sb("hq_T", [P, NH, S], stack=own)
            hk_T = sb("hk_T", [P, NH, S], stack=own)
            cum = sb("cum", [P, NH, S], stack=own)
            dec = sb("dec", [P, NH, S], stack=own)
            qs = sb("qs", [P, 2, NH * S], stack=own)
            ks = sb("ks", [P, 2, NH * S], stack=own)
            hsc = sb("hsc", [P, NT, NH, P], stack=own)
            hoff = sb("hoff", [P, NH, P], stack=own)
            mqk_pad = sb("mqk_pad", [P, 4, S + CW2 - 1], stack=own)
            mqk_T = sb("mqk_T", [P, 4, S], stack=own)
            mw = sb("mw", [P, NH, 3 * P], stack=own)
            level = sb("level", [P, 8, P], U8, stack=own)
            causal = sb("causal", [P, P], stack=own)
            gw = sb("gw", [P, KD * 8], stack=own)
            gw_hi = sb("gw_hi", [P, KD * 8], F32R, stack=own)
            gw_lo = sb("gw_lo", [P, KD * 8], F32R, stack=own)
            gbias = sb("gbias", [P, 8], stack=own)
            gt = sb("gt", [P, NT, 8], stack=own)
            lb = sb("lb", [P, 6, NH], stack=own)
            um = sb("um", [P, 16], stack=own)
            mden = sb("mden", [P, 2, 8], stack=own)
            mstat = sb("mstat", [P, 6, 8], stack=own)
            sel = sb("sel", [NH, NH, P], stack=own)
        keep = junk[:].rearrange("p (h s) -> p h s", h=NH)
        row = spread[0:NH, 1, :].rearrange("p (a s) -> p a s", a=4)

        def cv(name, j, n=1):
            return col[:, COLS[name] + j:COLS[name] + j + n]

        def drained(b, off=None):
            return pair_freed[b % 2], plus(b // 2 + 1, off)

        def done(b, off=None):
            return w_used, plus(group_end(b), off, UPG)

        def part_of(b, tau):
            return bank[2 * (b % 2) + tau]

        def plus(value, off, per=1):
            return value if off is None else value + off * per

        def side(key):
            return bank[SIDE[key][0]]

        def full(key, off=None):
            return side_filled[SIDE[key][0] - 4], plus(SIDE[key][1], off)

        def freed(key, off=None):
            return side_freed[SIDE[key][0] - 4], plus(SIDE[key][1], off)

        def side_free(key):
            return side_freed[SIDE[key][0] - 4]

        def pair_free(b):
            return pair_freed[b % 2]

        def sums(name):
            n = 8 * NORMS.index(name)
            return stat[:, n:n + 4], stat[:, n + 4:n + 6], stat[:, n + 6:n + 8]

        block = ctx.enter_context(nc.Block())

        @block.sync
        def _(sp):
            def load(dst, src, loaded):
                sp.dma_start(dst, src).then_inc(loaded, 16)

            load(x[:], x_in.rearrange("(t p) d -> p t d", p=P), x_loaded)
            load(col[:], cols, col_loaded)
            load(ident[:], ident_in, ident_loaded)
            load(pos_i[:], pos_in, pos_loaded)
            load(inv_freq[:], inv_freq_in, freq_loaded)
            for k in range(KD):
                if k >= 4:
                    sp.wait_ge(ada_summed, k - 3)
                load(ada_w[:, k % 4, :], ada[k], ada_loaded[k % 4])
            for n in range(RAW):
                load(raw[:, n, :], stream[n], raw_loaded[n])
            load(decay[:], decay_in.rearrange("p (h c) -> p h c", h=RH), decay_loaded)
            with sp.Fori(1, GROUPS // RAW) as i:
                for n in range(RAW):
                    sp.wait_ge(w_lo_ready, i * RAW + (n - RAW + 1))
                    load(raw[:, n, :], stream[i * RAW + n], raw_loaded[n])
            for tau in range(NT):
                sp.wait_ge(x_ready, 6 + tau + 1)
                load(out[tau * P:(tau + 1) * P, :], x[:, tau, :], out_written)
            sp.wait_ge(out_written, 16 * NT)

        @block.tensor
        def _(pe):
            def gemm(b, hi, lo, off=None, mid=None):
                k_tiles = _UNIT0[b + 1] - _UNIT0[b]
                if b >= 2:
                    pe.wait_ge(pair_free(b), plus(b // 2, off))
                for n in range(k_tiles):
                    unit = _UNIT0[b] + n
                    group, place = divmod(unit, UPG)
                    cs = slice(place * CB, (place + 1) * CB)
                    if place == 0 or n == 0:
                        pe.wait_ge(w_lo_ready, plus(group + 1, off, UPG))
                    wh, wl = w_hi[:, group % RING, cs], w_lo[:, group % RING, cs]
                    for tau in range(NT):
                        ah, al = hi(n)[:, tau * P:(tau + 1) * P], lo(n)[:, tau * P:(tau + 1) * P]
                        acc = part_of(b, tau)[:]
                        pe.matmul(acc, ah, wh, start=n == 0, stop=False)
                        pe.matmul(acc, ah, wl, start=False, stop=False)
                        mm = pe.matmul(acc, al, wh, start=False, stop=n == k_tiles - 1)
                    if place == UPG - 1:
                        mm.then_inc(w_used, 1)
                    if mid is not None and n == k_tiles // 2 - 1:
                        mid()

            def act(n):
                return act_hi[:, n, :]

            def act_l(n):
                return act_lo[:, n, :]

            def ret(n):
                return ret_hi[:, n, :]

            def ret_l(n):
                return ret_lo[:, n, :]

            def ff(n):
                return ff_hi[:, n // 2, (n % 2) * S:(n % 2 + 1) * S]

            def ff_l(n):
                return ff_lo[:, n // 2, (n % 2) * S:(n % 2 + 1) * S]

            def begin(key, off=None):
                n = SIDE[key][1] - 1
                if n or off is not None:
                    pe.wait_ge(side_free(key), plus(n, off))

            def end(ins, key):
                ins.then_inc(side_filled[SIDE[key][0] - 4], 1)

            def turn(key, sources, off=None):
                begin(key, off)
                for n, src in enumerate(sources):
                    mm = pe.transpose(side(key)[:, n * P:(n + 1) * P], src, ident[:])
                end(mm, key)

            def turn_tok(key, j, src):
                turn((key, j), [src(tau, k) for k in (2 * j, 2 * j + 1) for tau in range(NT)])

            def turn_norm(key, count):
                pe.wait_ge(normed, count)
                for j in range(4):
                    turn_tok(key, j, lambda tau, k: tmp[:, tau, k * P:(k + 1) * P])
                for j in range(4):
                    pe.wait_ge(*freed((key, j)))

            pe.wait_ge(ada_summed, KD)
            pe.wait_ge(ones_ready, 1)
            begin("shift_scale")
            for f in range(16):
                mm = pe.matmul(side("shift_scale")[:, f:f + 1], ada_acc[:, f * P:(f + 1) * P], ones[:, 0:1],
                               start=True, stop=True)
            end(mm, "shift_scale")
            for j in range(2):
                begin(("gate", j))
                mm = pe.matmul(side(("gate", j))[:], ones[:], ada_acc[:, 2 * D + j * CB:2 * D + (j + 1) * CB],
                               start=True, stop=True)
                end(mm, ("gate", j))
            pe.wait_ge(ident_loaded, 16)
            pe.wait_ge(normed, 2)
            for j in range(4):
                turn_tok("pre0", j, lambda tau, k: tmp[:, tau, k * P:(k + 1) * P])
            pe.wait_ge(act0_ready, 4)
            for b in range(4):
                gemm(b, act, act_l)
            pe.wait_ge(*drained(2))
            pe.wait_ge(*drained(3))
            for j in range(4):
                turn_tok("aT", j, lambda tau, k: tmp[:, tau, k * P:(k + 1) * P])
            with pe.Fori(0, 4) as i:
                for n in range(2):
                    gemm(first("qk") + n, act, act_l, off=i)
            with pe.Fori(0, 2) as i:
                for n in range(2):
                    gemm(first("z") + n, act, act_l, off=i)

            def head_turn(h):
                pe.wait_ge(rotated, 2 * NT)
                for w, key in ((0, "qT"), (1, "kT")):
                    turn((key, h), [qkv[:, w, tau, h * 256 + k * P:h * 256 + (k + 1) * P]
                                    for k in range(2) for tau in range(NT)])

            def head_scores(h):
                key = ("rs", h)
                begin(key)
                pe.wait_ge(*freed(("qT", h)))
                pe.wait_ge(*freed(("kT", h)))
                for k in range(2):
                    pe.matmul(side(key)[:, 0:S], qk_T[:, 1, k, 0:P], qk_T[:, 0, k, :], start=k == 0, stop=k == 1)
                for k in range(2):
                    mm = pe.matmul(side(key)[:, S:S + P], qk_T[:, 1, k, P:S], qk_T[:, 0, k, P:S],
                                   start=k == 0, stop=k == 1)
                end(mm, key)

            def head_out(h):
                def v(tau):
                    return qkv[:, 2 + h // 2, tau, (h % 2) * CB:(h % 2 + 1) * CB]

                pe.wait_ge(*freed(("rs", h)))
                begin(("ro", h, 0))
                end(pe.matmul(side(("ro", h, 0))[:], masked[:, h % 2, 0:P], v(0), start=True, stop=True), ("ro", h, 0))
                begin(("ro", h, 1))
                pe.matmul(side(("ro", h, 1))[:], masked[:, h % 2, P:2 * P], v(0), start=True, stop=False)
                end(pe.matmul(side(("ro", h, 1))[:], masked[:, h % 2, 2 * P:3 * P], v(1), start=False, stop=True),
                    ("ro", h, 1))

            def heads_mid(m):
                if 1 <= m <= 4:
                    head_scores(m - 1)
                if m <= 3:
                    head_turn(m)

            for m in range(6):
                if m >= 2:
                    head_out(m - 2)
                gemm(first("zc") + m, act, act_l, mid=lambda: heads_mid(m))
            pe.wait_ge(ret_ready, 2 * RH)
            for j in range(8):
                turn(("retT", j), [qkv[:, j % 2, tau, (j // 2) * 256 + k * P:(j // 2) * 256 + (k + 1) * P]
                                   for k in range(2) for tau in range(NT)])
            for j in range(8):
                pe.wait_ge(*freed(("retT", j)))

            def conv_turn():
                pe.wait_ge(conv_step, KD * (CW + 1) + 1)
                for tau in range(NT):
                    for half in range(2):
                        turn(("cvtok", 2 * tau + half), [tmp_T[:, 4 * half + k, tau * P:(tau + 1) * P] for k in range(4)])

            def conv_turn_back():
                pe.wait_ge(conv_act_ready, NT)
                for j in range(4):
                    turn_tok("cvT", j, lambda tau, k: tmp[:, tau, k * P:(k + 1) * P])

            gemm(first("ret"), ret, ret_l, mid=conv_turn)
            gemm(first("ret") + 1, ret, ret_l, mid=conv_turn_back)
            for j in range(4):
                pe.wait_ge(*freed(("cvT", j)))

            def merged_turn(c):
                pe.wait_ge(merged, NT * (c + 1))
                for j in range(2 * c, 2 * c + 2):
                    turn_tok("mgT", j, lambda tau, k: g[:, 0, tau, k * P:(k + 1) * P])

            gemm(first("conv"), act, act_l)
            gemm(first("conv") + 1, act, act_l, mid=lambda: merged_turn(0))
            merged_turn(1)
            for j in range(4):
                pe.wait_ge(*freed(("mgT", j)))
            for n in range(2):
                gemm(first("wout") + n, ret, ret_l)

            def feed_forward(which, stage_in, stage_out):
                b = first(stage_in)

                def hidden_turn(parity, off):
                    key = ("ffT", which, parity)
                    pe.wait_ge(*drained(b + parity, off))
                    turn(key, [ff_tok[:, parity, tau, k * P:(k + 1) * P] for k in range(2) for tau in range(NT)], off)

                gemm(b, act, act_l)
                with pe.Fori(0, (FB - 1) // 2) as i:
                    gemm(b + 1, act, act_l, off=i)
                    hidden_turn(0, i)
                    gemm(b + 2, act, act_l, off=i)
                    hidden_turn(1, i)
                hidden_turn(0, (FB - 1) // 2)
                pe.wait_ge(*freed(("ffT", which, 1), FB // 2 - 1))
                pe.wait_ge(*freed(("ffT", which, 0), FB // 2))
                for n in range(2):
                    gemm(first(stage_out) + n, ff, ff_l)

            turn_norm("pre1", 4)
            feed_forward(0, "f1i", "f1o")
            turn_norm("pre2", 6)

            pe.wait_ge(gw_ready, 2)
            begin("gates")
            for tau in range(NT):
                for k in range(KD):
                    ts_, cs = slice(tau * P, (tau + 1) * P), slice(8 * k, 8 * k + 8)
                    o = side("gates")[:, 8 * tau:8 * tau + 8]
                    pe.matmul(o, act_hi[:, k, ts_], gw_hi[:, cs], start=k == 0, stop=False)
                    pe.matmul(o, act_hi[:, k, ts_], gw_lo[:, cs], start=False, stop=False)
                    mm = pe.matmul(o, act_lo[:, k, ts_], gw_hi[:, cs], start=False, stop=k == KD - 1)
            end(mm, "gates")
            mix = first("mixi")

            def hgrn_turn(key, c):
                pe.wait_ge(*drained(mix + c))
                for j in range(2):
                    turn((key, j), [tmp[:, tau, c * CB + k * P:c * CB + (k + 1) * P]
                                    for k in (2 * j, 2 * j + 1) for tau in range(NT)])

            def gates_turn():
                pe.wait_ge(*freed("gates"))
                begin("gatesT")
                for w in range(2):
                    for tau in range(NT):
                        mm = pe.matmul(side("gatesT")[0:NH, w * S + tau * P:w * S + (tau + 1) * P],
                                       gt[:, tau, 4 * w:4 * w + 4], ident[:], start=True, stop=True)
                end(mm, "gatesT")

            def um_turn():
                pe.wait_ge(row_step, 7)
                begin("umT")
                for w, r in ((0, 0), (1, 3)):
                    for tau in range(NT):
                        n = 8 * w + 4 * tau
                        mm = pe.matmul(side("umT")[:, n:n + 4], row[:, r, tau * P:(tau + 1) * P], ident[0:NH, 0:NH],
                                       start=True, stop=True)
                end(mm, "umT")

            def m_spread():
                pe.wait_ge(row_step, 6)
                pe.wait_ge(sel_loaded, 16)
                for j in range(2):
                    begin(("mb", j))
                    for n in range(2):
                        mm = pe.matmul(side(("mb", j))[:, n * S:(n + 1) * S], sel[:, 2 * j + n, :], row[:, 2, :],
                                       start=True, stop=True)
                    end(mm, ("mb", j))

            def level_scores(lv):
                if lv == 0:
                    pe.wait_ge(*freed(("hqT", 0)))
                    pe.wait_ge(*freed(("hqT", 1)))
                    pe.wait_ge(hk_T_ready, 1)
                    q_of, k_of = hq_T[:], hk_T[:]
                else:
                    pe.wait_ge(scaled_ready, 2 * lv)
                    q_of = qs[:, lv % 2, :].rearrange("p (h s) -> p h s", h=NH)
                    k_of = ks[:, lv % 2, :].rearrange("p (h s) -> p h s", h=NH)
                for blk in range(NT if lv < 8 else 1):
                    key = ("lv", lv, blk)
                    begin(key)
                    for h in range(NH):
                        s_at = slice(blk * P, (blk + 1) * P)
                        t_at = s_at if lv < 8 else slice(P, S)
                        mm = pe.matmul(side(key)[:, h * P:(h + 1) * P], k_of[:, h, s_at], q_of[:, h, t_at],
                                       start=True, stop=True)
                    end(mm, key)

            def conv2_turn():
                pe.wait_ge(*drained(mix + 3))
                for j in range(2):
                    turn(("cv2T", j), [mqk[:, tau, k * P:(k + 1) * P] for k in (2 * j, 2 * j + 1) for tau in range(NT)])

            def mlstm_scores(h):
                key = ("ms", h)
                begin(key)
                rows_at = slice((h % 2) * QK, (h % 2 + 1) * QK)
                q_of, k_of = mqk_T[rows_at, h // 2, :], mqk_T[rows_at, 2 + h // 2, :]
                pe.matmul(side(key)[:, 0:S], k_of[:, 0:P], q_of, start=True, stop=True)
                end(pe.matmul(side(key)[:, S:S + P], k_of[:, P:S], q_of[:, P:S], start=True, stop=True), key)

            gemm(mix, act, act_l)
            gemm(mix + 1, act, act_l, mid=lambda: hgrn_turn("hqT", 0))
            hgrn_turn("hfT", 1)
            gemm(mix + 2, act, act_l, mid=gates_turn)
            um_turn()
            gemm(mix + 3, act, act_l, mid=m_spread)
            level_scores(0)

            def mid45():
                level_scores(1)
                conv2_turn()

            gemm(mix + 4, act, act_l, mid=mid45)
            level_scores(2)
            gemm(mix + 5, act, act_l, mid=lambda: level_scores(3))
            level_scores(4)
            gemm(mix + 6, act, act_l, mid=lambda: level_scores(5))
            level_scores(6)
            level_scores(7)
            pe.wait_ge(mqk_T_ready, 1)
            for h in range(NH):
                mlstm_scores(h)
            level_scores(8)
            for h in range(NH):
                pe.wait_ge(*freed(("ms", h)))
            pe.wait_ge(mv_ones, 1)
            pe.wait_ge(*drained(mix + 4))
            for tau in range(NT):
                for j in range(2):
                    key = ("mn", tau, j)
                    begin(key)
                    for n in range(2):
                        h = 2 * j + n
                        o = side(key)[:, n * (P + 1):(n + 1) * (P + 1)]
                        if tau == 0:
                            mm = pe.matmul(o, mw[:, h, 0:P], mv[:, 0, h, 0:P + 1], start=True, stop=True)
                        else:
                            pe.matmul(o, mw[:, h, P:S], mv[:, 0, h, 0:P + 1], start=True, stop=False)
                            mm = pe.matmul(o, mw[:, h, S:S + P], mv[:, 1, h, 0:P + 1], start=False, stop=True)
                    end(mm, key)
            pe.wait_ge(*freed(("lv", 7, 1)))
            pe.wait_ge(*freed(("lv", 8, 0)))
            for tau in range(NT):
                key = ("ho", tau)
                begin(key)
                for h in range(NH):
                    o = side(key)[:, h * P:(h + 1) * P]
                    if tau == 1:
                        pe.matmul(o, hoff[:, h, :], hv[:, 0, h * P:(h + 1) * P], start=True, stop=False)
                    mm = pe.matmul(o, hsc[:, tau, h, :], hv[:, tau, h * P:(h + 1) * P], start=tau == 0, stop=True)
                end(mm, key)
            pe.wait_ge(mixed, 4)
            for j in range(4):
                turn_tok("mxT", j, lambda tau, k: tmp[:, tau, k * P:(k + 1) * P])
            for j in range(4):
                pe.wait_ge(*freed(("mxT", j)))
            for n in range(2):
                gemm(first("mixo") + n, act, act_l)
            turn_norm("pre3", 8)
            feed_forward(1, "f2i", "f2o")

        @block.scalar
        def _(act):
            def hi_parts(b, off=None):
                for n in range(split_to(b - 1) if b >= 0 else 0, split_to(b)):
                    act.wait_ge(raw_loaded[n % RAW], plus(16 * (n // RAW + 1), off, 16 * UPG // RAW))
                    if n >= RING:
                        act.wait_ge(w_used, plus(n - RING + 1, off, UPG))
                    act.activation(w_hi[:, n % RING, :], raw[:, n % RAW, :], ACT.Copy).then_inc(w_hi_ready, 1)

            def squares(name, src, half=0, width=D):
                for tau in range(NT):
                    if SUMS_BEFORE[name] + 2 * half + tau:
                        act.wait_ge(ss_ready, SUMS_BEFORE[name] + 2 * half + tau)
                    act.activation(junk[:, 0:width], src(tau), ACT.Square,
                                   accum_out=sums(name)[0][:, 2 * half + tau:2 * half + tau + 1]
                                   ).then_inc(ss_ready, 1)

            def hi_of(key, j, dst, scale=1.0):
                act.wait_ge(*full((key, j)))
                act.activation(dst, side((key, j))[:].rearrange("p (k s) -> p k s", s=S), ACT.Copy,
                               scale=scale).then_inc(act_hi_ready, 1)

            def hi_scaled(key, at):
                for j in range(4):
                    act.wait_ge(*full((key, j)))
                    for n in range(2):
                        k = 2 * j + n
                        act.activation(act_hi[:, k, :], side((key, j))[:, n * S:(n + 1) * S], ACT.Copy,
                                       scale=cv("pre2", at + k)).then_inc(act_hi_ready, 1)

            def drain(b, dst, func, off=None, scale=1.0):
                act.wait_ge(*done(b, off))
                for tau in range(NT):
                    ins = act.activation(dst(tau), part_of(b, tau)[:], func, scale=scale)
                ins.then_inc(pair_free(b), 1)

            act.wait_ge(x_loaded, 16)
            squares("pre0", lambda tau: x[:, tau, :])
            act.wait_ge(trig_step, 13)
            act.activation(trig, ang[:], ACT.Sin).then_inc(trig_ready, 1)
            hi_parts(-1)
            for j in range(4):
                act.wait_ge(*freed(("pre0", j)))
                act.activation(act_hi[:, 2 * j:2 * j + 2, :], h_T[:, 2 * j:2 * j + 2, :], ACT.Copy
                               ).then_inc(act_hi_ready, 1)
            for b in range(4):
                hi_parts(b)
                act.wait_ge(*done(b))
                if b:
                    act.wait_ge(*drained(b - 1))
                for tau in range(NT):
                    act.activation(tanh_u[:, tau, :], part_of(b, tau)[:, 256:512], ACT.Tanh,
                                   scale=0.5).then_inc(tanh_ready, 1)
            act.wait_ge(pad_ready, 1)
            for j in range(4):
                act.wait_ge(*full(("aT", j)))
                act.activation(a_T[:, 2 * j:2 * j + 2, CW - 1:], side(("aT", j))[:].rearrange("p (k s) -> p k s", s=S),
                               ACT.Copy, scale=0.5).then_inc(side_free(("aT", j)), 1)
            with act.Fori(0, 4) as i:
                for n in range(2):
                    hi_parts(first("qk") + n, i)
                    drain(first("qk") + n, lambda tau: qkv[:, i, tau, n * CB:(n + 1) * CB], ACT.Copy, i)
            with act.Fori(0, 2) as i:
                for n in range(2):
                    hi_parts(first("z") + n, i)
                    drain(first("z") + n, lambda tau: z[:, i, tau, n * CB:(n + 1) * CB], ACT.Silu, i)
            for m in range(6):
                b = first("zc") + m
                hi_parts(b)
                if m <= 3:
                    if m:
                        act.wait_ge(*full(("rs", m - 1)))
                    for w, key in ((0, "qT"), (1, "kT")):
                        act.wait_ge(*full((key, m)))
                        act.activation(qk_T[:, w, :, :], side((key, m))[:].rearrange("p (k s) -> p k s", s=S),
                                       ACT.Copy).then_inc(side_free((key, m)), 1)
                if m < 2:
                    drain(b, lambda tau: x[:, tau, m * CB:(m + 1) * CB], ACT.Silu)
                else:
                    drain(b, lambda tau: g[:, (m - 2) // 2, tau, (m % 2) * CB:(m % 2 + 1) * CB], ACT.Tanh, scale=0.5)
            for j in range(8):
                hi_of("retT", j, ret_hi[:, 2 * j:2 * j + 2, :])
            hi_parts(first("ret"))
            for tau in range(NT):
                act.wait_ge(ln_step, 3 * NT + tau + 1)
                act.activation(tmp[:, tau, :], tmp[:, tau, :], ACT.Silu).then_inc(conv_silu, 1)
            hi_parts(first("ret") + 1)
            for j in range(4):
                hi_of("cvT", j, act_hi[:, 2 * j:2 * j + 2, :])
            hi_parts(first("conv"))
            hi_parts(first("conv") + 1)
            for j in range(4):
                hi_of("mgT", j, ret_hi[:, 2 * j:2 * j + 2, :], scale=0.5)

            def post(name, stage):
                for c in range(2):
                    b = first(stage) + c
                    hi_parts(b)
                    act.wait_ge(*drained(b))
                    squares(name, lambda tau: tmp[:, tau, c * CB:(c + 1) * CB], c, CB)

            def pre(name, ready, at):
                for tau in range(NT):
                    act.wait_ge(x_ready, ready + tau + 1)
                squares(name, lambda tau: x[:, tau, :])
                hi_scaled(name, at)

            def feed_forward(which, stage):
                b0 = first(stage)

                def silu(b, off=None):
                    act.wait_ge(*done(b, off))
                    if b > b0:
                        act.wait_ge(*drained(b - 1, off))
                    for tau in range(NT):
                        act.activation(silu_g[:, tau, :], part_of(b, tau)[:, 0:256], ACT.Silu
                                       ).then_inc(silu_ready, 1)

                def hidden_hi(parity, j, off=None):
                    key = ("ffT", which, parity)
                    act.wait_ge(*full(key, off))
                    act.activation(ff_hi[:, j, :], side(key)[:], ACT.Copy).then_inc(act_hi_ready, 1)

                hi_parts(b0)
                silu(b0)
                with act.Fori(0, (FB - 1) // 2) as i:
                    for n in range(2):
                        hi_parts(b0 + 1 + n, i)
                        silu(b0 + 1 + n, i)
                        hidden_hi(n, 2 * i + n, i)
                hidden_hi(0, FB - 1, FB // 2)

            post("post_w", "wout")
            pre("pre1", 0, 0)
            feed_forward(0, "f1i")
            post("post_f1", "f1o")
            act.wait_ge(gw_loaded, 16)
            act.activation(gw_hi[:], gw[:], ACT.Copy).then_inc(gw_hi_ready, 1)
            act.wait_ge(lb_step, 3)
            act.activation(lb[:, 1:3, :], lb[:, 1:3, :], ACT.Exp).then_inc(lb_exp, 1)
            pre("pre2", 2, 8)
            mix = first("mixi")
            hi_parts(mix)
            drain(mix, lambda tau: tmp[:, tau, 0:CB], ACT.Silu)
            hi_parts(mix + 1)
            for j in range(2):
                act.wait_ge(*full(("hqT", j)))
                act.activation(hq_T[:, 2 * j:2 * j + 2, :], side(("hqT", j))[:].rearrange("p (h s) -> p h s", s=S),
                               ACT.Copy).then_inc(side_free(("hqT", j)), 1)
            drain(mix + 1, lambda tau: tmp[:, tau, CB:D], ACT.Sigmoid)
            hi_parts(mix + 2)
            for j in range(2):
                act.wait_ge(*freed(("hfT", j)))
            act.activation(dec[:], hk_T[:], ACT.Ln).then_inc(log_f_ready, 1)
            act.wait_ge(*full("gatesT"))
            f_row = side("gatesT")[0:NH, S:2 * S]
            act.activation(row[:, 2, :], f_row, ACT.Abs).then_inc(row_step, 1)
            act.wait_ge(row_step, 1)
            act.activation(row[:, 2, :], row[:, 2, :], ACT.Exp, scale=-1.0).then_inc(row_step, 1)
            act.wait_ge(row_step, 2)
            act.activation(row[:, 2, :], row[:, 2, :], ACT.Ln, bias=1.0).then_inc(row_step, 1)
            drain(mix + 2, lambda tau: hv[:, tau, :], ACT.Copy)
            hi_parts(mix + 3)
            act.wait_ge(*full("umT"))
            act.activation(um[:, 8:16], side("umT")[:, 8:16], ACT.Exp, scale=-1.0)
            act.activation(um[:, 0:8], side("umT")[:, 0:8], ACT.Copy).then_inc(side_free("umT"), 1)
            for j in range(2):
                act.wait_ge(*freed(("mb", j)))
            act.activation(mw[:], mw[:], ACT.Exp, scale=-1.0).then_inc(mw_exp, 1)
            drain(mix + 3, lambda tau: mqk[:, tau, :], ACT.Copy)

            def level_exp(lv):
                act.wait_ge(diff_ready, lv)
                act.activation(dec[:], dec[:], ACT.Exp).then_inc(exp_ready, 1)

            level_exp(1)
            hi_parts(mix + 4)
            level_exp(2)
            act.wait_ge(mqk_pad_ready, 1)
            for j in range(2):
                act.wait_ge(*full(("cv2T", j)))
                act.activation(mqk_pad[:, 2 * j:2 * j + 2, CW2 - 1:],
                               side(("cv2T", j))[:].rearrange("p (h s) -> p h s", s=S), ACT.Copy
                               ).then_inc(side_free(("cv2T", j)), 1)
            act.wait_ge(*done(mix + 4))
            for tau in range(NT):
                ins = act.activation(mv[:, tau, :, 0:P], part_of(mix + 4, tau)[:].rearrange("p (h d) -> p h d", h=NH),
                                     ACT.Copy)
            ins.then_inc(pair_free(mix + 4), 1)
            level_exp(3)
            hi_parts(mix + 5)
            level_exp(4)
            drain(mix + 5, lambda tau: hgate[:, tau, :], ACT.Silu)
            level_exp(5)
            hi_parts(mix + 6)
            act.wait_ge(conv2_step, 4 * CW2)
            act.activation(mqk_T[:], mqk_T[:], ACT.Silu).then_inc(mqk_T_ready, 1)
            level_exp(6)
            drain(mix + 6, lambda tau: mo[:, tau, :], ACT.Tanh, scale=0.5)
            level_exp(7)
            level_exp(8)
            for tau in range(NT):
                for j in range(2):
                    act.wait_ge(*freed(("mn", tau, j)))
            act.activation(ks[:, 1, :], qs[:, 1, :], ACT.Square).then_inc(mix_sq, 1)
            for tau in range(NT):
                key = ("ho", tau)
                act.wait_ge(*full(key))
                act.activation(ks[:, 0, tau * CB:(tau + 1) * CB], side(key)[:], ACT.Square).then_inc(mix_sq, 1)
                act.activation(qs[:, 0, tau * CB:(tau + 1) * CB], side(key)[:], ACT.Copy).then_inc(side_free(key), 1)
            for j in range(4):
                hi_of("mxT", j, act_hi[:, 2 * j:2 * j + 2, :])
            post("post_m", "mixo")
            pre("pre3", 4, 16)
            feed_forward(1, "f2i")
            post("post_f2", "f2o")

        @block.gpsimd
        def _(pool):
            def spread_row(dst, name):
                r = ROWS.index(name)
                pool.dma_start(dst, rows[r, :].partition_broadcast(P)).then_inc(row_loaded[name], 16)

            def power(dst, src, ready, count):
                pool.wait_ge(ready, count)
                n = dst.shape[-1]
                return pool.tensor_tensor(dst, src, half_power[:, 0:n], ALU.pow)

            def norm(name):
                r = NORMS.index(name)
                ss, var, rstd = sums(name)
                posts = sum(n.startswith("post") for n in NORMS[:r + 1])
                if name.startswith("pre"):
                    pool.wait_ge(ss_ready, SUMS_BEFORE[name] + 2)
                    src = ss[:, 0:2]
                else:
                    pool.wait_ge(ss_ready, SUMS_BEFORE[name] + 4)
                    pool.tensor_tensor(ss[:, 0:2], ss[:, 0:2], ss[:, 2:4], ALU.add).then_inc(ss_whole, 1)
                    pool.wait_ge(ss_whole, posts)
                    src = ss[:, 0:2]
                pool.tensor_scalar(var, src, 1.0 / D, 1e-6, ALU.mult, ALU.add).then_inc(var_ready, 1)
                power(rstd, var, var_ready, r + 1).then_inc(rstd_ready, 1)

            spread_row(gate_bc[:], "b_gate")
            pool.memset(ones[:], 1.0).then_inc(ones_ready, 1)
            pool.memset(half_power[:], -0.5).then_inc(half_ready, 1)
            pool.wait_ge(half_ready, 1)
            norm("pre0")
            pool.wait_ge(pos_loaded, 16)
            pool.wait_ge(freq_loaded, 16)
            pool.tensor_copy(pos_f[:], pos_i[:]).then_inc(trig_step, 1)
            pool.wait_ge(trig_step, 1)
            for tau in range(NT):
                for w in range(2):
                    ins = pool.tensor_scalar(ang[:, tau, w, :], inv_freq[:], pos_f[:, tau:tau + 1], None, ALU.mult)
            ins.then_inc(trig_step, 1)
            pool.wait_ge(trig_step, 2)
            pool.tensor_scalar(turns[:, :, 0, :], ang[:, :, 0, :], 1 / TWO_PI, 0.25, ALU.mult, ALU.add)
            pool.tensor_scalar(turns[:, :, 1, :], ang[:, :, 1, :], 1 / TWO_PI, None, ALU.mult).then_inc(trig_step, 1)
            for n, value in enumerate((ROUND, -ROUND)):
                pool.wait_ge(trig_step, 3 + n)
                pool.tensor_scalar(turns[:], turns[:], value, None, ALU.add).then_inc(trig_step, 1)
            for n, value in enumerate((TWO_PI_1, TWO_PI_2, TWO_PI_3)):
                pool.wait_ge(trig_step, 5 + 2 * n)
                pool.tensor_scalar(part[:], turns[:], value, None, ALU.mult).then_inc(trig_step, 1)
                pool.wait_ge(trig_step, 6 + 2 * n)
                pool.tensor_tensor(ang[:], ang[:], part[:], ALU.subtract).then_inc(trig_step, 1)
            pool.wait_ge(trig_step, 11)
            pool.tensor_scalar(ang[:, :, 0, :], ang[:, :, 0, :], TWO_PI / 4, None, ALU.add).then_inc(trig_step, 1)
            pool.wait_ge(trig_step, 12)
            pool.tensor_scalar(ang[:], ang[:], PI_INSIDE, -PI_INSIDE, ALU.min, ALU.max).then_inc(trig_step, 1)
            pool.wait_ge(trig_ready, 1)
            pool.wait_ge(act0_ready, 4)
            pool.memset(a_T[:, :, 0:CW - 1], 0.0).then_inc(pad_ready, 1)
            for b in range(first("qk"), first("qk") + 4):
                pool.wait_ge(*drained(b))
            n = 0
            for w in range(2):
                for tau in range(NT):
                    t = qkv[:, w, tau, :].rearrange("p (h u f) -> p u h f", h=RH, u=2)
                    cos = trig[:, tau, 0, :].unsqueeze(1).to_broadcast([P, RH, P])
                    sin = trig[:, tau, 1, :].unsqueeze(1).to_broadcast([P, RH, P])
                    if n:
                        pool.wait_ge(rotated, n)
                    pool.tensor_tensor(rot[:, 0], t[:, 0], sin, ALU.mult)
                    pool.tensor_tensor(rot[:, 1], t[:, 1], sin, ALU.mult).then_inc(rot_step, 1)
                    pool.wait_ge(rot_step, 2 * n + 1)
                    pool.tensor_tensor(t[:, 0], t[:, 0], cos, ALU.mult)
                    pool.tensor_tensor(t[:, 1], t[:, 1], cos, ALU.mult).then_inc(rot_step, 1)
                    pool.wait_ge(rot_step, 2 * n + 2)
                    pool.tensor_tensor(t[:, 0], t[:, 0], rot[:, 1], ALU.subtract)
                    pool.tensor_tensor(t[:, 1], t[:, 1], rot[:, 0], ALU.add).then_inc(rotated, 1)
                    n += 1
            for h in range(RH):
                for tau in range(NT):
                    n = NT * h + tau
                    pool.wait_ge(head_var, n + 1)
                    pool.tensor_scalar(head_stat[:, n, 8:9], head_stat[:, n, 7:8], 1e-5, None, ALU.add
                                       ).then_inc(head_eps, 1)
                    power(head_stat[:, n, 9:10], head_stat[:, n, 8:9], head_eps, n + 1
                          ).then_inc(head_rstd, 1)
                for tau in range(NT):
                    pool.wait_ge(*freed(("ro", h, tau)))
                    y = qkv[:, 0:2, tau, h * 256:(h + 1) * 256]
                    zh = z[:, h // 2, tau, (h % 2) * CB:(h % 2 + 1) * CB].rearrange("p (a c) -> p a c", a=2)
                    pool.tensor_tensor(y, y, zh, ALU.mult).then_inc(ret_ready, 1)
            pool.wait_ge(*freed(("rs", RH - 1)))
            spread_row(spread[:, 0, :], "ln_g")
            spread_row(spread[:, 1, :], "ln_b")
            for tau in range(NT):
                pool.wait_ge(ln_var, tau + 1)
                pool.tensor_scalar(ln_stat[:, tau, 14:15], ln_stat[:, tau, 13:14], 1e-5, None, ALU.add
                                   ).then_inc(ln_eps, 1)
                power(ln_stat[:, tau, 15:16], ln_stat[:, tau, 14:15], ln_eps, tau + 1).then_inc(ln_rstd, 1)
            pool.wait_ge(ln_step, 4 * NT)
            spread_row(spread[:, 0, :], "post_g")
            spread_row(spread[:, 1, :], "post0")
            pool.wait_ge(conv_act_ready, NT)
            pool.dma_start(x[:], x_in.rearrange("(t p) d -> p t d", p=P)).then_inc(x_again, 16)
            pool.wait_ge(row_loaded["post_g"], 16)
            pool.wait_ge(*freed(("gate", 1)))
            pool.tensor_tensor(gate_bc[:], gate_bc[:], spread[:, 0, :], ALU.mult).then_inc(factor_ready, 1)
            pool.wait_ge(row_loaded["post0"], 16)
            pool.tensor_scalar(spread[:, 1, :], spread[:, 1, :], 0.5, None, ALU.mult).then_inc(factor_ready, 1)
            pool.wait_ge(factor_ready, 1)
            spread_row(spread[:, 0, :], "mix_norm")
            norm("post_w")
            norm("pre1")
            norm("post_f1")
            pool.wait_ge(ss_ready, SUMS_BEFORE["post_f1"] + 4)
            for dst, src, loaded in ((gw[:], gates_w, gw_loaded), (gbias[:], gate_bias.partition_broadcast(P), gbias_loaded),
                                   (qs[:, 0, :], level_in, level_loaded),
                                   (causal[:], causal_in, causal_loaded), (sel[:], sel_in, sel_loaded)):
                pool.dma_start(dst, src).then_inc(loaded, 16)
            pool.memset(hsc[:], 0.0).then_inc(hsc_clear, 1)
            pool.memset(mqk_pad[:, :, 0:CW2 - 1], 0.0).then_inc(mqk_pad_ready, 1)
            pool.memset(mv[:, :, :, P:P + 1], 1.0).then_inc(mv_ones, 1)
            norm("pre2")
            pool.wait_ge(level_loaded, 16)
            pool.tensor_copy(level[:], qs[:, 0, :].rearrange("p (l t) -> p l t", l=8)).then_inc(level_ready, 1)
            pool.memset(keep, 1.0).then_inc(keep_step, 1)
            pool.wait_ge(keep_step, 1)
            pool.memset(keep[:, :, 0:S:CHUNK], 0.0).then_inc(keep_step, 1)
            pool.wait_ge(log_f_ready, 1)
            pool.tensor_scalar(hk_T[:], hk_T[:], -1.0, 1.0, ALU.mult, ALU.add).then_inc(hk_T_ready, 1)
            pool.wait_ge(mw_exp, 1)
            pool.wait_ge(causal_loaded, 16)
            mask = causal[:].unsqueeze(1).to_broadcast([P, NH, P])
            pool.tensor_tensor(mw[:, :, 0:P], mw[:, :, 0:P], mask, ALU.mult)
            pool.tensor_tensor(mw[:, :, S:S + P], mw[:, :, S:S + P], mask, ALU.mult).then_inc(mw_masked, 1)
            mix = first("mixi")
            pool.wait_ge(row_loaded["mix_norm"], 16)
            pool.wait_ge(*drained(mix + 5))
            hg_n = spread[:, 0, 0:CB].unsqueeze(1).to_broadcast([P, NT, CB])
            ml_n = spread[:, 0, CB:D].unsqueeze(1).to_broadcast([P, NT, CB])
            pool.tensor_tensor(hgate[:], hgate[:], hg_n, ALU.mult).then_inc(gates_scaled, 1)
            pool.wait_ge(*drained(mix + 6))
            pool.tensor_scalar(mo[:], mo[:], 0.5, 0.5, ALU.mult, ALU.add).then_inc(mo_step, 1)
            pool.wait_ge(mo_step, 1)
            pool.tensor_tensor(mo[:], mo[:], ml_n, ALU.mult).then_inc(gates_scaled, 1)
            for n in range(2):
                pool.wait_ge(mix_ss, n + 1)
                pool.tensor_scalar(mstat[:, 2 * n + 1, :], mstat[:, 2 * n, :], 1.0 / P, 1e-6, ALU.mult, ALU.add
                                   ).then_inc(mix_var, 1)
                power(mstat[:, 4 + n, :], mstat[:, 2 * n + 1, :], mix_var, n + 1).then_inc(mix_rstd, 1)
            pool.wait_ge(gates_scaled, 2)
            spread_row(spread[:, 1, :], "post1")
            spread_row(spread[:, 0, :], "post2")
            pool.wait_ge(row_loaded["post2"], 16)
            pool.tensor_scalar(spread[:, 0, :], spread[:, 0, :], 0.5, None, ALU.mult).then_inc(factor_ready, 1)
            norm("post_m")
            norm("pre3")
            norm("post_f2")

        @block.vector
        def _(dve):
            def lo_parts(b, off=None):
                for n in range(split_to(b - 1) if b >= 0 else 0, split_to(b)):
                    dve.wait_ge(w_hi_ready, plus(n + 1, off, UPG))
                    dve.tensor_tensor(w_lo[:, n % RING, :], raw[:, n % RAW, :], w_hi[:, n % RING, :].bitcast(F32),
                                      ALU.subtract).then_inc(w_lo_ready, 1)

            def lo_of(key, j, dst, hi, count, scale=1.0):
                dve.wait_ge(act_hi_ready, count)
                src = side((key, j))[:].rearrange("p (k s) -> p k s", s=S)
                if scale == 1.0:
                    ins = dve.tensor_tensor(dst, src, hi.bitcast(F32), ALU.subtract)
                else:
                    ins = dve.scalar_tensor_tensor(dst, src, scale, hi.bitcast(F32), ALU.mult, ALU.subtract)
                ins.then_inc(side_free((key, j)), 1)

            def lo_scaled(key, at):
                for j in range(4):
                    for n in range(2):
                        k = 2 * j + n
                        dve.wait_ge(act_hi_ready, HI_BEFORE[key] + 2 * (j + 1))
                        ins = dve.scalar_tensor_tensor(act_lo[:, k, :], side((key, j))[:, n * S:(n + 1) * S],
                                                       cv("pre2", at + k), act_hi[:, k, :].bitcast(F32),
                                                       ALU.mult, ALU.subtract)
                    ins.then_inc(side_free((key, j)), 1)

            def normalise(name):
                dve.wait_ge(rstd_ready, NORMS.index(name) + 1)
                for tau in range(NT):
                    dve.tensor_scalar(tmp[:, tau, :], x[:, tau, :], sums(name)[2][:, tau:tau + 1], None, ALU.mult
                                      ).then_inc(normed, 1)

            dve.wait_ge(col_loaded, 16)
            for k in range(KD):
                dve.wait_ge(ada_loaded[k % 4], 16 * (k // 4 + 1))
                if k == 0:
                    ins = dve.tensor_scalar(ada_acc[:], ada_w[:, 0, :], cv("c", 0), None, ALU.mult)
                else:
                    dve.wait_ge(ada_summed, k)
                    ins = dve.scalar_tensor_tensor(ada_acc[:], ada_w[:, k % 4, :], cv("c", k), ada_acc[:],
                                                   ALU.mult, ALU.add)
                ins.then_inc(ada_summed, 1)
                if k == 1:
                    normalise("pre0")
            dve.wait_ge(*full("shift_scale"))
            dve.tensor_tensor(mod_T[:], side("shift_scale")[:, 0:16], cv("b_shift", 0, 16), ALU.add
                              ).then_inc(side_free("shift_scale"), 1)
            dve.wait_ge(*freed("shift_scale"))
            dve.scalar_tensor_tensor(mod_T[:, 8:16], mod_T[:, 8:16], 1.0, cv("pre_g", 0, 8), ALU.add, ALU.mult
                                     ).then_inc(mod_ready, 1)
            dve.wait_ge(row_loaded["b_gate"], 16)
            for j in range(2):
                dve.wait_ge(*full(("gate", j)))
                cs = slice(j * CB, (j + 1) * CB)
                dve.tensor_tensor(gate_bc[:, cs], gate_bc[:, cs], side(("gate", j))[:], ALU.add
                                  ).then_inc(side_free(("gate", j)), 1)
            dve.wait_ge(mod_ready, 1)
            for j in range(4):
                dve.wait_ge(*full(("pre0", j)))
                for k in (2 * j, 2 * j + 1):
                    ins = dve.tensor_scalar(h_T[:, k, :], side(("pre0", j))[:, (k % 2) * S:(k % 2 + 1) * S],
                                            mod_T[:, 8 + k:9 + k], mod_T[:, k:k + 1], ALU.mult, ALU.add)
                ins.then_inc(side_free(("pre0", j)), 1)
            lo_parts(-1)
            for j in range(4):
                dve.wait_ge(act_hi_ready, j + 1)
                dve.wait_ge(*freed(("pre0", j)))
                dve.tensor_tensor(act_lo[:, 2 * j:2 * j + 2, :], h_T[:, 2 * j:2 * j + 2, :],
                                  act_hi[:, 2 * j:2 * j + 2, :].bitcast(F32), ALU.subtract
                                  ).then_inc(act0_ready, 1)
            for b in range(4):
                lo_parts(b)
                for tau in range(NT):
                    dve.wait_ge(tanh_ready, 2 * b + tau + 1)
                    ins = dve.scalar_tensor_tensor(tmp[:, tau, b * 256:(b + 1) * 256], tanh_u[:, tau, :], 1.0,
                                                   part_of(b, tau)[:, 0:256], ALU.add, ALU.mult)
                ins.then_inc(pair_free(b), 1)

            def conv_taps(tile, taps, before):
                acc = (tmp_T[:, tile, :], odd_taps)
                for t in taps:
                    src = a_T[:, tile, t:t + S]
                    w = conv_w[:, bass.ds(tile, 1), t:t + 1]
                    if t >= 2:
                        dve.wait_ge(conv_step, before + (t - 1))
                    else:
                        dve.wait_ge(conv_step, before)
                    if t == 0:
                        ins = dve.tensor_scalar(acc[0], src, w, conv_b[:, bass.ds(tile, 1)], ALU.mult, ALU.add)
                    elif t == 1:
                        ins = dve.tensor_scalar(acc[1], src, w, None, ALU.mult)
                    else:
                        ins = dve.scalar_tensor_tensor(acc[t % 2], src, w, acc[t % 2], ALU.mult, ALU.add)
                    ins.then_inc(conv_step, 1)
                if taps[-1] == CW - 1:
                    dve.wait_ge(conv_step, before + CW)
                    dve.tensor_tensor(acc[0], acc[0], acc[1], ALU.add).then_inc(conv_step, 1)

            conv_w = cv("conv_w", 0, KD * CW).rearrange("p (k t) -> p k t", t=CW)
            conv_b = cv("conv_b", 0, KD)
            dve.memset(odd_taps, 0.0).then_inc(conv_step, 1)
            first_taps, last_taps = list(range(16)), list(range(16, CW))
            for j in range(4):
                dve.wait_ge(*freed(("aT", j)))
            with dve.Fori(0, 4) as i:
                for n, taps in enumerate((first_taps, last_taps)):
                    lo_parts(first("qk") + n, i)
                    conv_taps(i, taps, i * (CW + 1) + 1)
            with dve.Fori(0, 2) as i:
                for n, taps in enumerate((first_taps, last_taps)):
                    lo_parts(first("z") + n, i)
                    conv_taps(i + 4, taps, (i + 4) * (CW + 1) + 1)

            def head_mask(h):
                dve.wait_ge(*full(("rs", h)))
                dve.tensor_tensor(masked[:, h % 2, :], side(("rs", h))[:, 0:3 * P], decay[:, h, :], ALU.mult
                                  ).then_inc(side_free(("rs", h)), 1)

            def head_norm(h):
                for tau in range(NT):
                    n = NT * h + tau
                    dve.wait_ge(*full(("ro", h, tau)))
                    dve.bn_stats(head_stat[:, n, 0:6], side(("ro", h, tau))[:]).then_inc(head_bn, 1)
                for tau in range(NT):
                    n = NT * h + tau
                    dve.wait_ge(head_bn, n + 1)
                    dve.bn_aggr(head_stat[:, n, 6:8], head_stat[:, n, 0:6]).then_inc(head_var, 1)
                for tau in range(NT):
                    n = NT * h + tau
                    dve.wait_ge(head_rstd, n + 1)
                    dve.tensor_scalar(qkv[:, 0:2, tau, h * 256:(h + 1) * 256],
                                      side(("ro", h, tau))[:].rearrange("p (a c) -> p a c", a=2),
                                      head_stat[:, n, 6:7], head_stat[:, n, 9:10], ALU.subtract, ALU.mult
                                      ).then_inc(side_free(("ro", h, tau)), 1)

            dve.wait_ge(decay_loaded, 16)
            for m in range(6):
                lo_parts(first("zc") + m)
                if m >= 2:
                    head_norm(m - 2)
                if 1 <= m <= 4:
                    head_mask(m - 1)
                if m < 4:
                    conv_taps(6 + m // 2, last_taps if m % 2 else first_taps, (6 + m // 2) * (CW + 1) + 1)
            for j in range(8):
                lo_of("retT", j, ret_lo[:, 2 * j:2 * j + 2, :], ret_hi[:, 2 * j:2 * j + 2, :], HI_BEFORE["retT"] + j + 1)
            lo_parts(first("ret"))
            for tau in range(NT):
                for half in range(2):
                    key = ("cvtok", 2 * tau + half)
                    dve.wait_ge(*full(key))
                    dve.bn_stats(ln_stat[:, tau, 6 * half:6 * half + 6], side(key)[:]).then_inc(ln_bn, 1)
            for tau in range(NT):
                dve.wait_ge(ln_bn, 2 * tau + 2)
                dve.bn_aggr(ln_stat[:, tau, 12:14], ln_stat[:, tau, 0:12]).then_inc(ln_var, 1)
            for tau in range(NT):
                dve.wait_ge(ln_rstd, tau + 1)
                for half in range(2):
                    key = ("cvtok", 2 * tau + half)
                    dve.tensor_scalar(tmp[:, tau, half * CB:(half + 1) * CB], side(key)[:], ln_stat[:, tau, 12:13],
                                      ln_stat[:, tau, 15:16], ALU.subtract, ALU.mult).then_inc(side_free(key), 1)
            dve.wait_ge(row_loaded["ln_g"], 16)
            dve.wait_ge(row_loaded["ln_b"], 16)
            for tau in range(NT):
                dve.wait_ge(*freed(("cvtok", 2 * tau + 1)))
                dve.tensor_tensor(tmp[:, tau, :], tmp[:, tau, :], spread[:, 0, :], ALU.mult).then_inc(ln_step, 3)
            for tau in range(NT):
                dve.wait_ge(ln_step, 3 * (tau + 1))
                dve.tensor_tensor(tmp[:, tau, :], tmp[:, tau, :], spread[:, 1, :], ALU.add).then_inc(ln_step, 1)

            def branch(b, which, c):
                dve.wait_ge(*done(b))
                for tau in range(NT):
                    dst = g[:, which, tau, c * CB:(c + 1) * CB]
                    ins = dve.scalar_tensor_tensor(dst, dst, 1.0, part_of(b, tau)[:], ALU.add, ALU.mult)
                ins.then_inc(pair_free(b), 1)

            def merge(c):
                dve.wait_ge(*drained(first("conv") + c))
                for tau in range(NT):
                    cs = slice(c * CB, (c + 1) * CB)
                    dve.tensor_tensor(g[:, 0, tau, cs], g[:, 0, tau, cs], g[:, 1, tau, cs], ALU.add
                                      ).then_inc(merged, 1)

            for tau in range(NT):
                dve.wait_ge(conv_silu, tau + 1)
                dve.tensor_tensor(tmp[:, tau, :], tmp[:, tau, :], x[:, tau, :], ALU.mult).then_inc(conv_act_ready, 1)
            branch(first("ret"), 0, 0)
            lo_parts(first("ret") + 1)
            for j in range(4):
                lo_of("cvT", j, act_lo[:, 2 * j:2 * j + 2, :], act_hi[:, 2 * j:2 * j + 2, :], HI_BEFORE["cvT"] + j + 1)
            branch(first("ret") + 1, 0, 1)
            lo_parts(first("conv"))
            branch(first("conv"), 1, 0)
            merge(0)
            lo_parts(first("conv") + 1)
            for j in range(4):
                if j == 2:
                    branch(first("conv") + 1, 1, 1)
                    merge(1)
                lo_of("mgT", j, ret_lo[:, 2 * j:2 * j + 2, :], ret_hi[:, 2 * j:2 * j + 2, :],
                      HI_BEFORE["mgT"] + j + 1, scale=0.5)

            def post(name, stage, factor, scaled_before):
                for c in range(2):
                    b = first(stage) + c
                    lo_parts(b)
                    dve.wait_ge(*done(b))
                    for tau in range(NT):
                        ins = dve.tensor_copy(tmp[:, tau, c * CB:(c + 1) * CB], part_of(b, tau)[:])
                    ins.then_inc(pair_free(b), 1)
                dve.wait_ge(rstd_ready, NORMS.index(name) + 1)
                for tau in range(NT):
                    dve.scalar_tensor_tensor(tmp[:, tau, :], tmp[:, tau, :], sums(name)[2][:, tau:tau + 1], factor,
                                             ALU.mult, ALU.mult).then_inc(post_scaled, 1)
                for tau in range(NT):
                    dve.wait_ge(post_scaled, scaled_before + tau + 1)
                    dve.tensor_tensor(x[:, tau, :], x[:, tau, :], tmp[:, tau, :], ALU.add).then_inc(x_ready, 1)

            def pre(name, at):
                dve.wait_ge(x_ready, 2 * sum(n.startswith("post") for n in NORMS[:NORMS.index(name)]))
                normalise(name)
                lo_scaled(name, at)

            def feed_forward(which, stage):
                b0 = first(stage)
                hi_before = HI_BEFORE[("ffT", which)]
                silu_before = which * 2 * FB

                def gate(b, parity, off=None):
                    for tau in range(NT):
                        dve.wait_ge(silu_ready, plus(silu_before + 2 * (b - b0) + tau + 1, off, 4))
                        ins = dve.tensor_tensor(ff_tok[:, parity, tau, :], silu_g[:, tau, :], part_of(b, tau)[:, 256:512],
                                                ALU.mult)
                    ins.then_inc(pair_free(b), 1)

                def hidden_lo(parity, j, count, off=None):
                    key = ("ffT", which, parity)
                    dve.wait_ge(act_hi_ready, count)
                    dve.tensor_tensor(ff_lo[:, j, :], side(key)[:], ff_hi[:, j, :].bitcast(F32), ALU.subtract
                                      ).then_inc(side_free(key), 1)

                lo_parts(b0)
                gate(b0, 0)
                with dve.Fori(0, (FB - 1) // 2) as i:
                    for n in range(2):
                        lo_parts(b0 + 1 + n, i)
                        gate(b0 + 1 + n, 1 - n, i)
                        hidden_lo(n, 2 * i + n, plus(hi_before + n + 1, i, 2), i)
                hidden_lo(0, FB - 1, hi_before + FB)

            dve.wait_ge(x_again, 16)
            dve.wait_ge(factor_ready, 1)
            post("post_w", "wout", gate_bc[:], 0)
            pre("pre1", 0)
            feed_forward(0, "f1i")
            dve.wait_ge(factor_ready, 2)
            post("post_f1", "f1o", spread[:, 1, :], 2)
            l0, l1 = cv("lb", 0, NH), cv("lb", NH, NH)
            dve.tensor_tensor(lb[:, 0, :], l0, l1, ALU.max).then_inc(lb_step, 1)
            dve.wait_ge(lb_step, 1)
            dve.tensor_tensor(lb[:, 1, :], l0, lb[:, 0, :], ALU.subtract).then_inc(lb_step, 1)
            dve.tensor_tensor(lb[:, 2, :], l1, lb[:, 0, :], ALU.subtract).then_inc(lb_step, 1)
            dve.wait_ge(gw_hi_ready, 1)
            dve.tensor_tensor(gw_lo[:], gw[:], gw_hi[:].bitcast(F32), ALU.subtract).then_inc(gw_ready, 2)
            dve.wait_ge(lb_exp, 1)
            dve.tensor_tensor(lb[:, 3, :], lb[:, 1, :], lb[:, 2, :], ALU.add).then_inc(lb_step, 1)
            dve.wait_ge(lb_step, 4)
            dve.reciprocal(lb[:, 3, :], lb[:, 3, :]).then_inc(lb_step, 1)
            dve.wait_ge(lb_step, 5)
            dve.tensor_tensor(lb[:, 4, :], lb[:, 1, :], lb[:, 3, :], ALU.mult).then_inc(lb_step, 1)
            dve.tensor_tensor(lb[:, 5, :], lb[:, 2, :], lb[:, 3, :], ALU.mult).then_inc(lb_step, 1)
            pre("pre2", 8)
            mix = first("mixi")
            lo_parts(mix)
            dve.wait_ge(*full("gates"))
            dve.wait_ge(gbias_loaded, 16)
            dve.tensor_tensor(gt[:], side("gates")[:, 0:16].rearrange("p (t c) -> p t c", t=NT),
                              gbias[:].unsqueeze(1).to_broadcast([P, NT, 8]), ALU.add).then_inc(side_free("gates"), 1)
            lo_parts(mix + 1)
            dve.wait_ge(lb_step, 7)
            for j in range(2):
                dve.wait_ge(*full(("hfT", j)))
                for h in (2 * j, 2 * j + 1):
                    ins = dve.tensor_scalar(hk_T[:, h, :], side(("hfT", j))[:, (h % 2) * S:(h % 2 + 1) * S],
                                            lb[:, 5, h:h + 1], lb[:, 4, h:h + 1], ALU.mult, ALU.add)
                ins.then_inc(side_free(("hfT", j)), 1)
            lo_parts(mix + 2)
            dve.wait_ge(log_f_ready, 1)
            dve.wait_ge(keep_step, 2)
            dve.tensor_tensor_scan(cum[:].rearrange("p h s -> p (h s)"), keep.rearrange("p h s -> p (h s)"),
                                   dec[:].rearrange("p h s -> p (h s)"), 0.0, ALU.mult, ALU.add
                                   ).then_inc(cum_ready, 1)

            def level_diff(lv):
                n = 2 ** (lv - 1)
                if lv == 1:
                    dve.wait_ge(cum_ready, 1)
                else:
                    dve.wait_ge(scaled_ready, 2 * (lv - 1))
                if lv <= 6:
                    c = cum[:].rearrange("p h (b a n) -> p (h b) a n", a=2, n=n)
                    d = dec[:].rearrange("p h (b a n) -> p (h b) a n", a=2, n=n)
                    middle = c[:, :, 0, n - 1:n].to_broadcast([P, NH * S // (2 * n), n])
                    dve.tensor_tensor(d[:, :, 1, :], c[:, :, 1, :], middle, ALU.subtract)
                    ins = dve.tensor_tensor(d[:, :, 0, :], middle, c[:, :, 0, :], ALU.subtract)
                else:
                    c = cum[:].rearrange("p h (b n) -> p h b n", n=CHUNK)
                    d = dec[:].rearrange("p h (b n) -> p h b n", n=CHUNK)

                    def chunk_sum(b):
                        return c[:, :, b, CHUNK - 1:CHUNK].to_broadcast([P, NH, CHUNK])

                    if lv == 7:
                        for b in (0, 2):
                            dve.tensor_tensor(d[:, :, b, :], chunk_sum(b), c[:, :, b, :], ALU.subtract)
                            ins = dve.tensor_copy(d[:, :, b + 1, :], c[:, :, b + 1, :])
                    else:
                        dve.tensor_tensor(d[:, :, 0, :], chunk_sum(0), c[:, :, 0, :], ALU.subtract)
                        dve.tensor_tensor(d[:, :, 1, :], chunk_sum(1), c[:, :, 1, :], ALU.subtract)
                        dve.tensor_copy(d[:, :, 2, :], c[:, :, 2, :])
                        dve.tensor_tensor(d[:, :, 3, :], c[:, :, 3, :], chunk_sum(2), ALU.add
                                          ).then_inc(diff_part, 1)
                        dve.wait_ge(diff_part, 1)
                        ins = dve.tensor_tensor(d[:, :, 0, :], d[:, :, 0, :], chunk_sum(1), ALU.add)
                ins.then_inc(diff_ready, 1)

            def level_scale(lv):
                dve.wait_ge(exp_ready, lv)
                d = dec[:].rearrange("p h s -> p (h s)")
                dve.tensor_tensor(qs[:, lv % 2, :], hq_T[:].rearrange("p h s -> p (h s)"), d, ALU.mult
                                  ).then_inc(scaled_ready, 1)
                dve.tensor_tensor(ks[:, lv % 2, :], hk_T[:].rearrange("p h s -> p (h s)"), d, ALU.mult
                                  ).then_inc(scaled_ready, 1)

            def level_take(lv):
                for blk in range(NT):
                    key = ("lv", lv, blk)
                    dve.wait_ge(*full(key))
                    if lv:
                        dve.wait_ge(*freed(("lv", lv - 1, blk)))
                    dve.copy_predicated(hsc[:, blk, :, :], level[:, lv, :].unsqueeze(1).to_broadcast([P, NH, P]),
                                        side(key)[:].rearrange("p (h t) -> p h t", h=NH)).then_inc(side_free(key), 1)

            level_diff(1)
            dve.wait_ge(row_step, 3)
            i_row, f_row = side("gatesT")[0:NH, 0:S], side("gatesT")[0:NH, S:2 * S]
            dve.scalar_tensor_tensor(row[:, 0, :], f_row, 0.0, row[:, 2, :], ALU.min, ALU.subtract
                                     ).then_inc(row_step, 1)
            dve.wait_ge(row_step, 4)
            dve.tensor_tensor_scan(row[:, 1, :], row[:, 0, :], row[:, 0, :], 0.0, ALU.add, ALU.min
                                   ).then_inc(row_step, 1)
            dve.wait_ge(row_step, 5)
            dve.tensor_tensor(row[:, 0, :], i_row, row[:, 1, :], ALU.subtract).then_inc(side_free("gatesT"), 1)
            dve.wait_ge(*freed("gatesT"))
            dve.tensor_tensor_scan(row[:, 2, :], row[:, 0, :], row[:, 0, :], 0.0, ALU.max, ALU.max
                                   ).then_inc(row_step, 1)
            dve.wait_ge(row_step, 6)
            dve.tensor_tensor(row[:, 3, :], row[:, 1, :], row[:, 2, :], ALU.add).then_inc(row_step, 1)
            lo_parts(mix + 3)
            dve.wait_ge(*freed("umT"))
            for j in range(2):
                dve.wait_ge(*full(("mb", j)))
                for n in range(2):
                    h = 2 * j + n
                    m_all = side(("mb", j))[:, n * S:(n + 1) * S]
                    dve.tensor_scalar(mw[:, h, 0:S], m_all, um[:, h:h + 1], 0.0, ALU.subtract, ALU.max)
                    ins = dve.tensor_scalar(mw[:, h, S:S + P], m_all[:, P:S], um[:, 4 + h:5 + h], 0.0,
                                            ALU.subtract, ALU.max)
                ins.then_inc(side_free(("mb", j)), 1)
            dve.wait_ge(hk_T_ready, 1)
            dve.wait_ge(hsc_clear, 1)
            dve.wait_ge(level_ready, 1)
            level_scale(1)
            level_diff(2)
            lo_parts(mix + 4)
            level_take(0)
            level_scale(2)
            level_diff(3)
            level_take(1)
            level_scale(3)
            level_diff(4)
            lo_parts(mix + 5)
            level_take(2)
            level_scale(4)
            level_diff(5)
            level_take(3)
            for j in range(2):
                dve.wait_ge(*freed(("cv2T", j)))
            for t in range(CW2):
                for k in range(4):
                    w = cv("conv_w2", k * CW2 + t)
                    if t:
                        dve.wait_ge(conv2_step, 4 * (t - 1) + k + 1)
                        ins = dve.scalar_tensor_tensor(mqk_T[:, k, :], mqk_pad[:, k, t:t + S], w, mqk_T[:, k, :],
                                                       ALU.mult, ALU.add)
                    else:
                        ins = dve.tensor_scalar(mqk_T[:, k, :], mqk_pad[:, k, 0:S], w, cv("conv_b2", k),
                                                ALU.mult, ALU.add)
                    ins.then_inc(conv2_step, 1)
            level_scale(5)
            level_diff(6)
            lo_parts(mix + 6)
            level_take(4)
            level_scale(6)
            level_diff(7)
            level_take(5)
            level_scale(7)
            level_diff(8)
            level_take(6)
            level_scale(8)
            level_take(7)
            dve.wait_ge(mw_masked, 1)
            for h in range(NH):
                dve.wait_ge(*full(("ms", h)))
                dve.scalar_tensor_tensor(mw[:, h, :], side(("ms", h))[:, 0:3 * P], QK ** -0.5, mw[:, h, :],
                                         ALU.mult, ALU.mult).then_inc(side_free(("ms", h)), 1)
            dve.wait_ge(*full(("lv", 8, 0)))
            dve.tensor_copy(hoff[:], side(("lv", 8, 0))[:].rearrange("p (h t) -> p h t", h=NH)
                            ).then_inc(side_free(("lv", 8, 0)), 1)
            for tau in range(NT):
                for j in range(2):
                    key = ("mn", tau, j)
                    dve.wait_ge(*full(key))
                    n = 4 * tau + 2 * j
                    den = side(key)[:, 0:2 * (P + 1)].rearrange("p (h d) -> p h d", h=2)[:, :, P]
                    dve.scalar_tensor_tensor(mden[:, 0, n:n + 2], den, -1.0, um[:, 8 + n:10 + n], ALU.mult, ALU.max
                                             ).then_inc(mden_step, 1)
                    dve.wait_ge(mden_step, n + 1)
                    dve.tensor_tensor(mden[:, 0, n:n + 2], den, mden[:, 0, n:n + 2], ALU.max
                                      ).then_inc(mden_step, 1)
            dve.wait_ge(mden_step, 8)
            dve.reciprocal(mden[:, 1, :], mden[:, 0, :]).then_inc(mden_step, 1)
            dve.wait_ge(mden_step, 9)
            for tau in range(NT):
                for j in range(2):
                    key = ("mn", tau, j)
                    n = 4 * tau + 2 * j
                    num = side(key)[:, 0:2 * (P + 1)].rearrange("p (h d) -> p h d", h=2)[:, :, 0:P]
                    dst = qs[:, 1, n * P:(n + 2) * P].rearrange("p (h d) -> p h d", h=2)
                    dve.tensor_tensor(dst, num, mden[:, 1, n:n + 2].unsqueeze(2).to_broadcast([P, 2, P]), ALU.mult
                                      ).then_inc(side_free(key), 1)
            for n, (slot, gates, count) in enumerate(((1, mo, 1), (0, hgate, 3))):
                dve.wait_ge(mix_sq, count)
                dve.tensor_reduce(mstat[:, 2 * n, :], ks[:, slot, :].rearrange("p (h d) -> p h d", d=P), AX.X, ALU.add
                                  ).then_inc(mix_ss, 1)
                if slot == 0:
                    dve.wait_ge(*freed(("ho", 1)))
                o = qs[:, slot, :].rearrange("p (h d) -> p h d", d=P)
                dve.wait_ge(mix_rstd, n + 1)
                dve.tensor_tensor(o, o, mstat[:, 4 + n, :].unsqueeze(2).to_broadcast([P, 8, P]), ALU.mult
                                  ).then_inc(mix_scaled, 1)
                dve.wait_ge(mix_scaled, n + 1)
                dve.wait_ge(gates_scaled, 2)
                for tau in range(NT):
                    dve.tensor_tensor(tmp[:, tau, slot * CB:(slot + 1) * CB], qs[:, slot, tau * CB:(tau + 1) * CB],
                                      gates[:, tau, :], ALU.mult).then_inc(mixed, 1)
            for j in range(4):
                lo_of("mxT", j, act_lo[:, 2 * j:2 * j + 2, :], act_hi[:, 2 * j:2 * j + 2, :], HI_BEFORE["mxT"] + j + 1)
            dve.wait_ge(row_loaded["post1"], 16)
            post("post_m", "mixo", spread[:, 1, :], 4)
            pre("pre3", 16)
            feed_forward(1, "f2i")
            dve.wait_ge(factor_ready, 3)
            post("post_f2", "f2o", spread[:, 0, :], 6)


def kernel(**inputs):
    from concourse import bacc
    from concourse.bass_utils import run_bass_kernel_spmd

    a = {k: np.asarray(v) for k, v in inputs.items()}

    def units(w):
        k, n = w.shape
        return w.reshape(k // P, P, n // CB, CB).transpose(2, 0, 1, 3).reshape(-1, P, CB)

    def pairs(left, right):
        k, n = left.shape
        return np.stack([left.reshape(k, n // 256, 256), right.reshape(k, n // 256, 256)], axis=2).reshape(k, 2 * n)

    w_in = a["w_in"][0]
    q, k, v, z_ret, u_val, u_gate, z_conv, g_a, g_b = np.split(
        w_in, [1024, 2048, 4096, 6144, 7168, 8192, 9216, 10240], axis=1)
    mix_in = a["w_mix_in_2"][0]
    hq, hf, hi, hgate, mqk, mv, mo, gates = np.split(mix_in, [512, 1024, 1536, 2048, 2560, 3072, 3584], axis=1)
    all_units = np.concatenate([
        units(pairs(u_val, u_gate)), units(q), units(k), units(v), units(z_ret), units(z_conv), units(g_a), units(g_b),
        units(a["w_ret_out"][0]), units(a["w_conv_out"][0]), units(a["w_out"][0]),
        units(pairs(a["ffn1_w_in_2"][0][:, :FF], a["ffn1_w_in_2"][0][:, FF:])), units(a["ffn1_w_out_2"][0]),
        units(hq), units(hf), units(hi), units(mqk), units(mv), units(hgate), units(mo), units(a["w_mix_out_2"][0]),
        units(pairs(a["ffn2_w_in_2"][0][:, :FF], a["ffn2_w_in_2"][0][:, FF:])), units(a["ffn2_w_out_2"][0])])
    stream = np.ascontiguousarray(all_units.reshape(GROUPS, UPG, P, CB).transpose(0, 2, 1, 3)).reshape(
        GROUPS, P, UPG * CB)

    def columns(vec):
        return vec.reshape(-1, P).T

    def taps(w):
        return w.reshape(w.shape[0], -1, P).transpose(2, 1, 0).reshape(P, -1)

    b_ada = a["b_ada"][0]
    cols = np.ascontiguousarray(np.concatenate([
        columns(a["c"][0]), columns(a["pre_norm_g"][0]), columns(b_ada[:2 * D]), columns(a["conv_b"][0]),
        taps(a["conv_w"][0]), columns(a["norm_pre_2"][0]), columns(a["hgrn_lb_logits_2"][:2]), taps(a["conv_w_2"][0]),
        columns(a["conv_b_2"][0])], axis=1))
    rows = np.ascontiguousarray(np.stack([
        b_ada[2 * D:], a["conv_ln_g"][0], a["conv_ln_b"][0], a["post_norm_g"][0], a["norm_post_2"][0, 0],
        np.concatenate([a["hgrn_norm_2"][0], a["mlstm_norm_2"][0]]), a["norm_post_2"][0, 1], a["norm_post_2"][0, 2]]))

    idx = np.arange(P)
    log_gamma = np.log1p(-np.exp2(-5.0 - np.arange(RH)))
    gap = idx[None, :] - idx[:, None]
    decay = np.zeros((P, RH, 3 * P))
    for h in range(RH):
        same = np.where(gap >= 0, np.exp(log_gamma[h] * np.maximum(gap, 0)), 0.0)
        decay[:, h] = np.concatenate([same, np.exp(log_gamma[h] * (gap + P)), same], axis=1) / 16.0
    levels = np.zeros((P, 8, P), np.float32)
    levels[:, 0] = gap == 0
    for lv in range(1, 8):
        size = 2 ** lv
        s_, t_ = idx[:, None], idx[None, :]
        levels[:, lv] = (s_ // size == t_ // size) & (s_ % size < size // 2) & (t_ % size >= size // 2)
    sel = np.zeros((NH, NH, P), np.float32)
    for h in range(NH):
        sel[h, h] = 1.0
    inv_freq = np.float32(10000.0) ** (-np.arange(P, dtype=np.float32) / np.float32(P))
    arrays = {
        "stream": stream,
        "ada": np.ascontiguousarray(a["w_ada"][0].reshape(KD, P, 3 * D)),
        "gates_w": np.ascontiguousarray(gates.reshape(KD, P, 8).transpose(1, 0, 2).reshape(P, KD * 8)),
        "cols": cols, "rows": rows, "gate_bias": np.ascontiguousarray(a["mlstm_gate_bias_2"][0]),
        "x": np.ascontiguousarray(a["x"][0]),
        "pos": np.ascontiguousarray(a["positions"][0].reshape(NT, P).T),
        "ident": np.eye(P, dtype=np.float32),
        "inv_freq": np.ascontiguousarray(np.broadcast_to(inv_freq, (P, P))),
        "decay": decay.reshape(P, -1).astype(np.float32),
        "level": levels.reshape(P, -1),
        "causal": (gap >= 0).astype(np.float32),
        "sel": sel,
    }
    nc = bacc.Bacc("TRN2", target_bir_lowering=False, num_devices=1)
    args = [nc.dram_tensor(f"in_{n}", v.shape, mybir.dt.from_np(v.dtype), kind="ExternalInput").ap()
            for n, v in arrays.items()]
    args.append(nc.dram_tensor("out_x", (S, D), F32, kind="ExternalOutput").ap())
    build_program(nc, *args)
    r = run_bass_kernel_spmd(nc, [{f"in_{n}": v for n, v in arrays.items()}], core_ids=[0])
    return r.results[0]["out_x"].reshape(1, S, D)
```

```python
from contextlib import ExitStack

import numpy as np

import concourse.bass as bass
from concourse import mybir

F32 = mybir.dt.float32
F32R = mybir.dt.float32r
U8 = mybir.dt.uint8
I32 = mybir.dt.int32
ALU = mybir.AluOpType
ACT = mybir.ActivationFunctionType
AX = mybir.AxisListType

P = 128
S = 256
NT = S // P
D = 1024
KD = D // P
CB = 512
UPG = 4
RH = 4
CW = 31
CW2 = 4
FF = 2816
FB = FF // 256
KF = FF // P
NH = 4
CHUNK = 64
QK = 64

STAGES = {}
_b = 0
_UNIT0 = [0]
for _name, _n, _k in (("u", 4, KD), ("qk", 4, KD), ("v", 4, KD), ("z", 4, KD), ("zc", 2, KD), ("g", 4, KD),
                      ("ret", 2, 2 * KD), ("conv", 2, KD), ("wout", 2, KD),
                      ("f1i", FB, KD), ("f1o", 2, KF), ("mixi", 7, KD), ("mixo", 2, KD),
                      ("f2i", FB, KD), ("f2o", 2, KF)):
    STAGES[_name] = (_b, _n, _k)
    for _ in range(_n):
        _UNIT0.append(_UNIT0[-1] + _k)
    _b += _n
BLOCKS = _b
UNITS = _UNIT0[-1]
GROUPS = UNITS // UPG
assert UNITS % UPG == 0
RAW = 2
RING = 4


def first(stage):
    return STAGES[stage][0]


def group_end(b):
    return -(-_UNIT0[b + 1] // UPG)


def split_to(b):
    return min(group_end(min(b + 1, BLOCKS - 1)), group_end(b) + 2)


COLS = {}
_c = 0
for _name, _n in (("c", 8), ("pre_g", 8), ("b_shift", 8), ("b_scale", 8), ("conv_b", 8), ("conv_w", 8 * CW),
                  ("pre2", 24), ("lb", 8), ("conv_w2", 4 * CW2), ("conv_b2", 4)):
    COLS[_name] = _c
    _c += _n
NCOLS = _c

ROWS = ["b_gate", "ln_g", "ln_b", "post_g", "post0", "mix_norm", "post1", "post2"]

SIDE = {}
_uses = {4: 0, 5: 0, 6: 0, 7: 0}


def _side(key, bank, times=1):
    SIDE[key] = (bank, _uses[bank] + 1)
    _uses[bank] += times


def _side4(key):
    for j in range(4):
        _side((key, j), 4 + j)


def _plan_side():
    _side4("pre0")
    _side4("aT")
    _side(("gate", 0), 5)
    _side(("gate", 1), 6)
    for m in range(6):
        if m >= 2:
            _side(("ro", m - 2, 0), 7)
            _side(("ro", m - 2, 1), 4)
        if 1 <= m <= 4:
            _side(("rs", m - 1), 6)
        if m <= 3:
            _side(("qT", m), 4)
            _side(("kT", m), 5)
    for j in range(8):
        _side(("retT", j), 4 + j % 4)
    for key in ("cvtok", "cvT", "mgT", "pre1"):
        _side4(key)
    _side(("ffT", 0, 0), 4, (FB + 1) // 2)
    _side(("ffT", 0, 1), 5, FB // 2)
    _side4("pre2")
    _side("gates", 7)
    _side(("hqT", 0), 4)
    _side(("hqT", 1), 5)
    _side(("hfT", 0), 6)
    _side(("hfT", 1), 7)
    _side("gatesT", 6)
    _side("umT", 6)
    _side(("mb", 0), 4)
    _side(("mb", 1), 5)
    for lv in range(8):
        for blk in range(NT):
            _side(("lv", lv, blk), 4 + 2 * (lv % 2) + blk)
        if lv == 1:
            _side(("cv2T", 0), 4)
            _side(("cv2T", 1), 5)
    for h in range(NH):
        _side(("ms", h), 4 + h)
    _side(("lv", 8, 0), 4)
    for t in range(NT):
        for j in range(2):
            _side(("mn", t, j), 4 + 2 * t + j)
    _side(("ho", 0), 6)
    _side(("ho", 1), 7)
    for key in ("mxT", "pre3"):
        _side4(key)
    _side(("ffT", 1, 0), 4, (FB + 1) // 2)
    _side(("ffT", 1, 1), 5, FB // 2)


_plan_side()

HI_BEFORE = {}
_n = 0
for _name, _k in (("pre0", 4), ("retT", 8), ("cvT", 4), ("mgT", 4), ("pre1", 8), (("ffT", 0), FB), ("pre2", 8),
                  ("mxT", 4), ("pre3", 8), (("ffT", 1), FB)):
    HI_BEFORE[_name] = _n
    _n += _k

NORMS = ["pre0", "post_w", "pre1", "post_f1", "pre2", "post_m", "pre3", "post_f2"]
SUMS_BEFORE = {}
_n = 0
for _name in NORMS:
    SUMS_BEFORE[_name] = _n
    _n += 2 if _name.startswith("pre") else 4

PRES = [_name for _name in NORMS if _name.startswith("pre")]

TWO_PI = 2 * np.pi
TWO_PI_1 = 6.28125
TWO_PI_2 = float(np.round((TWO_PI - TWO_PI_1) * 2**21) / 2**21)
TWO_PI_3 = float(TWO_PI - TWO_PI_1 - TWO_PI_2)
ROUND = 1.5 * 2**23
PI_INSIDE = 3.1415925


def build_program(nc, stream, ada, gates_w, cols, rows, gate_bias, x_in, pos_in,
                  ident_in, inv_freq_in, decay_in, level_in, causal_in, sel_in, out):
    ctx = ExitStack()
    with ctx:
        def sb(name, shape, dt=F32, stack=ctx):
            return stack.enter_context(nc.sbuf_tensor(name, shape, dt))

        def sem(name):
            return ctx.enter_context(nc.semaphore(name))

        gate_w_loaded = [sem(f"gate_w_loaded{n}") for n in range(KD)]
        mod_summed = sem("mod_summed")
        post_bank_read = sem("post_bank_read")
        ada_summed = sem("ada_summed")
        gate_scaled = sem("gate_scaled")
        gate_summed = sem("gate_summed")
        pre_var_ready = sem("pre_var_ready")
        pre_rstd_ready = sem("pre_rstd_ready")
        post_var_ready = sem("post_var_ready")
        post_rstd_ready = sem("post_rstd_ready")
        half_rstd_ready = sem("half_rstd_ready")
        raw_loaded = [sem(f"raw_loaded{n}") for n in range(RAW)]
        ada_loaded = [sem(f"ada_loaded{n}") for n in range(KD)]
        row_loaded = {name: sem(f"{name}_loaded") for name in ROWS}
        pair_freed = [sem(f"pair_freed{n}") for n in range(2)]
        side_filled = [sem(f"side_filled{n}") for n in range(4, 8)]
        side_freed = [sem(f"side_freed{n}") for n in range(4, 8)]
        x_loaded = sem("x_loaded")
        col_loaded = sem("col_loaded")
        ident_loaded = sem("ident_loaded")
        pos_loaded = sem("pos_loaded")
        freq_loaded = sem("freq_loaded")
        decay_loaded = sem("decay_loaded")
        w_lo_ready = sem("w_lo_ready")
        x_ready = sem("x_ready")
        out_written = sem("out_written")
        w_used = sem("w_used")
        normed = sem("normed")
        ones_ready = sem("ones_ready")
        act0_ready = sem("act0_ready")
        rotated = sem("rotated")
        ret_ready = sem("ret_ready")
        conv_step = sem("conv_step")
        conv_act_ready = sem("conv_act_ready")
        merged = sem("merged")
        gw_ready = sem("gw_ready")
        row_step = sem("row_step")
        sel_loaded = sem("sel_loaded")
        scaled_ready = sem("scaled_ready")
        hk_T_ready = sem("hk_T_ready")
        mqk_T_ready = sem("mqk_T_ready")
        mv_ones = sem("mv_ones")
        mixed = sem("mixed")
        w_hi_ready = sem("w_hi_ready")
        ss_ready = sem("ss_ready")
        act_hi_ready = sem("act_hi_ready")
        trig_step = sem("trig_step")
        trig_ready = sem("trig_ready")
        tanh_ready = sem("tanh_ready")
        pad_ready = sem("pad_ready")
        ln_step = sem("ln_step")
        conv_silu = sem("conv_silu")
        silu_ready = sem("silu_ready")
        gw_loaded = sem("gw_loaded")
        gw_hi_ready = sem("gw_hi_ready")
        lb_step = sem("lb_step")
        lb_exp = sem("lb_exp")
        log_f_ready = sem("log_f_ready")
        mw_exp = sem("mw_exp")
        diff_ready = sem("diff_ready")
        exp_ready = sem("exp_ready")
        mqk_pad_ready = sem("mqk_pad_ready")
        conv2_step = sem("conv2_step")
        mix_sq = sem("mix_sq")
        half_ready = sem("half_ready")
        rot_step = sem("rot_step")
        head_var = sem("head_var")
        head_eps = sem("head_eps")
        head_rstd = sem("head_rstd")
        ln_var = sem("ln_var")
        ln_eps = sem("ln_eps")
        ln_rstd = sem("ln_rstd")
        x_again = sem("x_again")
        factor_ready = sem("factor_ready")
        gbias_loaded = sem("gbias_loaded")
        level_loaded = sem("level_loaded")
        causal_loaded = sem("causal_loaded")
        hsc_clear = sem("hsc_clear")
        level_ready = sem("level_ready")
        keep_step = sem("keep_step")
        mw_masked = sem("mw_masked")
        gates_scaled = sem("gates_scaled")
        mo_step = sem("mo_step")
        mix_ss = sem("mix_ss")
        mix_var = sem("mix_var")
        mix_rstd = sem("mix_rstd")
        mod_ready = sem("mod_ready")
        head_bn = sem("head_bn")
        ln_bn = sem("ln_bn")
        cum_ready = sem("cum_ready")
        diff_part = sem("diff_part")
        mden_step = sem("mden_step")
        mix_scaled = sem("mix_scaled")

        raw = sb("raw", [P, RAW, UPG * CB])
        w_hi = sb("w_hi", [P, RING, UPG * CB], F32R)
        w_lo = sb("w_lo", [P, RING, UPG * CB], F32R)
        act_hi = sb("act_hi", [P, KD, S], F32R)
        act_lo = sb("act_lo", [P, KD, S], F32R)
        x = sb("x", [P, NT, D])
        tmp = sb("tmp", [P, NT, D])
        tmp_T = tmp[:].rearrange("p t d -> p (t d)").rearrange("p (k s) -> p k s", s=S)
        spread = sb("spread", [P, 2, D])
        gate_bc = sb("gate_bc", [P, D])
        ident = sb("ident", [P, P])
        col = sb("col", [P, NCOLS])
        half_power = sb("half_power", [P, 8])
        stat = sb("stat", [P, 8 * len(NORMS)])
        head_stat = sb("head_stat", [P, NT * RH, 10])
        ln_stat = sb("ln_stat", [P, NT, 16])
        junk = sb("junk", [P, D])
        bank = [ctx.enter_context(nc.psum_tensor(f"bank{i}", [P, CB], F32)) for i in range(8)]

        with ExitStack() as own:
            ada_w = sb("ada_w", [P, KD, 2 * D], stack=own)
            mod_T = sb("mod_T", [P, 16], stack=own)
            h_T = sb("h_T", [P, KD, S], stack=own)
            ang = sb("ang", [P, NT, 2, P], stack=own)
            turns = sb("turns", [P, NT, 2, P], stack=own)
            inv_freq = sb("inv_freq", [P, P], stack=own)
            pos_i = sb("pos_i", [P, NT], I32, stack=own)
            pos_f = sb("pos_f", [P, NT], stack=own)
        with ExitStack() as own:
            qkv = sb("qkv", [P, 4, NT, D], stack=own)
            z = sb("z", [P, 2, NT, D], stack=own)
            g = sb("g", [P, 2, NT, D], stack=own)
            a_T = sb("a_T", [P, KD, S + CW - 1], stack=own)
            qk_T = sb("qk_T", [P, 2, 2, S], stack=own)
        with ExitStack() as own:
            sb("under_ret", [P, 2, NT, D], stack=own)
            ret_hi = sb("ret_hi", [P, 2 * KD, S], F32R, stack=own)
            ret_lo = sb("ret_lo", [P, 2 * KD, S], F32R, stack=own)
        flat = spread[:].rearrange("p a d -> p (a d)")
        trig = flat[:, 0:512].rearrange("p (t w f) -> p t w f", t=NT, w=2)
        decay = flat[:, 512:2048].rearrange("p (h c) -> p h c", h=RH)
        part = flat[:, 512:1024].rearrange("p (t w f) -> p t w f", t=NT, w=2)
        masked = junk[:, 0:768].rearrange("p (a c) -> p a c", a=2)
        odd_taps = junk[:, 768:1024]
        ones = junk[:, 512:640]
        tanh_u = junk[:, 0:512].rearrange("p (t c) -> p t c", t=NT)
        gate_sum = qk_T[:].rearrange("p w k s -> p (w k s)")
        rot = g[:, 0, 0, :].rearrange("p (a h f) -> p a h f", a=2, h=RH)
        with ExitStack() as own:
            ff_hi = sb("ff_hi", [P, FB, 2 * S], F32R, stack=own)
            ff_lo = sb("ff_lo", [P, FB, 2 * S], F32R, stack=own)
            silu_g = sb("silu_g", [P, NT, 256], stack=own)
            ff_tok = sb("ff_tok", [P, 2, NT, 256], stack=own)
        with ExitStack() as own:
            hv = sb("hv", [P, NT, CB], stack=own)
            hgate = sb("hgate", [P, NT, CB], stack=own)
            mo = sb("mo", [P, NT, CB], stack=own)
            mqk = sb("mqk", [P, NT, CB], stack=own)
            mv = sb("mv", [P, NT, NH, P + 2], stack=own)
            hq_T = sb("hq_T", [P, NH, S], stack=own)
            hk_T = sb("hk_T", [P, NH, S], stack=own)
            cum = sb("cum", [P, NH, S], stack=own)
            dec = sb("dec", [P, NH, S], stack=own)
            half_rstd = sb("half_rstd", [P, NT], stack=own)
            qs = sb("qs", [P, 2, NH * S], stack=own)
            ks = sb("ks", [P, 2, NH * S], stack=own)
            hsc = sb("hsc", [P, NT, NH, P], stack=own)
            hoff = sb("hoff", [P, NH, P], stack=own)
            mqk_pad = sb("mqk_pad", [P, 4, S + CW2 - 1], stack=own)
            mqk_T = sb("mqk_T", [P, 4, S], stack=own)
            mw = sb("mw", [P, NH, 3 * P], stack=own)
            level = sb("level", [P, 8, P], U8, stack=own)
            causal = sb("causal", [P, P], stack=own)
            gw = sb("gw", [P, KD * 8], stack=own)
            gw_hi = sb("gw_hi", [P, KD * 8], F32R, stack=own)
            gw_lo = sb("gw_lo", [P, KD * 8], F32R, stack=own)
            gbias = sb("gbias", [P, 8], stack=own)
            gt = sb("gt", [P, NT, 8], stack=own)
            lb = sb("lb", [P, 6, NH], stack=own)
            um = sb("um", [P, 16], stack=own)
            mden = sb("mden", [P, 2, 8], stack=own)
            mstat = sb("mstat", [P, 6, 8], stack=own)
            sel = sb("sel", [NH, NH, P], stack=own)
        mod_bank = bank[2]
        keep = junk[:].rearrange("p (h s) -> p h s", h=NH)
        row = spread[0:NH, 1, :].rearrange("p (a s) -> p a s", a=4)

        def cv(name, j, n=1):
            return col[:, COLS[name] + j:COLS[name] + j + n]

        def drained(b, off=None):
            return pair_freed[b % 2], plus(b // 2 + 1, off)

        def done(b, off=None):
            return w_used, plus(group_end(b), off, UPG)

        def part_of(b, tau):
            return bank[2 * (b % 2) + tau]

        def plus(value, off, per=1):
            return value if off is None else value + off * per

        def side(key):
            return bank[SIDE[key][0]]

        def full(key, off=None):
            return side_filled[SIDE[key][0] - 4], plus(SIDE[key][1], off)

        def freed(key, off=None):
            return side_freed[SIDE[key][0] - 4], plus(SIDE[key][1], off)

        def side_free(key):
            return side_freed[SIDE[key][0] - 4]

        def pair_free(b):
            return pair_freed[b % 2]

        def sums(name):
            n = 8 * NORMS.index(name)
            return stat[:, n:n + 4], stat[:, n + 4:n + 6], stat[:, n + 6:n + 8]

        block = ctx.enter_context(nc.Block())

        @block.sync
        def _(sp):
            def load(dst, src, loaded):
                sp.dma_start(dst, src).then_inc(loaded, 16)

            load(col[:], cols, col_loaded)
            load(ident[:], ident_in, ident_loaded)
            for k in range(KD):
                load(ada_w[:, k, :], ada[k, :, 0:2 * D], ada_loaded[k])
                if k == 1:
                    load(x[:], x_in.rearrange("(t p) d -> p t d", p=P), x_loaded)
                    load(pos_i[:], pos_in, pos_loaded)
                    load(inv_freq[:], inv_freq_in, freq_loaded)
            for n in range(RAW):
                load(raw[:, n, :], stream[n], raw_loaded[n])
            sp.wait_ge(trig_step, 13)
            load(decay[:], decay_in.rearrange("p (h c) -> p h c", h=RH), decay_loaded)
            with sp.Fori(1, GROUPS // RAW) as i:
                for n in range(RAW):
                    sp.wait_ge(w_lo_ready, i * RAW + (n - RAW + 1))
                    load(raw[:, n, :], stream[i * RAW + n], raw_loaded[n])
            for n in range(2 * NT):
                c, tau = divmod(n, NT)
                sp.wait_ge(x_ready, 3 * 2 * NT + n + 1)
                load(out[tau * P:(tau + 1) * P, c * CB:(c + 1) * CB], x[:, tau, c * CB:(c + 1) * CB], out_written)
            sp.wait_ge(out_written, 16 * 2 * NT)

        @block.tensor
        def _(pe):
            def gemm(b, hi, lo, off=None, mid=None, mid_at=None, parts=None):
                k_tiles = _UNIT0[b + 1] - _UNIT0[b]
                if b >= 2:
                    pe.wait_ge(pair_free(b), plus(b // 2, off))
                for n in range(k_tiles):
                    if parts is not None and n % 2 == 0 and parts(n // 2) is not None:
                        pe.wait_ge(*parts(n // 2))
                    unit = _UNIT0[b] + n
                    group, place = divmod(unit, UPG)
                    cs = slice(place * CB, (place + 1) * CB)
                    if place == 0 or n == 0:
                        pe.wait_ge(w_lo_ready, plus(group + 1, off, UPG))
                    wh, wl = w_hi[:, group % RING, cs], w_lo[:, group % RING, cs]
                    for tau in range(NT):
                        ah, al = hi(n)[:, tau * P:(tau + 1) * P], lo(n)[:, tau * P:(tau + 1) * P]
                        acc = part_of(b, tau)[:]
                        pe.matmul(acc, ah, wh, start=n == 0, stop=False)
                        pe.matmul(acc, ah, wl, start=False, stop=False)
                        mm = pe.matmul(acc, al, wh, start=False, stop=n == k_tiles - 1)
                    if place == UPG - 1:
                        mm.then_inc(w_used, 1)
                    if mid is not None and n == (k_tiles // 2 - 1 if mid_at is None else mid_at):
                        mid()

            def act(n):
                return act_hi[:, n, :]

            def act_l(n):
                return act_lo[:, n, :]

            def ret(n):
                return ret_hi[:, n, :]

            def ret_l(n):
                return ret_lo[:, n, :]

            def ff(n):
                return ff_hi[:, n // 2, (n % 2) * S:(n % 2 + 1) * S]

            def ff_l(n):
                return ff_lo[:, n // 2, (n % 2) * S:(n % 2 + 1) * S]

            def begin(key, off=None):
                n = SIDE[key][1] - 1
                if n or off is not None:
                    pe.wait_ge(side_free(key), plus(n, off))

            def end(ins, key):
                ins.then_inc(side_filled[SIDE[key][0] - 4], 1)

            def turn(key, sources, off=None):
                begin(key, off)
                for n, src in enumerate(sources):
                    mm = pe.transpose(side(key)[:, n * P:(n + 1) * P], src, ident[:])
                end(mm, key)

            def turn_tok(key, j, src):
                turn((key, j), [src(tau, k) for k in (2 * j, 2 * j + 1) for tau in range(NT)])

            def turn_x(key, posts):
                for j in range(4):
                    pe.wait_ge(x_ready, 2 * NT * (posts - 1) + NT * (j // 2 + 1))
                    turn_tok(key, j, lambda tau, k: x[:, tau, k * P:(k + 1) * P])

            pe.wait_ge(ident_loaded, 16)
            pe.wait_ge(normed, 2)
            for j in range(4):
                turn_tok("pre0", j, lambda tau, k: tmp[:, tau, k * P:(k + 1) * P])
            pe.wait_ge(ones_ready, 1)
            for f in range(16):
                if f % 8 == 0:
                    pe.wait_ge(ada_summed, KD + f // 8)
                mm = pe.matmul(mod_bank[:, f:f + 1], h_T[:, f // 2, (f % 2) * P:(f % 2 + 1) * P], ones[:, 0:1],
                               start=True, stop=True)
            mm.then_inc(mod_summed, 1)
            for b in range(4):
                gemm(b, act, act_l, parts=lambda j: (act0_ready, j + 1) if b == 0 else None)
            pe.wait_ge(*drained(2))
            pe.wait_ge(*drained(3))
            for j in range(4):
                turn_tok("aT", j, lambda tau, k: tmp[:, tau, k * P:(k + 1) * P])
            with pe.Fori(0, 4) as i:
                for n in range(2):
                    gemm(first("qk") + n, act, act_l, off=i)
            pe.wait_ge(gate_summed, KD)
            for j in range(2):
                begin(("gate", j))
                end(pe.matmul(side(("gate", j))[:], ones, gate_sum[:, j * CB:(j + 1) * CB], start=True, stop=True),
                    ("gate", j))
            with pe.Fori(0, 2) as i:
                for n in range(2):
                    gemm(first("z") + n, act, act_l, off=i)

            def head_turn(h):
                pe.wait_ge(rotated, 2 * NT)
                for w, key in ((0, "qT"), (1, "kT")):
                    turn((key, h), [qkv[:, w, tau, h * 256 + k * P:h * 256 + (k + 1) * P]
                                    for k in range(2) for tau in range(NT)])

            def head_scores(h):
                key = ("rs", h)
                begin(key)
                pe.wait_ge(*freed(("qT", h)))
                pe.wait_ge(*freed(("kT", h)))
                for k in range(2):
                    pe.matmul(side(key)[:, 0:S], qk_T[:, 1, k, 0:P], qk_T[:, 0, k, :], start=k == 0, stop=k == 1)
                for k in range(2):
                    mm = pe.matmul(side(key)[:, S:S + P], qk_T[:, 1, k, P:S], qk_T[:, 0, k, P:S],
                                   start=k == 0, stop=k == 1)
                end(mm, key)

            def head_out(h):
                def v(tau):
                    return qkv[:, 2 + h // 2, tau, (h % 2) * CB:(h % 2 + 1) * CB]

                pe.wait_ge(*freed(("rs", h)))
                begin(("ro", h, 0))
                end(pe.matmul(side(("ro", h, 0))[:], masked[:, h % 2, 0:P], v(0), start=True, stop=True), ("ro", h, 0))
                begin(("ro", h, 1))
                pe.matmul(side(("ro", h, 1))[:], masked[:, h % 2, P:2 * P], v(0), start=True, stop=False)
                end(pe.matmul(side(("ro", h, 1))[:], masked[:, h % 2, 2 * P:3 * P], v(1), start=False, stop=True),
                    ("ro", h, 1))

            def heads_mid(m):
                if 1 <= m <= 4:
                    head_scores(m - 1)
                if m <= 3:
                    head_turn(m)

            for m in range(6):
                if m >= 2:
                    head_out(m - 2)
                gemm(first("zc") + m, act, act_l, mid=lambda: heads_mid(m))
            pe.wait_ge(ret_ready, 2 * RH)
            for j in range(8):
                turn(("retT", j), [qkv[:, j % 2, tau, (j // 2) * 256 + k * P:(j // 2) * 256 + (k + 1) * P]
                                   for k in range(2) for tau in range(NT)])
            def conv_turn():
                pe.wait_ge(conv_step, KD * (CW + 1) + 1)
                for tau in range(NT):
                    for half in range(2):
                        turn(("cvtok", 2 * tau + half), [tmp_T[:, 4 * half + k, tau * P:(tau + 1) * P] for k in range(4)])

            def conv_turn_back():
                pe.wait_ge(conv_act_ready, NT)
                for j in range(4):
                    turn_tok("cvT", j, lambda tau, k: tmp[:, tau, k * P:(k + 1) * P])

            gemm(first("ret"), ret, ret_l, mid=conv_turn, parts=lambda j: freed(("retT", j)))
            gemm(first("ret") + 1, ret, ret_l, mid=conv_turn_back)

            def merged_turn(c):
                pe.wait_ge(merged, NT * (c + 1))
                for j in range(2 * c, 2 * c + 2):
                    turn_tok("mgT", j, lambda tau, k: g[:, 0, tau, k * P:(k + 1) * P])

            gemm(first("conv"), act, act_l, parts=lambda j: freed(("cvT", j)))
            gemm(first("conv") + 1, act, act_l, mid=lambda: merged_turn(0))
            merged_turn(1)
            gemm(first("wout"), ret, ret_l, parts=lambda j: freed(("mgT", j)))
            gemm(first("wout") + 1, ret, ret_l)

            def feed_forward(which, key, stage_in, stage_out):
                b = first(stage_in)

                def hidden_turn(parity, off):
                    key = ("ffT", which, parity)
                    pe.wait_ge(*drained(b + parity, off))
                    turn(key, [ff_tok[:, parity, tau, k * P:(k + 1) * P] for k in range(2) for tau in range(NT)], off)

                def hidden(j):
                    if j == FB - 2:
                        return freed(("ffT", which, 1), FB // 2 - 1)
                    if j == FB - 1:
                        return freed(("ffT", which, 0), FB // 2)
                    return None

                gemm(b, act, act_l, parts=lambda j: freed((key, j)))
                with pe.Fori(0, (FB - 1) // 2) as i:
                    gemm(b + 1, act, act_l, off=i)
                    hidden_turn(0, i)
                    gemm(b + 2, act, act_l, off=i)
                    hidden_turn(1, i)
                gemm(first(stage_out), ff, ff_l, mid=lambda: hidden_turn(0, (FB - 1) // 2), mid_at=3, parts=hidden)
                gemm(first(stage_out) + 1, ff, ff_l)

            turn_x("pre1", 1)
            feed_forward(0, "pre1", "f1i", "f1o")
            turn_x("pre2", 2)

            mix = first("mixi")

            def hgrn_turn(key, c):
                pe.wait_ge(*drained(mix + c))
                for j in range(2):
                    turn((key, j), [tmp[:, tau, c * CB + k * P:c * CB + (k + 1) * P]
                                    for k in (2 * j, 2 * j + 1) for tau in range(NT)])

            def gates_turn():
                pe.wait_ge(*freed("gates"))
                begin("gatesT")
                for w in range(2):
                    for tau in range(NT):
                        mm = pe.matmul(side("gatesT")[0:NH, w * S + tau * P:w * S + (tau + 1) * P],
                                       gt[:, tau, 4 * w:4 * w + 4], ident[:], start=True, stop=True)
                end(mm, "gatesT")

            def um_turn():
                pe.wait_ge(row_step, 7)
                begin("umT")
                for w, r in ((0, 0), (1, 3)):
                    for tau in range(NT):
                        n = 8 * w + 4 * tau
                        mm = pe.matmul(side("umT")[:, n:n + 4], row[:, r, tau * P:(tau + 1) * P], ident[0:NH, 0:NH],
                                       start=True, stop=True)
                end(mm, "umT")

            def m_spread():
                pe.wait_ge(row_step, 6)
                pe.wait_ge(sel_loaded, 16)
                for j in range(2):
                    begin(("mb", j))
                    for n in range(2):
                        mm = pe.matmul(side(("mb", j))[:, n * S:(n + 1) * S], sel[:, 2 * j + n, :], row[:, 2, :],
                                       start=True, stop=True)
                    end(mm, ("mb", j))

            def level_scores(lv):
                if lv == 0:
                    pe.wait_ge(*freed(("hqT", 0)))
                    pe.wait_ge(*freed(("hqT", 1)))
                    pe.wait_ge(hk_T_ready, 1)
                    q_of, k_of = hq_T[:], hk_T[:]
                else:
                    pe.wait_ge(scaled_ready, 2 * lv)
                    q_of = qs[:, lv % 2, :].rearrange("p (h s) -> p h s", h=NH)
                    k_of = ks[:, lv % 2, :].rearrange("p (h s) -> p h s", h=NH)
                for blk in range(NT if lv < 8 else 1):
                    key = ("lv", lv, blk)
                    begin(key)
                    for h in range(NH):
                        s_at = slice(blk * P, (blk + 1) * P)
                        t_at = s_at if lv < 8 else slice(P, S)
                        mm = pe.matmul(side(key)[:, h * P:(h + 1) * P], k_of[:, h, s_at], q_of[:, h, t_at],
                                       start=True, stop=True)
                    end(mm, key)

            def conv2_turn():
                pe.wait_ge(*drained(mix + 3))
                for j in range(2):
                    turn(("cv2T", j), [mqk[:, tau, k * P:(k + 1) * P] for k in (2 * j, 2 * j + 1) for tau in range(NT)])

            def mlstm_scores(h):
                key = ("ms", h)
                begin(key)
                rows_at = slice((h % 2) * QK, (h % 2 + 1) * QK)
                q_of, k_of = mqk_T[rows_at, h // 2, :], mqk_T[rows_at, 2 + h // 2, :]
                pe.matmul(side(key)[:, 0:S], k_of[:, 0:P], q_of, start=True, stop=True)
                end(pe.matmul(side(key)[:, S:S + P], k_of[:, P:S], q_of[:, P:S], start=True, stop=True), key)

            def gates_product():
                pe.wait_ge(gw_ready, 2)
                begin("gates")
                for tau in range(NT):
                    for k in range(KD):
                        ts_, cs = slice(tau * P, (tau + 1) * P), slice(8 * k, 8 * k + 8)
                        o = side("gates")[:, 8 * tau:8 * tau + 8]
                        pe.matmul(o, act_hi[:, k, ts_], gw_hi[:, cs], start=k == 0, stop=False)
                        pe.matmul(o, act_hi[:, k, ts_], gw_lo[:, cs], start=False, stop=False)
                        mm = pe.matmul(o, act_lo[:, k, ts_], gw_hi[:, cs], start=False, stop=k == KD - 1)
                end(mm, "gates")

            gemm(mix, act, act_l, parts=lambda j: freed(("pre2", j)))
            gates_product()
            gemm(mix + 1, act, act_l, mid=lambda: hgrn_turn("hqT", 0))
            hgrn_turn("hfT", 1)
            gemm(mix + 2, act, act_l, mid=gates_turn)
            um_turn()
            gemm(mix + 3, act, act_l, mid=m_spread)
            level_scores(0)

            def mid45():
                level_scores(1)
                conv2_turn()

            gemm(mix + 4, act, act_l, mid=mid45)
            level_scores(2)
            gemm(mix + 5, act, act_l, mid=lambda: level_scores(3))
            level_scores(4)
            gemm(mix + 6, act, act_l, mid=lambda: level_scores(5))
            level_scores(6)
            level_scores(7)
            pe.wait_ge(mqk_T_ready, 1)
            for h in range(NH):
                mlstm_scores(h)
            level_scores(8)
            for h in range(NH):
                pe.wait_ge(*freed(("ms", h)))
            pe.wait_ge(mv_ones, 1)
            pe.wait_ge(*drained(mix + 4))
            for tau in range(NT):
                for j in range(2):
                    key = ("mn", tau, j)
                    begin(key)
                    for n in range(2):
                        h = 2 * j + n
                        o = side(key)[:, n * (P + 1):(n + 1) * (P + 1)]
                        if tau == 0:
                            mm = pe.matmul(o, mw[:, h, 0:P], mv[:, 0, h, 0:P + 1], start=True, stop=True)
                        else:
                            pe.matmul(o, mw[:, h, P:S], mv[:, 0, h, 0:P + 1], start=True, stop=False)
                            mm = pe.matmul(o, mw[:, h, S:S + P], mv[:, 1, h, 0:P + 1], start=False, stop=True)
                    end(mm, key)
            pe.wait_ge(*freed(("lv", 7, 1)))
            pe.wait_ge(*freed(("lv", 8, 0)))
            for tau in range(NT):
                key = ("ho", tau)
                begin(key)
                for h in range(NH):
                    o = side(key)[:, h * P:(h + 1) * P]
                    if tau == 1:
                        pe.matmul(o, hoff[:, h, :], hv[:, 0, h * P:(h + 1) * P], start=True, stop=False)
                    mm = pe.matmul(o, hsc[:, tau, h, :], hv[:, tau, h * P:(h + 1) * P], start=tau == 0, stop=True)
                end(mm, key)
            pe.wait_ge(mixed, 4)
            for j in range(4):
                turn_tok("mxT", j, lambda tau, k: tmp[:, tau, k * P:(k + 1) * P])
            gemm(first("mixo"), act, act_l, parts=lambda j: freed(("mxT", j)))
            gemm(first("mixo") + 1, act, act_l)
            turn_x("pre3", 3)
            feed_forward(1, "pre3", "f2i", "f2o")

        @block.scalar
        def _(act):
            def hi_parts(b, off=None):
                for n in range(split_to(b - 1) if b >= 0 else 0, split_to(b)):
                    act.wait_ge(raw_loaded[n % RAW], plus(16 * (n // RAW + 1), off, 16 * UPG // RAW))
                    if n >= RING:
                        act.wait_ge(w_used, plus(n - RING + 1, off, UPG))
                    act.activation(w_hi[:, n % RING, :], raw[:, n % RAW, :], ACT.Copy).then_inc(w_hi_ready, 1)

            def squares(name, src):
                for tau in range(NT):
                    if SUMS_BEFORE[name] + tau:
                        act.wait_ge(ss_ready, SUMS_BEFORE[name] + tau)
                    act.activation(junk[:], src(tau), ACT.Square, accum_out=sums(name)[0][:, tau:tau + 1]
                                   ).then_inc(ss_ready, 1)

            def hi_of(key, j, dst, scale=1.0):
                act.wait_ge(*full((key, j)))
                act.activation(dst, side((key, j))[:].rearrange("p (k s) -> p k s", s=S), ACT.Copy,
                               scale=scale).then_inc(act_hi_ready, 1)

            def hi_scaled(key, at):
                for j in range(4):
                    act.wait_ge(*full((key, j)))
                    for n in range(2):
                        k = 2 * j + n
                        act.activation(act_hi[:, k, :], side((key, j))[:, n * S:(n + 1) * S], ACT.Copy,
                                       scale=cv("pre2", at + k)).then_inc(act_hi_ready, 1)

            def drain(b, dst, func, off=None, scale=1.0):
                act.wait_ge(*done(b, off))
                for tau in range(NT):
                    ins = act.activation(dst(tau), part_of(b, tau)[:], func, scale=scale)
                ins.then_inc(pair_free(b), 1)

            act.wait_ge(x_loaded, 16)
            squares("pre0", lambda tau: x[:, tau, :])
            hi_parts(-1)
            for j in range(4):
                act.wait_ge(*freed(("pre0", j)))
                act.activation(act_hi[:, 2 * j:2 * j + 2, :], h_T[:, 2 * j:2 * j + 2, :], ACT.Copy
                               ).then_inc(act_hi_ready, 1)
            act.wait_ge(trig_step, 13)
            act.activation(trig, ang[:], ACT.Sin).then_inc(trig_ready, 1)
            for b in range(4):
                hi_parts(b)
                act.wait_ge(*done(b))
                if b:
                    act.wait_ge(*drained(b - 1))
                for tau in range(NT):
                    act.activation(tanh_u[:, tau, :], part_of(b, tau)[:, 256:512], ACT.Tanh,
                                   scale=0.5).then_inc(tanh_ready, 1)
            act.wait_ge(pad_ready, 1)
            for j in range(4):
                act.wait_ge(*full(("aT", j)))
                act.activation(a_T[:, 2 * j:2 * j + 2, CW - 1:], side(("aT", j))[:].rearrange("p (k s) -> p k s", s=S),
                               ACT.Copy, scale=0.5).then_inc(side_free(("aT", j)), 1)
            with act.Fori(0, 4) as i:
                for n in range(2):
                    hi_parts(first("qk") + n, i)
                    drain(first("qk") + n, lambda tau: qkv[:, i, tau, n * CB:(n + 1) * CB], ACT.Copy, i)
            with act.Fori(0, 2) as i:
                for n in range(2):
                    hi_parts(first("z") + n, i)
                    drain(first("z") + n, lambda tau: z[:, i, tau, n * CB:(n + 1) * CB], ACT.Silu, i)
            for m in range(6):
                b = first("zc") + m
                hi_parts(b)
                if m <= 3:
                    if m:
                        act.wait_ge(*full(("rs", m - 1)))
                    for w, key in ((0, "qT"), (1, "kT")):
                        act.wait_ge(*full((key, m)))
                        act.activation(qk_T[:, w, :, :], side((key, m))[:].rearrange("p (k s) -> p k s", s=S),
                                       ACT.Copy).then_inc(side_free((key, m)), 1)
                if m < 2:
                    drain(b, lambda tau: x[:, tau, m * CB:(m + 1) * CB], ACT.Silu)
                else:
                    drain(b, lambda tau: g[:, (m - 2) // 2, tau, (m % 2) * CB:(m % 2 + 1) * CB], ACT.Tanh, scale=0.5)
            for j in range(8):
                hi_of("retT", j, ret_hi[:, 2 * j:2 * j + 2, :])
            hi_parts(first("ret"))
            for tau in range(NT):
                act.wait_ge(ln_step, 3 * NT + tau + 1)
                act.activation(tmp[:, tau, :], tmp[:, tau, :], ACT.Silu).then_inc(conv_silu, 1)
            hi_parts(first("ret") + 1)
            for j in range(4):
                hi_of("cvT", j, act_hi[:, 2 * j:2 * j + 2, :])
            hi_parts(first("conv"))
            hi_parts(first("conv") + 1)
            for j in range(4):
                hi_of("mgT", j, ret_hi[:, 2 * j:2 * j + 2, :], scale=0.5)

            def post(name, stage, before):
                for c in range(2):
                    b = first(stage) + c
                    hi_parts(b)
                    act.wait_ge(*done(b))
                    for tau in range(NT):
                        n = SUMS_BEFORE[name] + 2 * c + tau
                        act.wait_ge(ss_ready, n)
                        if tau == 1:
                            act.wait_ge(post_bank_read, 2 * before + c + 1)
                        act.activation(junk[:, 0:CB], part_of(b, tau)[:], ACT.Square,
                                       accum_out=sums(name)[0][:, 2 * c + tau:2 * c + tau + 1]).then_inc(ss_ready, 1)

            def pre(name, at):
                hi_scaled(name, at)
                act.wait_ge(x_ready, 2 * NT * (1 + at // 8))
                squares(name, lambda tau: x[:, tau, :])

            def rstd_of(name, tau):
                return sums(name)[2][:, tau:tau + 1]

            def feed_forward(which, name, stage):
                b0 = first(stage)

                def silu(b, off=None):
                    act.wait_ge(*done(b, off))
                    if b > b0:
                        act.wait_ge(*drained(b - 1, off))
                    for tau in range(NT):
                        act.activation(silu_g[:, tau, :], part_of(b, tau)[:, 0:256], ACT.Silu,
                                       scale=rstd_of(name, tau)).then_inc(silu_ready, 1)

                def hidden_hi(parity, j, off=None):
                    key = ("ffT", which, parity)
                    act.wait_ge(*full(key, off))
                    act.activation(ff_hi[:, j, :], side(key)[:], ACT.Copy).then_inc(act_hi_ready, 1)

                hi_parts(b0)
                act.wait_ge(pre_rstd_ready, 2 + 2 * which)
                silu(b0)
                with act.Fori(0, (FB - 1) // 2) as i:
                    for n in range(2):
                        hi_parts(b0 + 1 + n, i)
                        silu(b0 + 1 + n, i)
                        hidden_hi(n, 2 * i + n, i)
                hidden_hi(0, FB - 1, FB // 2)

            post("post_w", "wout", 0)
            pre("pre1", 0)
            feed_forward(0, "pre1", "f1i")
            post("post_f1", "f1o", 1)
            act.wait_ge(gw_loaded, 16)
            act.activation(gw_hi[:], gw[:], ACT.Copy).then_inc(gw_hi_ready, 1)
            act.wait_ge(lb_step, 3)
            act.activation(lb[:, 1:3, :], lb[:, 1:3, :], ACT.Exp).then_inc(lb_exp, 1)
            pre("pre2", 8)
            mix = first("mixi")

            def drain_scaled(b, dst, func):
                act.wait_ge(*done(b))
                for tau in range(NT):
                    ins = act.activation(dst(tau), part_of(b, tau)[:], func, scale=rstd_of("pre2", tau))
                ins.then_inc(pair_free(b), 1)

            hi_parts(mix)
            act.wait_ge(pre_rstd_ready, 3)
            drain_scaled(mix, lambda tau: tmp[:, tau, 0:CB], ACT.Silu)
            hi_parts(mix + 1)
            for j in range(2):
                act.wait_ge(*full(("hqT", j)))
                act.activation(hq_T[:, 2 * j:2 * j + 2, :], side(("hqT", j))[:].rearrange("p (h s) -> p h s", s=S),
                               ACT.Copy).then_inc(side_free(("hqT", j)), 1)
            drain_scaled(mix + 1, lambda tau: tmp[:, tau, CB:D], ACT.Sigmoid)
            hi_parts(mix + 2)
            for j in range(2):
                act.wait_ge(*freed(("hfT", j)))
            act.activation(dec[:], hk_T[:], ACT.Ln).then_inc(log_f_ready, 1)
            act.wait_ge(*full("gatesT"))
            f_row = side("gatesT")[0:NH, S:2 * S]
            act.activation(row[:, 2, :], f_row, ACT.Abs).then_inc(row_step, 1)
            act.wait_ge(row_step, 1)
            act.activation(row[:, 2, :], row[:, 2, :], ACT.Exp, scale=-1.0).then_inc(row_step, 1)
            act.wait_ge(row_step, 2)
            act.activation(row[:, 2, :], row[:, 2, :], ACT.Ln, bias=1.0).then_inc(row_step, 1)
            drain_scaled(mix + 2, lambda tau: hv[:, tau, :], ACT.Copy)
            hi_parts(mix + 3)
            act.wait_ge(*full("umT"))
            act.activation(um[:, 8:16], side("umT")[:, 8:16], ACT.Exp, scale=-1.0)
            act.activation(um[:, 0:8], side("umT")[:, 0:8], ACT.Copy).then_inc(side_free("umT"), 1)
            for j in range(2):
                act.wait_ge(*freed(("mb", j)))
            act.activation(mw[:], mw[:], ACT.Exp, scale=-1.0).then_inc(mw_exp, 1)
            drain_scaled(mix + 3, lambda tau: mqk[:, tau, :], ACT.Copy)

            def level_exp(lv):
                act.wait_ge(diff_ready, lv)
                act.activation(dec[:], dec[:], ACT.Exp).then_inc(exp_ready, 1)

            level_exp(1)
            hi_parts(mix + 4)
            level_exp(2)
            act.wait_ge(mqk_pad_ready, 1)
            for j in range(2):
                act.wait_ge(*full(("cv2T", j)))
                act.activation(mqk_pad[:, 2 * j:2 * j + 2, CW2 - 1:],
                               side(("cv2T", j))[:].rearrange("p (h s) -> p h s", s=S), ACT.Copy
                               ).then_inc(side_free(("cv2T", j)), 1)
            act.wait_ge(*done(mix + 4))
            for tau in range(NT):
                ins = act.activation(mv[:, tau, :, 0:P], part_of(mix + 4, tau)[:].rearrange("p (h d) -> p h d", h=NH),
                                     ACT.Copy, scale=rstd_of("pre2", tau))
            ins.then_inc(pair_free(mix + 4), 1)
            level_exp(3)
            hi_parts(mix + 5)
            level_exp(4)
            drain_scaled(mix + 5, lambda tau: hgate[:, tau, :], ACT.Silu)
            level_exp(5)
            hi_parts(mix + 6)
            act.wait_ge(conv2_step, 4 * CW2)
            act.activation(mqk_T[:], mqk_T[:], ACT.Silu).then_inc(mqk_T_ready, 1)
            level_exp(6)
            act.wait_ge(*done(mix + 6))
            act.wait_ge(half_rstd_ready, 1)
            for tau in range(NT):
                ins = act.activation(mo[:, tau, :], part_of(mix + 6, tau)[:], ACT.Tanh, scale=half_rstd[:, tau:tau + 1])
            ins.then_inc(pair_free(mix + 6), 1)
            level_exp(7)
            level_exp(8)
            for tau in range(NT):
                for j in range(2):
                    act.wait_ge(*freed(("mn", tau, j)))
            act.activation(ks[:, 1, :], qs[:, 1, :], ACT.Square).then_inc(mix_sq, 1)
            for tau in range(NT):
                key = ("ho", tau)
                act.wait_ge(*full(key))
                act.activation(ks[:, 0, tau * CB:(tau + 1) * CB], side(key)[:], ACT.Square).then_inc(mix_sq, 1)
                act.activation(qs[:, 0, tau * CB:(tau + 1) * CB], side(key)[:], ACT.Copy).then_inc(side_free(key), 1)
            for j in range(4):
                hi_of("mxT", j, act_hi[:, 2 * j:2 * j + 2, :])
            post("post_m", "mixo", 2)
            pre("pre3", 16)
            feed_forward(1, "pre3", "f2i")
            post("post_f2", "f2o", 3)

        @block.gpsimd
        def _(pool):
            def spread_row(dst, name):
                r = ROWS.index(name)
                pool.dma_start(dst, rows[r, :].partition_broadcast(P)).then_inc(row_loaded[name], 16)

            def power(dst, src, ready, count):
                pool.wait_ge(ready, count)
                n = dst.shape[-1]
                return pool.tensor_tensor(dst, src, half_power[:, 0:n], ALU.pow)

            def norm(name):
                ss, var, rstd = sums(name)
                n = PRES.index(name) + 1
                pool.wait_ge(ss_ready, SUMS_BEFORE[name] + 2)
                pool.tensor_scalar(var, ss[:, 0:2], 1.0 / D, 1e-6, ALU.mult, ALU.add).then_inc(pre_var_ready, 1)
                power(rstd, var, pre_var_ready, n).then_inc(pre_rstd_ready, 1)

            spread_row(gate_bc[:], "b_gate")
            pool.memset(half_power[:], -0.5).then_inc(half_ready, 1)
            pool.wait_ge(half_ready, 1)
            norm("pre0")
            pool.memset(ones, 1.0).then_inc(ones_ready, 1)
            pool.wait_ge(pos_loaded, 16)
            pool.wait_ge(freq_loaded, 16)
            pool.tensor_copy(pos_f[:], pos_i[:]).then_inc(trig_step, 1)
            pool.wait_ge(trig_step, 1)
            for tau in range(NT):
                for w in range(2):
                    ins = pool.tensor_scalar(ang[:, tau, w, :], inv_freq[:], pos_f[:, tau:tau + 1], None, ALU.mult)
            ins.then_inc(trig_step, 1)
            pool.wait_ge(trig_step, 2)
            pool.tensor_scalar(turns[:, :, 0, :], ang[:, :, 0, :], 1 / TWO_PI, 0.25, ALU.mult, ALU.add)
            pool.tensor_scalar(turns[:, :, 1, :], ang[:, :, 1, :], 1 / TWO_PI, None, ALU.mult).then_inc(trig_step, 1)
            for n, value in enumerate((ROUND, -ROUND)):
                pool.wait_ge(trig_step, 3 + n)
                pool.tensor_scalar(turns[:], turns[:], value, None, ALU.add).then_inc(trig_step, 1)
            for n, value in enumerate((TWO_PI_1, TWO_PI_2, TWO_PI_3)):
                pool.wait_ge(trig_step, 5 + 2 * n)
                pool.tensor_scalar(part, turns[:], value, None, ALU.mult).then_inc(trig_step, 1)
                pool.wait_ge(trig_step, 6 + 2 * n)
                pool.tensor_tensor(ang[:], ang[:], part, ALU.subtract).then_inc(trig_step, 1)
            pool.wait_ge(trig_step, 11)
            pool.tensor_scalar(ang[:, :, 0, :], ang[:, :, 0, :], TWO_PI / 4, None, ALU.add).then_inc(trig_step, 1)
            pool.wait_ge(trig_step, 12)
            pool.tensor_scalar(ang[:], ang[:], PI_INSIDE, -PI_INSIDE, ALU.min, ALU.max).then_inc(trig_step, 1)
            pool.wait_ge(trig_ready, 1)
            pool.wait_ge(act0_ready, 4)
            pool.memset(a_T[:, :, 0:CW - 1], 0.0).then_inc(pad_ready, 1)
            def post_norm(name, before):
                _, var, rstd = sums(name)
                power(rstd, var, post_var_ready, 2 * before + 2).then_inc(post_rstd_ready, 1)

            def gate_w(k):
                return (z, g)[k // 4][:, k % 4 // 2, k % 2, :]

            for k in range(KD + 1):
                if k < KD:
                    pool.wait_ge(w_used, 2 * k + 1)
                    pool.dma_start(gate_w(k), ada[k, :, 2 * D:3 * D]).then_inc(gate_w_loaded[k], 16)
                if k == 1:
                    pool.wait_ge(gate_w_loaded[0], 16)
                    pool.tensor_scalar(gate_sum, gate_w(0), cv("c", 0), None, ALU.mult).then_inc(gate_summed, 1)
                elif k:
                    pool.wait_ge(gate_w_loaded[k - 1], 16)
                    pool.tensor_scalar(gate_w(k - 1), gate_w(k - 1), cv("c", k - 1), None, ALU.mult
                                       ).then_inc(gate_scaled, 1)
                    pool.wait_ge(gate_scaled, k - 1)
                    pool.wait_ge(gate_summed, k - 1)
                    pool.tensor_tensor(gate_sum, gate_sum, gate_w(k - 1), ALU.add).then_inc(gate_summed, 1)
            for b in range(first("qk"), first("qk") + 4):
                pool.wait_ge(*drained(b))
            n = 0
            for w in range(2):
                for tau in range(NT):
                    t = qkv[:, w, tau, :].rearrange("p (h u f) -> p u h f", h=RH, u=2)
                    cos = trig[:, tau, 0, :].unsqueeze(1).to_broadcast([P, RH, P])
                    sin = trig[:, tau, 1, :].unsqueeze(1).to_broadcast([P, RH, P])
                    if n:
                        pool.wait_ge(rotated, n)
                    pool.tensor_tensor(rot[:, 0], t[:, 0], sin, ALU.mult)
                    pool.tensor_tensor(rot[:, 1], t[:, 1], sin, ALU.mult).then_inc(rot_step, 1)
                    pool.wait_ge(rot_step, 2 * n + 1)
                    pool.tensor_tensor(t[:, 0], t[:, 0], cos, ALU.mult)
                    pool.tensor_tensor(t[:, 1], t[:, 1], cos, ALU.mult).then_inc(rot_step, 1)
                    pool.wait_ge(rot_step, 2 * n + 2)
                    pool.tensor_tensor(t[:, 0], t[:, 0], rot[:, 1], ALU.subtract)
                    pool.tensor_tensor(t[:, 1], t[:, 1], rot[:, 0], ALU.add).then_inc(rotated, 1)
                    n += 1
            for h in range(RH):
                for tau in range(NT):
                    n = NT * h + tau
                    pool.wait_ge(head_var, n + 1)
                    pool.tensor_scalar(head_stat[:, n, 8:9], head_stat[:, n, 7:8], 1e-5, None, ALU.add
                                       ).then_inc(head_eps, 1)
                    power(head_stat[:, n, 9:10], head_stat[:, n, 8:9], head_eps, n + 1
                          ).then_inc(head_rstd, 1)
                for tau in range(NT):
                    pool.wait_ge(*freed(("ro", h, tau)))
                    y = qkv[:, 0:2, tau, h * 256:(h + 1) * 256]
                    zh = z[:, h // 2, tau, (h % 2) * CB:(h % 2 + 1) * CB].rearrange("p (a c) -> p a c", a=2)
                    pool.tensor_tensor(y, y, zh, ALU.mult).then_inc(ret_ready, 1)
            pool.wait_ge(*freed(("rs", RH - 1)))
            spread_row(spread[:, 0, :], "ln_g")
            spread_row(spread[:, 1, :], "ln_b")
            for tau in range(NT):
                pool.wait_ge(ln_var, tau + 1)
                pool.tensor_scalar(ln_stat[:, tau, 14:15], ln_stat[:, tau, 13:14], 1e-5, None, ALU.add
                                   ).then_inc(ln_eps, 1)
                power(ln_stat[:, tau, 15:16], ln_stat[:, tau, 14:15], ln_eps, tau + 1).then_inc(ln_rstd, 1)
            pool.wait_ge(ln_step, 4 * NT)
            spread_row(spread[:, 0, :], "post_g")
            spread_row(spread[:, 1, :], "post0")
            pool.wait_ge(conv_act_ready, NT)
            pool.dma_start(x[:], x_in.rearrange("(t p) d -> p t d", p=P)).then_inc(x_again, 16)
            pool.wait_ge(row_loaded["post_g"], 16)
            pool.wait_ge(*freed(("gate", 1)))
            pool.tensor_tensor(gate_bc[:], gate_bc[:], spread[:, 0, :], ALU.mult).then_inc(factor_ready, 1)
            pool.wait_ge(row_loaded["post0"], 16)
            pool.tensor_scalar(spread[:, 1, :], spread[:, 1, :], 0.5, None, ALU.mult).then_inc(factor_ready, 1)
            pool.wait_ge(factor_ready, 1)
            spread_row(spread[:, 0, :], "mix_norm")
            post_norm("post_w", 0)
            norm("pre1")
            post_norm("post_f1", 1)
            pool.wait_ge(ss_ready, SUMS_BEFORE["post_f1"] + 4)
            for dst, src, loaded in ((gw[:], gates_w, gw_loaded), (gbias[:], gate_bias.partition_broadcast(P), gbias_loaded),
                                   (qs[:, 0, :], level_in, level_loaded),
                                   (causal[:], causal_in, causal_loaded), (sel[:], sel_in, sel_loaded)):
                pool.dma_start(dst, src).then_inc(loaded, 16)
            pool.memset(hsc[:], 0.0).then_inc(hsc_clear, 1)
            pool.memset(mqk_pad[:, :, 0:CW2 - 1], 0.0).then_inc(mqk_pad_ready, 1)
            pool.memset(mv[:, :, :, P:P + 1], 1.0).then_inc(mv_ones, 1)
            norm("pre2")
            pool.wait_ge(pre_rstd_ready, 3)
            pool.tensor_scalar(half_rstd[:], sums("pre2")[2], 0.5, None, ALU.mult).then_inc(half_rstd_ready, 1)
            pool.wait_ge(level_loaded, 16)
            pool.tensor_copy(level[:], qs[:, 0, :].rearrange("p (l t) -> p l t", l=8)).then_inc(level_ready, 1)
            pool.memset(keep, 1.0).then_inc(keep_step, 1)
            pool.wait_ge(keep_step, 1)
            pool.memset(keep[:, :, 0:S:CHUNK], 0.0).then_inc(keep_step, 1)
            pool.wait_ge(log_f_ready, 1)
            pool.tensor_scalar(hk_T[:], hk_T[:], -1.0, 1.0, ALU.mult, ALU.add).then_inc(hk_T_ready, 1)
            pool.wait_ge(mw_exp, 1)
            pool.wait_ge(causal_loaded, 16)
            mask = causal[:].unsqueeze(1).to_broadcast([P, NH, P])
            pool.tensor_tensor(mw[:, :, 0:P], mw[:, :, 0:P], mask, ALU.mult)
            pool.tensor_tensor(mw[:, :, S:S + P], mw[:, :, S:S + P], mask, ALU.mult).then_inc(mw_masked, 1)
            mix = first("mixi")
            pool.wait_ge(row_loaded["mix_norm"], 16)
            pool.wait_ge(*drained(mix + 5))
            hg_n = spread[:, 0, 0:CB].unsqueeze(1).to_broadcast([P, NT, CB])
            ml_n = spread[:, 0, CB:D].unsqueeze(1).to_broadcast([P, NT, CB])
            pool.tensor_tensor(hgate[:], hgate[:], hg_n, ALU.mult).then_inc(gates_scaled, 1)
            pool.wait_ge(*drained(mix + 6))
            pool.tensor_scalar(mo[:], mo[:], 0.5, 0.5, ALU.mult, ALU.add).then_inc(mo_step, 1)
            pool.wait_ge(mo_step, 1)
            pool.tensor_tensor(mo[:], mo[:], ml_n, ALU.mult).then_inc(gates_scaled, 1)
            for n in range(2):
                pool.wait_ge(mix_ss, n + 1)
                pool.tensor_scalar(mstat[:, 2 * n + 1, :], mstat[:, 2 * n, :], 1.0 / P, 1e-6, ALU.mult, ALU.add
                                   ).then_inc(mix_var, 1)
                power(mstat[:, 4 + n, :], mstat[:, 2 * n + 1, :], mix_var, n + 1).then_inc(mix_rstd, 1)
            pool.wait_ge(gates_scaled, 2)
            spread_row(spread[:, 1, :], "post1")
            spread_row(spread[:, 0, :], "post2")
            pool.wait_ge(row_loaded["post2"], 16)
            pool.tensor_scalar(spread[:, 0, :], spread[:, 0, :], 0.5, None, ALU.mult).then_inc(factor_ready, 1)
            post_norm("post_m", 2)
            norm("pre3")
            post_norm("post_f2", 3)

        @block.vector
        def _(dve):
            def lo_part(n, off=None):
                dve.wait_ge(w_hi_ready, plus(n + 1, off, UPG))
                dve.tensor_tensor(w_lo[:, n % RING, :], raw[:, n % RAW, :], w_hi[:, n % RING, :].bitcast(F32),
                                  ALU.subtract).then_inc(w_lo_ready, 1)

            def lo_parts(b, off=None):
                for n in range(split_to(b - 1), split_to(b)):
                    lo_part(n, off)

            def lo_of(key, j, dst, hi, count, scale=1.0):
                dve.wait_ge(act_hi_ready, count)
                src = side((key, j))[:].rearrange("p (k s) -> p k s", s=S)
                if scale == 1.0:
                    ins = dve.tensor_tensor(dst, src, hi.bitcast(F32), ALU.subtract)
                else:
                    ins = dve.scalar_tensor_tensor(dst, src, scale, hi.bitcast(F32), ALU.mult, ALU.subtract)
                ins.then_inc(side_free((key, j)), 1)

            def lo_scaled(key, at):
                for j in range(4):
                    for n in range(2):
                        k = 2 * j + n
                        dve.wait_ge(act_hi_ready, HI_BEFORE[key] + 2 * (j + 1))
                        ins = dve.scalar_tensor_tensor(act_lo[:, k, :], side((key, j))[:, n * S:(n + 1) * S],
                                                       cv("pre2", at + k), act_hi[:, k, :].bitcast(F32),
                                                       ALU.mult, ALU.subtract)
                    ins.then_inc(side_free((key, j)), 1)

            def act0_lo(j):
                dve.wait_ge(act_hi_ready, j + 1)
                dve.wait_ge(*freed(("pre0", j)))
                dve.tensor_tensor(act_lo[:, 2 * j:2 * j + 2, :], h_T[:, 2 * j:2 * j + 2, :],
                                  act_hi[:, 2 * j:2 * j + 2, :].bitcast(F32), ALU.subtract
                                  ).then_inc(act0_ready, 1)

            ada_sum = h_T[:].rearrange("p k s -> p (k s)")
            dve.wait_ge(col_loaded, 16)
            for k in range(KD - 1):
                dve.wait_ge(ada_loaded[k], 16)
                if k == 0:
                    ins = dve.tensor_scalar(ada_sum, ada_w[:, 0, :], cv("c", 0), None, ALU.mult)
                else:
                    dve.wait_ge(ada_summed, k)
                    ins = dve.scalar_tensor_tensor(ada_sum, ada_w[:, k, :], cv("c", k), ada_sum, ALU.mult, ALU.add)
                ins.then_inc(ada_summed, 1)
                if k == 4:
                    dve.wait_ge(pre_rstd_ready, 1)
                    for tau in range(NT):
                        dve.tensor_scalar(tmp[:, tau, :], x[:, tau, :], sums("pre0")[2][:, tau:tau + 1], None, ALU.mult
                                          ).then_inc(normed, 1)
            dve.wait_ge(ada_loaded[KD - 1], 16)
            dve.wait_ge(ada_summed, KD - 1)
            for half in range(2):
                cs = slice(half * D, (half + 1) * D)
                dve.scalar_tensor_tensor(ada_sum[:, cs], ada_w[:, KD - 1, cs], cv("c", KD - 1), ada_sum[:, cs],
                                         ALU.mult, ALU.add).then_inc(ada_summed, 1)
            lo_part(0)
            dve.wait_ge(mod_summed, 1)
            dve.tensor_tensor(mod_T[:], mod_bank[:, 0:16], cv("b_shift", 0, 16), ALU.add).then_inc(mod_ready, 1)
            dve.wait_ge(mod_ready, 1)
            dve.scalar_tensor_tensor(mod_T[:, 8:16], mod_T[:, 8:16], 1.0, cv("pre_g", 0, 8), ALU.add, ALU.mult
                                     ).then_inc(mod_ready, 1)
            dve.wait_ge(mod_ready, 2)
            for j in range(4):
                dve.wait_ge(*full(("pre0", j)))
                for k in (2 * j, 2 * j + 1):
                    ins = dve.tensor_scalar(h_T[:, k, :], side(("pre0", j))[:, (k % 2) * S:(k % 2 + 1) * S],
                                            mod_T[:, 8 + k:9 + k], mod_T[:, k:k + 1], ALU.mult, ALU.add)
                ins.then_inc(side_free(("pre0", j)), 1)
                if j:
                    act0_lo(j - 1)
                if j == 1:
                    lo_part(1)
            act0_lo(3)
            for b in range(4):
                lo_parts(b)
                for tau in range(NT):
                    dve.wait_ge(tanh_ready, 2 * b + tau + 1)
                    ins = dve.scalar_tensor_tensor(tmp[:, tau, b * 256:(b + 1) * 256], tanh_u[:, tau, :], 1.0,
                                                   part_of(b, tau)[:, 0:256], ALU.add, ALU.mult)
                ins.then_inc(pair_free(b), 1)

            def conv_taps(tile, taps, before):
                acc = (tmp_T[:, tile, :], odd_taps)
                for t in taps:
                    src = a_T[:, tile, t:t + S]
                    w = conv_w[:, bass.ds(tile, 1), t:t + 1]
                    if t >= 2:
                        dve.wait_ge(conv_step, before + (t - 1))
                    else:
                        dve.wait_ge(conv_step, before)
                    if t == 0:
                        ins = dve.tensor_scalar(acc[0], src, w, conv_b[:, bass.ds(tile, 1)], ALU.mult, ALU.add)
                    elif t == 1:
                        ins = dve.tensor_scalar(acc[1], src, w, None, ALU.mult)
                    else:
                        ins = dve.scalar_tensor_tensor(acc[t % 2], src, w, acc[t % 2], ALU.mult, ALU.add)
                    ins.then_inc(conv_step, 1)
                if taps[-1] == CW - 1:
                    dve.wait_ge(conv_step, before + CW)
                    dve.tensor_tensor(acc[0], acc[0], acc[1], ALU.add).then_inc(conv_step, 1)

            conv_w = cv("conv_w", 0, KD * CW).rearrange("p (k t) -> p k t", t=CW)
            conv_b = cv("conv_b", 0, KD)
            dve.memset(odd_taps, 0.0).then_inc(conv_step, 1)
            first_taps, last_taps = list(range(16)), list(range(16, CW))
            for j in range(4):
                dve.wait_ge(*freed(("aT", j)))
            with dve.Fori(0, 4) as i:
                for n, taps in enumerate((first_taps, last_taps)):
                    lo_parts(first("qk") + n, i)
                    conv_taps(i, taps, i * (CW + 1) + 1)
            dve.wait_ge(row_loaded["b_gate"], 16)
            for j in range(2):
                dve.wait_ge(*full(("gate", j)))
                cs = slice(j * CB, (j + 1) * CB)
                dve.tensor_tensor(gate_bc[:, cs], gate_bc[:, cs], side(("gate", j))[:], ALU.add
                                  ).then_inc(side_free(("gate", j)), 1)
            with dve.Fori(0, 2) as i:
                for n, taps in enumerate((first_taps, last_taps)):
                    lo_parts(first("z") + n, i)
                    conv_taps(i + 4, taps, (i + 4) * (CW + 1) + 1)

            def head_mask(h):
                dve.wait_ge(*full(("rs", h)))
                dve.tensor_tensor(masked[:, h % 2, :], side(("rs", h))[:, 0:3 * P], decay[:, h, :], ALU.mult
                                  ).then_inc(side_free(("rs", h)), 1)

            def head_norm(h):
                for tau in range(NT):
                    n = NT * h + tau
                    dve.wait_ge(*full(("ro", h, tau)))
                    dve.bn_stats(head_stat[:, n, 0:6], side(("ro", h, tau))[:]).then_inc(head_bn, 1)
                for tau in range(NT):
                    n = NT * h + tau
                    dve.wait_ge(head_bn, n + 1)
                    dve.bn_aggr(head_stat[:, n, 6:8], head_stat[:, n, 0:6]).then_inc(head_var, 1)
                for tau in range(NT):
                    n = NT * h + tau
                    dve.wait_ge(head_rstd, n + 1)
                    dve.tensor_scalar(qkv[:, 0:2, tau, h * 256:(h + 1) * 256],
                                      side(("ro", h, tau))[:].rearrange("p (a c) -> p a c", a=2),
                                      head_stat[:, n, 6:7], head_stat[:, n, 9:10], ALU.subtract, ALU.mult
                                      ).then_inc(side_free(("ro", h, tau)), 1)

            dve.wait_ge(decay_loaded, 16)
            for m in range(6):
                lo_parts(first("zc") + m)
                if m >= 2:
                    head_norm(m - 2)
                if 1 <= m <= 4:
                    head_mask(m - 1)
                if m < 4:
                    conv_taps(6 + m // 2, last_taps if m % 2 else first_taps, (6 + m // 2) * (CW + 1) + 1)
            for j in range(8):
                lo_of("retT", j, ret_lo[:, 2 * j:2 * j + 2, :], ret_hi[:, 2 * j:2 * j + 2, :], HI_BEFORE["retT"] + j + 1)
            lo_parts(first("ret"))
            for tau in range(NT):
                for half in range(2):
                    key = ("cvtok", 2 * tau + half)
                    dve.wait_ge(*full(key))
                    dve.bn_stats(ln_stat[:, tau, 6 * half:6 * half + 6], side(key)[:]).then_inc(ln_bn, 1)
            for tau in range(NT):
                dve.wait_ge(ln_bn, 2 * tau + 2)
                dve.bn_aggr(ln_stat[:, tau, 12:14], ln_stat[:, tau, 0:12]).then_inc(ln_var, 1)
            for tau in range(NT):
                dve.wait_ge(ln_rstd, tau + 1)
                for half in range(2):
                    key = ("cvtok", 2 * tau + half)
                    dve.tensor_scalar(tmp[:, tau, half * CB:(half + 1) * CB], side(key)[:], ln_stat[:, tau, 12:13],
                                      ln_stat[:, tau, 15:16], ALU.subtract, ALU.mult).then_inc(side_free(key), 1)
            dve.wait_ge(row_loaded["ln_g"], 16)
            dve.wait_ge(row_loaded["ln_b"], 16)
            for tau in range(NT):
                dve.wait_ge(*freed(("cvtok", 2 * tau + 1)))
                dve.tensor_tensor(tmp[:, tau, :], tmp[:, tau, :], spread[:, 0, :], ALU.mult).then_inc(ln_step, 3)
            for tau in range(NT):
                dve.wait_ge(ln_step, 3 * (tau + 1))
                dve.tensor_tensor(tmp[:, tau, :], tmp[:, tau, :], spread[:, 1, :], ALU.add).then_inc(ln_step, 1)

            def branch(b, which, c):
                dve.wait_ge(*done(b))
                for tau in range(NT):
                    dst = g[:, which, tau, c * CB:(c + 1) * CB]
                    ins = dve.scalar_tensor_tensor(dst, dst, 1.0, part_of(b, tau)[:], ALU.add, ALU.mult)
                ins.then_inc(pair_free(b), 1)

            def merge(c):
                dve.wait_ge(*drained(first("conv") + c))
                for tau in range(NT):
                    cs = slice(c * CB, (c + 1) * CB)
                    dve.tensor_tensor(g[:, 0, tau, cs], g[:, 0, tau, cs], g[:, 1, tau, cs], ALU.add
                                      ).then_inc(merged, 1)

            for tau in range(NT):
                dve.wait_ge(conv_silu, tau + 1)
                dve.tensor_tensor(tmp[:, tau, :], tmp[:, tau, :], x[:, tau, :], ALU.mult).then_inc(conv_act_ready, 1)
            branch(first("ret"), 0, 0)
            lo_parts(first("ret") + 1)
            for j in range(4):
                lo_of("cvT", j, act_lo[:, 2 * j:2 * j + 2, :], act_hi[:, 2 * j:2 * j + 2, :], HI_BEFORE["cvT"] + j + 1)
            branch(first("ret") + 1, 0, 1)
            lo_parts(first("conv"))
            branch(first("conv"), 1, 0)
            merge(0)
            lo_parts(first("conv") + 1)
            for j in range(4):
                if j == 2:
                    branch(first("conv") + 1, 1, 1)
                    merge(1)
                lo_of("mgT", j, ret_lo[:, 2 * j:2 * j + 2, :], ret_hi[:, 2 * j:2 * j + 2, :],
                      HI_BEFORE["mgT"] + j + 1, scale=0.5)

            def post(name, stage, factor, before):
                ss, var, rstd = sums(name)
                for c in range(2):
                    b = first(stage) + c
                    cs = slice(c * CB, (c + 1) * CB)
                    lo_parts(b)
                    dve.wait_ge(*done(b))
                    dve.tensor_tensor(tmp[:, 1, cs], part_of(b, 1)[:], factor[:, cs], ALU.mult).then_inc(post_bank_read, 1)
                    dve.wait_ge(ss_ready, SUMS_BEFORE[name] + 2 * c + 1)
                    dve.tensor_tensor(tmp[:, 0, cs], part_of(b, 0)[:], factor[:, cs], ALU.mult).then_inc(pair_free(b), 1)
                    dve.wait_ge(ss_ready, SUMS_BEFORE[name] + 2 * (c + 1))
                    if c == 0:
                        dve.tensor_scalar(var, ss[:, 0:2], 1.0 / D, 1e-6, ALU.mult, ALU.add).then_inc(post_var_ready, 1)
                dve.wait_ge(post_var_ready, 2 * before + 1)
                dve.scalar_tensor_tensor(var, ss[:, 2:4], 1.0 / D, var, ALU.mult, ALU.add).then_inc(post_var_ready, 1)
                dve.wait_ge(post_rstd_ready, before + 1)
                for c in range(2):
                    cs = slice(c * CB, (c + 1) * CB)
                    dve.wait_ge(*drained(first(stage) + c))
                    for tau in range(NT):
                        dve.scalar_tensor_tensor(x[:, tau, cs], tmp[:, tau, cs], rstd[:, tau:tau + 1], x[:, tau, cs],
                                                 ALU.mult, ALU.add).then_inc(x_ready, 1)

            def feed_forward(which, name, stage):
                b0 = first(stage)
                hi_before = HI_BEFORE[("ffT", which)]
                silu_before = which * 2 * FB

                def gate(b, parity, off=None):
                    for tau in range(NT):
                        dve.wait_ge(silu_ready, plus(silu_before + 2 * (b - b0) + tau + 1, off, 4))
                        ins = dve.scalar_tensor_tensor(ff_tok[:, parity, tau, :], part_of(b, tau)[:, 256:512],
                                                       sums(name)[2][:, tau:tau + 1], silu_g[:, tau, :],
                                                       ALU.mult, ALU.mult)
                    ins.then_inc(pair_free(b), 1)

                def hidden_lo(parity, j, count, off=None):
                    key = ("ffT", which, parity)
                    dve.wait_ge(act_hi_ready, count)
                    dve.tensor_tensor(ff_lo[:, j, :], side(key)[:], ff_hi[:, j, :].bitcast(F32), ALU.subtract
                                      ).then_inc(side_free(key), 1)

                lo_parts(b0)
                dve.wait_ge(pre_rstd_ready, 2 + 2 * which)
                gate(b0, 0)
                with dve.Fori(0, (FB - 1) // 2) as i:
                    for n in range(2):
                        lo_parts(b0 + 1 + n, i)
                        gate(b0 + 1 + n, 1 - n, i)
                        hidden_lo(n, 2 * i + n, plus(hi_before + n + 1, i, 2), i)
                hidden_lo(0, FB - 1, hi_before + FB)

            dve.wait_ge(x_again, 16)
            dve.wait_ge(factor_ready, 1)
            post("post_w", "wout", gate_bc[:], 0)
            lo_scaled("pre1", 0)
            feed_forward(0, "pre1", "f1i")
            dve.wait_ge(factor_ready, 2)
            post("post_f1", "f1o", spread[:, 1, :], 1)
            l0, l1 = cv("lb", 0, NH), cv("lb", NH, NH)
            dve.tensor_tensor(lb[:, 0, :], l0, l1, ALU.max).then_inc(lb_step, 1)
            dve.wait_ge(lb_step, 1)
            dve.tensor_tensor(lb[:, 1, :], l0, lb[:, 0, :], ALU.subtract).then_inc(lb_step, 1)
            dve.tensor_tensor(lb[:, 2, :], l1, lb[:, 0, :], ALU.subtract).then_inc(lb_step, 1)
            dve.wait_ge(gw_hi_ready, 1)
            dve.tensor_tensor(gw_lo[:], gw[:], gw_hi[:].bitcast(F32), ALU.subtract).then_inc(gw_ready, 2)
            dve.wait_ge(lb_exp, 1)
            dve.tensor_tensor(lb[:, 3, :], lb[:, 1, :], lb[:, 2, :], ALU.add).then_inc(lb_step, 1)
            dve.wait_ge(lb_step, 4)
            dve.reciprocal(lb[:, 3, :], lb[:, 3, :]).then_inc(lb_step, 1)
            dve.wait_ge(lb_step, 5)
            dve.tensor_tensor(lb[:, 4, :], lb[:, 1, :], lb[:, 3, :], ALU.mult).then_inc(lb_step, 1)
            dve.tensor_tensor(lb[:, 5, :], lb[:, 2, :], lb[:, 3, :], ALU.mult).then_inc(lb_step, 1)
            lo_scaled("pre2", 8)
            mix = first("mixi")
            lo_parts(mix)
            dve.wait_ge(*full("gates"))
            dve.wait_ge(gbias_loaded, 16)
            dve.wait_ge(pre_rstd_ready, 3)
            for tau in range(NT):
                ins = dve.scalar_tensor_tensor(gt[:, tau, :], side("gates")[:, 8 * tau:8 * tau + 8],
                                               sums("pre2")[2][:, tau:tau + 1], gbias[:], ALU.mult, ALU.add)
            ins.then_inc(side_free("gates"), 1)
            lo_parts(mix + 1)
            dve.wait_ge(lb_step, 7)
            for j in range(2):
                dve.wait_ge(*full(("hfT", j)))
                for h in (2 * j, 2 * j + 1):
                    ins = dve.tensor_scalar(hk_T[:, h, :], side(("hfT", j))[:, (h % 2) * S:(h % 2 + 1) * S],
                                            lb[:, 5, h:h + 1], lb[:, 4, h:h + 1], ALU.mult, ALU.add)
                ins.then_inc(side_free(("hfT", j)), 1)
            lo_parts(mix + 2)
            dve.wait_ge(log_f_ready, 1)
            dve.wait_ge(keep_step, 2)
            dve.tensor_tensor_scan(cum[:].rearrange("p h s -> p (h s)"), keep.rearrange("p h s -> p (h s)"),
                                   dec[:].rearrange("p h s -> p (h s)"), 0.0, ALU.mult, ALU.add
                                   ).then_inc(cum_ready, 1)

            def level_diff(lv):
                n = 2 ** (lv - 1)
                if lv == 1:
                    dve.wait_ge(cum_ready, 1)
                else:
                    dve.wait_ge(scaled_ready, 2 * (lv - 1))
                if lv <= 6:
                    c = cum[:].rearrange("p h (b a n) -> p (h b) a n", a=2, n=n)
                    d = dec[:].rearrange("p h (b a n) -> p (h b) a n", a=2, n=n)
                    middle = c[:, :, 0, n - 1:n].to_broadcast([P, NH * S // (2 * n), n])
                    dve.tensor_tensor(d[:, :, 1, :], c[:, :, 1, :], middle, ALU.subtract)
                    ins = dve.tensor_tensor(d[:, :, 0, :], middle, c[:, :, 0, :], ALU.subtract)
                else:
                    c = cum[:].rearrange("p h (b n) -> p h b n", n=CHUNK)
                    d = dec[:].rearrange("p h (b n) -> p h b n", n=CHUNK)

                    def chunk_sum(b):
                        return c[:, :, b, CHUNK - 1:CHUNK].to_broadcast([P, NH, CHUNK])

                    if lv == 7:
                        for b in (0, 2):
                            dve.tensor_tensor(d[:, :, b, :], chunk_sum(b), c[:, :, b, :], ALU.subtract)
                            ins = dve.tensor_copy(d[:, :, b + 1, :], c[:, :, b + 1, :])
                    else:
                        dve.tensor_tensor(d[:, :, 0, :], chunk_sum(0), c[:, :, 0, :], ALU.subtract)
                        dve.tensor_tensor(d[:, :, 1, :], chunk_sum(1), c[:, :, 1, :], ALU.subtract)
                        dve.tensor_copy(d[:, :, 2, :], c[:, :, 2, :])
                        dve.tensor_tensor(d[:, :, 3, :], c[:, :, 3, :], chunk_sum(2), ALU.add
                                          ).then_inc(diff_part, 1)
                        dve.wait_ge(diff_part, 1)
                        ins = dve.tensor_tensor(d[:, :, 0, :], d[:, :, 0, :], chunk_sum(1), ALU.add)
                ins.then_inc(diff_ready, 1)

            def level_scale(lv):
                dve.wait_ge(exp_ready, lv)
                d = dec[:].rearrange("p h s -> p (h s)")
                dve.tensor_tensor(qs[:, lv % 2, :], hq_T[:].rearrange("p h s -> p (h s)"), d, ALU.mult
                                  ).then_inc(scaled_ready, 1)
                dve.tensor_tensor(ks[:, lv % 2, :], hk_T[:].rearrange("p h s -> p (h s)"), d, ALU.mult
                                  ).then_inc(scaled_ready, 1)

            def level_take(lv):
                for blk in range(NT):
                    key = ("lv", lv, blk)
                    dve.wait_ge(*full(key))
                    if lv:
                        dve.wait_ge(*freed(("lv", lv - 1, blk)))
                    dve.copy_predicated(hsc[:, blk, :, :], level[:, lv, :].unsqueeze(1).to_broadcast([P, NH, P]),
                                        side(key)[:].rearrange("p (h t) -> p h t", h=NH)).then_inc(side_free(key), 1)

            level_diff(1)
            dve.wait_ge(row_step, 3)
            i_row, f_row = side("gatesT")[0:NH, 0:S], side("gatesT")[0:NH, S:2 * S]
            dve.scalar_tensor_tensor(row[:, 0, :], f_row, 0.0, row[:, 2, :], ALU.min, ALU.subtract
                                     ).then_inc(row_step, 1)
            dve.wait_ge(row_step, 4)
            dve.tensor_tensor_scan(row[:, 1, :], row[:, 0, :], row[:, 0, :], 0.0, ALU.add, ALU.min
                                   ).then_inc(row_step, 1)
            dve.wait_ge(row_step, 5)
            dve.tensor_tensor(row[:, 0, :], i_row, row[:, 1, :], ALU.subtract).then_inc(side_free("gatesT"), 1)
            dve.wait_ge(*freed("gatesT"))
            dve.tensor_tensor_scan(row[:, 2, :], row[:, 0, :], row[:, 0, :], 0.0, ALU.max, ALU.max
                                   ).then_inc(row_step, 1)
            dve.wait_ge(row_step, 6)
            dve.tensor_tensor(row[:, 3, :], row[:, 1, :], row[:, 2, :], ALU.add).then_inc(row_step, 1)
            lo_parts(mix + 3)
            dve.wait_ge(*freed("umT"))
            for j in range(2):
                dve.wait_ge(*full(("mb", j)))
                for n in range(2):
                    h = 2 * j + n
                    m_all = side(("mb", j))[:, n * S:(n + 1) * S]
                    dve.tensor_scalar(mw[:, h, 0:S], m_all, um[:, h:h + 1], 0.0, ALU.subtract, ALU.max)
                    ins = dve.tensor_scalar(mw[:, h, S:S + P], m_all[:, P:S], um[:, 4 + h:5 + h], 0.0,
                                            ALU.subtract, ALU.max)
                ins.then_inc(side_free(("mb", j)), 1)
            dve.wait_ge(hk_T_ready, 1)
            dve.wait_ge(hsc_clear, 1)
            dve.wait_ge(level_ready, 1)
            level_scale(1)
            level_diff(2)
            lo_parts(mix + 4)
            level_take(0)
            level_scale(2)
            level_diff(3)
            level_take(1)
            level_scale(3)
            level_diff(4)
            lo_parts(mix + 5)
            level_take(2)
            level_scale(4)
            level_diff(5)
            level_take(3)
            for j in range(2):
                dve.wait_ge(*freed(("cv2T", j)))
            for t in range(CW2):
                for k in range(4):
                    w = cv("conv_w2", k * CW2 + t)
                    if t:
                        dve.wait_ge(conv2_step, 4 * (t - 1) + k + 1)
                        ins = dve.scalar_tensor_tensor(mqk_T[:, k, :], mqk_pad[:, k, t:t + S], w, mqk_T[:, k, :],
                                                       ALU.mult, ALU.add)
                    else:
                        ins = dve.tensor_scalar(mqk_T[:, k, :], mqk_pad[:, k, 0:S], w, cv("conv_b2", k),
                                                ALU.mult, ALU.add)
                    ins.then_inc(conv2_step, 1)
            level_scale(5)
            level_diff(6)
            lo_parts(mix + 6)
            level_take(4)
            level_scale(6)
            level_diff(7)
            level_take(5)
            level_scale(7)
            level_diff(8)
            level_take(6)
            level_scale(8)
            level_take(7)
            dve.wait_ge(mw_masked, 1)
            for h in range(NH):
                dve.wait_ge(*full(("ms", h)))
                dve.scalar_tensor_tensor(mw[:, h, :], side(("ms", h))[:, 0:3 * P], QK ** -0.5, mw[:, h, :],
                                         ALU.mult, ALU.mult).then_inc(side_free(("ms", h)), 1)
            dve.wait_ge(*full(("lv", 8, 0)))
            dve.tensor_copy(hoff[:], side(("lv", 8, 0))[:].rearrange("p (h t) -> p h t", h=NH)
                            ).then_inc(side_free(("lv", 8, 0)), 1)
            for tau in range(NT):
                for j in range(2):
                    key = ("mn", tau, j)
                    dve.wait_ge(*full(key))
                    n = 4 * tau + 2 * j
                    den = side(key)[:, 0:2 * (P + 1)].rearrange("p (h d) -> p h d", h=2)[:, :, P]
                    dve.scalar_tensor_tensor(mden[:, 0, n:n + 2], den, -1.0, um[:, 8 + n:10 + n], ALU.mult, ALU.max
                                             ).then_inc(mden_step, 1)
                    dve.wait_ge(mden_step, n + 1)
                    dve.tensor_tensor(mden[:, 0, n:n + 2], den, mden[:, 0, n:n + 2], ALU.max
                                      ).then_inc(mden_step, 1)
            dve.wait_ge(mden_step, 8)
            dve.reciprocal(mden[:, 1, :], mden[:, 0, :]).then_inc(mden_step, 1)
            dve.wait_ge(mden_step, 9)
            for tau in range(NT):
                for j in range(2):
                    key = ("mn", tau, j)
                    n = 4 * tau + 2 * j
                    num = side(key)[:, 0:2 * (P + 1)].rearrange("p (h d) -> p h d", h=2)[:, :, 0:P]
                    dst = qs[:, 1, n * P:(n + 2) * P].rearrange("p (h d) -> p h d", h=2)
                    dve.tensor_tensor(dst, num, mden[:, 1, n:n + 2].unsqueeze(2).to_broadcast([P, 2, P]), ALU.mult
                                      ).then_inc(side_free(key), 1)
            for n, (slot, gates, count) in enumerate(((1, mo, 1), (0, hgate, 3))):
                dve.wait_ge(mix_sq, count)
                dve.tensor_reduce(mstat[:, 2 * n, :], ks[:, slot, :].rearrange("p (h d) -> p h d", d=P), AX.X, ALU.add
                                  ).then_inc(mix_ss, 1)
                if slot == 0:
                    dve.wait_ge(*freed(("ho", 1)))
                o = qs[:, slot, :].rearrange("p (h d) -> p h d", d=P)
                dve.wait_ge(mix_rstd, n + 1)
                dve.tensor_tensor(o, o, mstat[:, 4 + n, :].unsqueeze(2).to_broadcast([P, 8, P]), ALU.mult
                                  ).then_inc(mix_scaled, 1)
                dve.wait_ge(mix_scaled, n + 1)
                dve.wait_ge(gates_scaled, 2)
                for tau in range(NT):
                    dve.tensor_tensor(tmp[:, tau, slot * CB:(slot + 1) * CB], qs[:, slot, tau * CB:(tau + 1) * CB],
                                      gates[:, tau, :], ALU.mult).then_inc(mixed, 1)
            for j in range(4):
                lo_of("mxT", j, act_lo[:, 2 * j:2 * j + 2, :], act_hi[:, 2 * j:2 * j + 2, :], HI_BEFORE["mxT"] + j + 1)
            dve.wait_ge(row_loaded["post1"], 16)
            post("post_m", "mixo", spread[:, 1, :], 2)
            lo_scaled("pre3", 16)
            feed_forward(1, "pre3", "f2i")
            dve.wait_ge(factor_ready, 3)
            post("post_f2", "f2o", spread[:, 0, :], 3)


def kernel(**inputs):
    from concourse import bacc
    from concourse.bass_utils import run_bass_kernel_spmd

    a = {k: np.asarray(v) for k, v in inputs.items()}

    def units(w):
        k, n = w.shape
        return w.reshape(k // P, P, n // CB, CB).transpose(2, 0, 1, 3).reshape(-1, P, CB)

    def pairs(left, right):
        k, n = left.shape
        return np.stack([left.reshape(k, n // 256, 256), right.reshape(k, n // 256, 256)], axis=2).reshape(k, 2 * n)

    w_in = a["w_in"][0]
    q, k, v, z_ret, u_val, u_gate, z_conv, g_a, g_b = np.split(
        w_in, [1024, 2048, 4096, 6144, 7168, 8192, 9216, 10240], axis=1)
    mix_in = a["w_mix_in_2"][0]
    hq, hf, hi, hgate, mqk, mv, mo, gates = np.split(mix_in, [512, 1024, 1536, 2048, 2560, 3072, 3584], axis=1)
    all_units = np.concatenate([
        units(pairs(u_val, u_gate)), units(q), units(k), units(v), units(z_ret), units(z_conv), units(g_a), units(g_b),
        units(a["w_ret_out"][0]), units(a["w_conv_out"][0]), units(a["w_out"][0]),
        units(pairs(a["ffn1_w_in_2"][0][:, :FF], a["ffn1_w_in_2"][0][:, FF:])), units(a["ffn1_w_out_2"][0]),
        units(hq), units(hf), units(hi), units(mqk), units(mv), units(hgate), units(mo), units(a["w_mix_out_2"][0]),
        units(pairs(a["ffn2_w_in_2"][0][:, :FF], a["ffn2_w_in_2"][0][:, FF:])), units(a["ffn2_w_out_2"][0])])
    stream = np.ascontiguousarray(all_units.reshape(GROUPS, UPG, P, CB).transpose(0, 2, 1, 3)).reshape(
        GROUPS, P, UPG * CB)

    def columns(vec):
        return vec.reshape(-1, P).T

    def taps(w):
        return w.reshape(w.shape[0], -1, P).transpose(2, 1, 0).reshape(P, -1)

    b_ada = a["b_ada"][0]
    cols = np.ascontiguousarray(np.concatenate([
        columns(a["c"][0]), columns(a["pre_norm_g"][0]), columns(b_ada[:2 * D]), columns(a["conv_b"][0]),
        taps(a["conv_w"][0]), columns(a["norm_pre_2"][0]), columns(a["hgrn_lb_logits_2"][:2]), taps(a["conv_w_2"][0]),
        columns(a["conv_b_2"][0])], axis=1))
    rows = np.ascontiguousarray(np.stack([
        b_ada[2 * D:], a["conv_ln_g"][0], a["conv_ln_b"][0], a["post_norm_g"][0], a["norm_post_2"][0, 0],
        np.concatenate([a["hgrn_norm_2"][0], a["mlstm_norm_2"][0]]), a["norm_post_2"][0, 1], a["norm_post_2"][0, 2]]))

    idx = np.arange(P)
    log_gamma = np.log1p(-np.exp2(-5.0 - np.arange(RH)))
    gap = idx[None, :] - idx[:, None]
    decay = np.zeros((P, RH, 3 * P))
    for h in range(RH):
        same = np.where(gap >= 0, np.exp(log_gamma[h] * np.maximum(gap, 0)), 0.0)
        decay[:, h] = np.concatenate([same, np.exp(log_gamma[h] * (gap + P)), same], axis=1) / 16.0
    levels = np.zeros((P, 8, P), np.float32)
    levels[:, 0] = gap == 0
    for lv in range(1, 8):
        size = 2 ** lv
        s_, t_ = idx[:, None], idx[None, :]
        levels[:, lv] = (s_ // size == t_ // size) & (s_ % size < size // 2) & (t_ % size >= size // 2)
    sel = np.zeros((NH, NH, P), np.float32)
    for h in range(NH):
        sel[h, h] = 1.0
    inv_freq = np.float32(10000.0) ** (-np.arange(P, dtype=np.float32) / np.float32(P))
    arrays = {
        "stream": stream,
        "ada": np.ascontiguousarray(a["w_ada"][0].reshape(KD, P, 3 * D)),
        "gates_w": np.ascontiguousarray(gates.reshape(KD, P, 8).transpose(1, 0, 2).reshape(P, KD * 8)),
        "cols": cols, "rows": rows, "gate_bias": np.ascontiguousarray(a["mlstm_gate_bias_2"][0]),
        "x": np.ascontiguousarray(a["x"][0]),
        "pos": np.ascontiguousarray(a["positions"][0].reshape(NT, P).T),
        "ident": np.eye(P, dtype=np.float32),
        "inv_freq": np.ascontiguousarray(np.broadcast_to(inv_freq, (P, P))),
        "decay": decay.reshape(P, -1).astype(np.float32),
        "level": levels.reshape(P, -1),
        "causal": (gap >= 0).astype(np.float32),
        "sel": sel,
    }
    nc = bacc.Bacc("TRN2", target_bir_lowering=False, num_devices=1)
    args = [nc.dram_tensor(f"in_{n}", v.shape, mybir.dt.from_np(v.dtype), kind="ExternalInput").ap()
            for n, v in arrays.items()]
    args.append(nc.dram_tensor("out_x", (S, D), F32, kind="ExternalOutput").ap())
    build_program(nc, *args)
    r = run_bass_kernel_spmd(nc, [{f"in_{n}": v for n, v in arrays.items()}], core_ids=[0])
    return r.results[0]["out_x"].reshape(1, S, D)
```

```python
from contextlib import ExitStack

import numpy as np

import concourse.bass as bass
from concourse import mybir

F32 = mybir.dt.float32
F32R = mybir.dt.float32r
U8 = mybir.dt.uint8
I32 = mybir.dt.int32
ALU = mybir.AluOpType
ACT = mybir.ActivationFunctionType
AX = mybir.AxisListType

P = 128
S = 256
NT = S // P
D = 1024
KD = D // P
CB = 512
UPG = 2
RH = 4
CW = 31
CW2 = 4
FF = 2816
FB = FF // 256
KF = FF // P
NH = 4
CHUNK = 64
QK = 64

STAGES = {}
_b = 0
_UNIT0 = [0]
for _name, _n, _k in (("u", 4, KD), ("qk", 4, KD), ("v", 4, KD), ("z", 4, KD), ("zc", 2, KD), ("g", 4, KD),
                      ("ret", 2, 2 * KD), ("conv", 2, KD), ("wout", 2, KD),
                      ("f1i", FB, KD), ("f1o", 2, KF), ("mixi", 7, KD), ("mixo", 2, KD),
                      ("f2i", FB, KD), ("f2o", 2, KF)):
    STAGES[_name] = (_b, _n, _k)
    for _ in range(_n):
        _UNIT0.append(_UNIT0[-1] + _k)
    _b += _n
BLOCKS = _b
UNITS = _UNIT0[-1]
GROUPS = UNITS // UPG
assert UNITS % UPG == 0
RAW = 4
RING = 8
LOOP_GROUPS = 2 * KD // UPG


ROUNDS = KD // 2
SUMMED = 6
START = 2 * KD // UPG


def first(stage):
    return STAGES[stage][0]


def group_end(b):
    if b in (0, 1):
        return START
    return -(-_UNIT0[b + 1] // UPG)


def split_to(b):
    if b < 0:
        return START
    return min(group_end(min(b + 1, BLOCKS - 1)), group_end(b) + RING // 2)


COLS = {}
_c = 0
for _name, _n in (("c", 8), ("pre_g", 8), ("b_mod", 16), ("conv_b", 8), ("conv_w", 8 * CW),
                  ("pre2", 24), ("lb", 8), ("conv_w2", 4 * CW2), ("conv_b2", 4)):
    COLS[_name] = _c
    _c += _n
NCOLS = _c

ROWS = ["b_gate", "ln_g", "ln_b", "post_g", "post0", "mix_norm", "post1", "post2"]

SIDE = {}
_uses = {4: 0, 5: 0, 6: 0, 7: 0}


def _side(key, bank, times=1):
    SIDE[key] = (bank, _uses[bank] + 1)
    _uses[bank] += times


def _side4(key):
    for j in range(4):
        _side((key, j), 4 + j)


def _side_x(key):
    for tau in range(NT):
        for half in range(2):
            _side((key, tau, half), 4 + 2 * tau + half)


def _plan_side():
    _side4("pre0")
    for r in range(ROUNDS):
        _side(("mod", r), 4 + r)
    _side4("aT")
    _side(("gate", 0), 5)
    _side(("gate", 1), 6)
    for m in range(6):
        if m >= 2:
            _side(("ro", m - 2, 0), 7)
            _side(("ro", m - 2, 1), 4)
        if 1 <= m <= 4:
            _side(("rs", m - 1), 6)
        if m <= 3:
            _side(("qT", m), 4)
            _side(("kT", m), 5)
    for j in range(8):
        _side(("retT", j), 4 + j % 4)
    for key in ("cvtok", "cvT", "mgT"):
        _side4(key)
    _side_x("pre1")
    _side(("ffT", 0, 0), 4, (FB + 1) // 2)
    _side(("ffT", 0, 1), 5, FB // 2)
    _side_x("pre2")
    _side("gate_rows", 7)
    _side("gates", 6)
    _side(("hqT", 0), 4)
    _side(("hqT", 1), 5)
    _side(("hfT", 0), 6)
    _side(("hfT", 1), 7)
    _side("gatesT", 6)
    _side("umT", 6)
    _side(("mb", 0), 4)
    _side(("mb", 1), 5)
    for lv in range(8):
        if lv == 1:
            _side(("cv2T", 0), 6)
            _side(("cv2T", 1), 7)
        if lv == 4:
            for h in range(NH):
                _side(("ms", h), 4 + h)
        if lv == 7:
            for t in range(NT):
                for j in range(2):
                    _side(("mn", t, j), 4 + 2 * t + j)
        for blk in range(NT):
            _side(("lv", lv, blk), 4 + 2 * (lv % 2) + blk)
    _side(("lv", 8, 0), 4)
    _side(("ho", 0), 6)
    _side(("ho", 1), 7)
    _side4("mxT")
    _side_x("pre3")
    _side(("ffT", 1, 0), 4, (FB + 1) // 2)
    _side(("ffT", 1, 1), 5, FB // 2)


_plan_side()

HI_BEFORE = {}
_n = 0
for _name, _k in (("pre0", 4), ("retT", 8), ("cvT", 4), ("mgT", 4), ("pre1", 16), (("ffT", 0), FB), ("pre2", 16),
                  ("mxT", 4), ("pre3", 16), (("ffT", 1), FB)):
    HI_BEFORE[_name] = _n
    _n += _k

NORMS = ["pre0", "post_w", "pre1", "post_f1", "pre2", "post_m", "pre3", "post_f2"]
SUMS_BEFORE = {}
_n = 0
for _name in NORMS:
    SUMS_BEFORE[_name] = _n
    _n += 2 if _name.startswith("pre") else 4

PRES = [_name for _name in NORMS if _name.startswith("pre")]

TAIL = RING // 2 * UPG

TWO_PI = 2 * np.pi
TWO_PI_1 = 6.28125
TWO_PI_2 = float(np.round((TWO_PI - TWO_PI_1) * 2**21) / 2**21)
TWO_PI_3 = float(TWO_PI - TWO_PI_1 - TWO_PI_2)
ROUND = 1.5 * 2**23
PI_INSIDE = 3.1415925


def build_program(nc, stream, ada, ada_gate, gates_w, cols, rows, gate_bias, x_in, pos_in,
                  ident_in, inv_freq_in, decay_in, level_in, causal_in, sel_in, out):
    ctx = ExitStack()
    with ctx:
        def sb(name, shape, dt=F32, stack=ctx):
            return stack.enter_context(nc.sbuf_tensor(name, shape, dt))

        def sem(name):
            return ctx.enter_context(nc.semaphore(name))

        gate_w_loaded = [sem(f"gate_w_loaded{n}") for n in range(KD)]
        h_T_ready = sem("h_T_ready")
        block0_done = sem("block0_done")
        tile0_done = sem("tile0_done")
        x_half_ready = sem("x_half_ready")
        post_bank_read = sem("post_bank_read")
        ada_summed = sem("ada_summed")
        gate_scaled = sem("gate_scaled")
        gate_summed = sem("gate_summed")
        pre_var_ready = sem("pre_var_ready")
        pre_rstd_ready = sem("pre_rstd_ready")
        post_var_ready = sem("post_var_ready")
        post_rstd_ready = sem("post_rstd_ready")
        half_rstd_ready = sem("half_rstd_ready")
        raw_loaded = [sem(f"raw_loaded{n}") for n in range(RAW)]
        ada_loaded = [sem(f"ada_loaded{n}") for n in range(KD)]
        row_loaded = {name: sem(f"{name}_loaded") for name in ROWS}
        pair_freed = [sem(f"pair_freed{n}") for n in range(2)]
        side_filled = [sem(f"side_filled{n}") for n in range(4, 8)]
        side_freed = [sem(f"side_freed{n}") for n in range(4, 8)]
        x_loaded = sem("x_loaded")
        col_loaded = sem("col_loaded")
        ident_loaded = sem("ident_loaded")
        pos_loaded = sem("pos_loaded")
        freq_loaded = sem("freq_loaded")
        decay_loaded = sem("decay_loaded")
        w_lo_ready = sem("w_lo_ready")
        x_ready = sem("x_ready")
        out_written = sem("out_written")
        w_used = sem("w_used")
        normed = sem("normed")
        ones_ready = sem("ones_ready")
        act0_ready = sem("act0_ready")
        rotated = sem("rotated")
        ret_ready = sem("ret_ready")
        conv_step = sem("conv_step")
        conv_act_ready = sem("conv_act_ready")
        merged = sem("merged")
        gw_ready = sem("gw_ready")
        row_step = sem("row_step")
        sel_loaded = sem("sel_loaded")
        q_scaled = sem("q_scaled")
        k_scaled = sem("k_scaled")
        hgrn_squared = sem("hgrn_squared")
        hk_T_ready = sem("hk_T_ready")
        mqk_T_ready = sem("mqk_T_ready")
        mv_ones = sem("mv_ones")
        mixed = sem("mixed")
        w_hi_ready = sem("w_hi_ready")
        ss_ready = sem("ss_ready")
        act_hi_ready = sem("act_hi_ready")
        trig_step = sem("trig_step")
        trig_ready = sem("trig_ready")
        tanh_ready = sem("tanh_ready")
        pad_ready = sem("pad_ready")
        ln_step = sem("ln_step")
        conv_silu = sem("conv_silu")
        silu_ready = sem("silu_ready")
        gw_loaded = sem("gw_loaded")
        gw_hi_ready = sem("gw_hi_ready")
        lb_step = sem("lb_step")
        lb_exp = sem("lb_exp")
        log_f_ready = sem("log_f_ready")
        mw_exp = sem("mw_exp")
        diff_ready = sem("diff_ready")
        exp_ready = sem("exp_ready")
        mqk_pad_ready = sem("mqk_pad_ready")
        conv2_step = sem("conv2_step")
        mix_sq = sem("mix_sq")
        half_ready = sem("half_ready")
        rot_step = sem("rot_step")
        head_var = sem("head_var")
        head_eps = sem("head_eps")
        head_rstd = sem("head_rstd")
        ln_var = sem("ln_var")
        ln_eps = sem("ln_eps")
        ln_rstd = sem("ln_rstd")
        x_again = sem("x_again")
        factor_ready = sem("factor_ready")
        gbias_loaded = sem("gbias_loaded")
        level_loaded = sem("level_loaded")
        causal_loaded = sem("causal_loaded")
        hsc_clear = sem("hsc_clear")
        level_ready = sem("level_ready")
        keep_step = sem("keep_step")
        mw_masked = sem("mw_masked")
        gates_scaled = sem("gates_scaled")
        mo_step = sem("mo_step")
        mix_ss = sem("mix_ss")
        mix_var = sem("mix_var")
        mix_rstd = sem("mix_rstd")
        mod_ready = sem("mod_ready")
        head_bn = sem("head_bn")
        ln_bn = sem("ln_bn")
        cum_ready = sem("cum_ready")
        diff_part = sem("diff_part")
        mden_step = sem("mden_step")
        mix_scaled = sem("mix_scaled")

        raw = sb("raw", [P, RAW, UPG * CB])
        w_hi = sb("w_hi", [P, RING, UPG * CB], F32R)
        w_lo = sb("w_lo", [P, RING, UPG * CB], F32R)
        act_hi = sb("act_hi", [P, KD, S], F32R)
        act_lo = sb("act_lo", [P, KD, S], F32R)
        x = sb("x", [P, NT, D])
        tmp = sb("tmp", [P, NT, D])
        tmp_T = tmp[:].rearrange("p t d -> p (t d)").rearrange("p (k s) -> p k s", s=S)
        spread = sb("spread", [P, 2, D])
        gate_bc = sb("gate_bc", [P, D])
        ident = sb("ident", [P, P])
        col = sb("col", [P, NCOLS])
        half_power = sb("half_power", [P, 8])
        stat = sb("stat", [P, 8 * len(NORMS)])
        head_stat = sb("head_stat", [P, NT * RH, 10])
        ln_stat = sb("ln_stat", [P, NT, 16])
        junk = sb("junk", [P, D])
        bank = [ctx.enter_context(nc.psum_tensor(f"bank{i}", [P, CB], F32)) for i in range(8)]

        with ExitStack() as own:
            ada_w = sb("ada_w", [P, ROUNDS, KD, CB], stack=own)
            mod_T = sb("mod_T", [P, 16], stack=own)
            h_T = sb("h_T", [P, KD, S], stack=own)
            ang = sb("ang", [P, NT, 2, P], stack=own)
            turns = sb("turns", [P, NT, 2, P], stack=own)
            inv_freq = sb("inv_freq", [P, P], stack=own)
            pos_i = sb("pos_i", [P, NT], I32, stack=own)
            pos_f = sb("pos_f", [P, NT], stack=own)
        with ExitStack() as own:
            qkv = sb("qkv", [P, 4, NT, D], stack=own)
            z = sb("z", [P, 2, NT, D], stack=own)
            g = sb("g", [P, 2, NT, D], stack=own)
            a_T = sb("a_T", [P, KD, S + CW - 1], stack=own)
            qk_T = sb("qk_T", [P, 2, 2, S], stack=own)
        with ExitStack() as own:
            sb("under_ret", [P, 2, NT, D], stack=own)
            ret_hi = sb("ret_hi", [P, 2 * KD, S], F32R, stack=own)
            ret_lo = sb("ret_lo", [P, 2 * KD, S], F32R, stack=own)
        flat = spread[:].rearrange("p a d -> p (a d)")
        trig = flat[:, 0:512].rearrange("p (t w f) -> p t w f", t=NT, w=2)
        decay = flat[:, 512:2048].rearrange("p (h c) -> p h c", h=RH)
        part = flat[:, 512:1024].rearrange("p (t w f) -> p t w f", t=NT, w=2)
        masked = junk[:, 0:768].rearrange("p (a c) -> p a c", a=2)
        odd_taps = junk[:, 768:1024]
        ones = junk[:, 512:640]
        tanh_u = junk[:, 0:512].rearrange("p (t c) -> p t c", t=NT)
        gate_sum = qk_T[:].rearrange("p w k s -> p (w k s)")
        rot = g[:, 0, 0, :].rearrange("p (a h f) -> p a h f", a=2, h=RH)
        with ExitStack() as own:
            ff_hi = sb("ff_hi", [P, FB, 2 * S], F32R, stack=own)
            ff_lo = sb("ff_lo", [P, FB, 2 * S], F32R, stack=own)
            silu_g = sb("silu_g", [P, NT, 256], stack=own)
            ff_tok = sb("ff_tok", [P, 2, NT, 256], stack=own)
        with ExitStack() as own:
            hv = sb("hv", [P, NT, CB], stack=own)
            hgate = sb("hgate", [P, NT, CB], stack=own)
            mo = sb("mo", [P, NT, CB], stack=own)
            mqk = sb("mqk", [P, NT, CB], stack=own)
            mv = sb("mv", [P, NT, NH, P + 2], stack=own)
            hq_T = sb("hq_T", [P, NH, S], stack=own)
            hk_T = sb("hk_T", [P, NH, S], stack=own)
            cum = sb("cum", [P, NH, S], stack=own)
            dec = sb("dec", [P, NH, S], stack=own)
            half_rstd = sb("half_rstd", [P, NT], stack=own)
            qs = sb("qs", [P, 2, NH * S], stack=own)
            ks = sb("ks", [P, 2, NH * S], stack=own)
            hsc = sb("hsc", [P, NT, NH, P], stack=own)
            hoff = sb("hoff", [P, NH, P], stack=own)
            mqk_pad = sb("mqk_pad", [P, 4, S + CW2 - 1], stack=own)
            mqk_T = sb("mqk_T", [P, 4, S], stack=own)
            mw = sb("mw", [P, NH, 3 * P], stack=own)
            level = sb("level", [P, 8, P], U8, stack=own)
            causal = sb("causal", [P, P], stack=own)
            gw = sb("gw", [P, KD * 8], stack=own)
            gw_hi = sb("gw_hi", [P, KD * 8], F32R, stack=own)
            gw_lo = sb("gw_lo", [P, KD * 8], F32R, stack=own)
            gbias = sb("gbias", [P, 8], stack=own)
            gt = sb("gt", [P, NT, 8], stack=own)
            lb = sb("lb", [P, 6, NH], stack=own)
            um = sb("um", [P, 16], stack=own)
            mden = sb("mden", [P, 2, 8], stack=own)
            mstat = sb("mstat", [P, 6, 8], stack=own)
            sel = sb("sel", [NH, NH, P], stack=own)
        keep = junk[:].rearrange("p (h s) -> p h s", h=NH)
        gate_rows = spread[0:8, 1, 0:S]
        row = spread[0:NH, 1, :].rearrange("p (a s) -> p a s", a=4)

        def decays(lv):
            return dec[:] if lv % 2 else keep

        def cv(name, j, n=1):
            return col[:, COLS[name] + j:COLS[name] + j + n]

        def drained(b, off=None):
            return pair_freed[b % 2], plus(b // 2 + 1, off)

        def done(b, off=None):
            if b == 0:
                return block0_done, 1
            return w_used, plus(group_end(b), off, LOOP_GROUPS)

        def part_of(b, tau):
            return bank[2 * (b % 2) + tau]

        def plus(value, off, per=1):
            return value if off is None else value + off * per

        def side(key):
            return bank[SIDE[key][0]]

        def full(key, off=None):
            return side_filled[SIDE[key][0] - 4], plus(SIDE[key][1], off)

        def freed(key, off=None):
            return side_freed[SIDE[key][0] - 4], plus(SIDE[key][1], off)

        def side_free(key):
            return side_freed[SIDE[key][0] - 4]

        def pair_free(b):
            return pair_freed[b % 2]

        tiles0 = {"post_w": 1, "post_f1": 3, "post_m": 5, "post_f2": 7}

        def sums(name):
            n = 8 * NORMS.index(name)
            return stat[:, n:n + 4], stat[:, n + 4:n + 6], stat[:, n + 6:n + 8]

        block = ctx.enter_context(nc.Block())

        @block.sync
        def _(sp):
            def load(dst, src, loaded):
                sp.dma_start(dst, src).then_inc(loaded, 16)

            load(col[:], cols, col_loaded)
            load(ident[:], ident_in, ident_loaded)
            load(x[:], x_in.rearrange("(t p) d -> p t d", p=P), x_loaded)
            for r in range(ROUNDS):
                for half in range(2):
                    ks_ = slice(half * KD // 2, (half + 1) * KD // 2)
                    load(ada_w[:, r, ks_, :], ada[r].rearrange("p (k c) -> p k c", k=KD)[:, ks_, :], ada_loaded[2 * r + half])
                if r == 0:
                    load(pos_i[:], pos_in, pos_loaded)
                    load(inv_freq[:], inv_freq_in, freq_loaded)
                for n in range(r * START // ROUNDS, (r + 1) * START // ROUNDS):
                    if n >= RAW:
                        sp.wait_ge(w_lo_ready, n - RAW + 1)
                    load(raw[:, n % RAW, :], stream[n], raw_loaded[n % RAW])
            sp.wait_ge(trig_step, 13)
            load(decay[:], decay_in.rearrange("p (h c) -> p h c", h=RH), decay_loaded)
            with sp.Fori(START // RAW, GROUPS // RAW) as i:
                for n in range(RAW):
                    sp.wait_ge(w_lo_ready, i * RAW + (n - RAW + 1))
                    load(raw[:, n, :], stream[i * RAW + n], raw_loaded[n])
            for n in range(2 * NT):
                tau, c = divmod(n, 2)
                sp.wait_ge(x_ready, 3 * 2 * NT + n + 1)
                load(out[tau * P:(tau + 1) * P, c * CB:(c + 1) * CB], x[:, tau, c * CB:(c + 1) * CB], out_written)
            sp.wait_ge(out_written, 16 * 2 * NT)

        @block.tensor
        def _(pe):
            def gemm(b, hi, lo, off=None, mid=None, parts=None):
                k_tiles = _UNIT0[b + 1] - _UNIT0[b]
                if b >= 2:
                    pe.wait_ge(pair_free(b), plus(b // 2, off))
                for n in range(k_tiles):
                    if parts is not None and n % 2 == 0 and parts(n // 2) is not None:
                        pe.wait_ge(*parts(n // 2))
                    unit = _UNIT0[b] + n
                    group, place = divmod(unit, UPG)
                    cs = slice(place * CB, (place + 1) * CB)
                    if place == 0 or n == 0:
                        pe.wait_ge(w_lo_ready, plus(group + 1, off, LOOP_GROUPS))
                    wh, wl = w_hi[:, group % RING, cs], w_lo[:, group % RING, cs]
                    for tau in range(NT):
                        ah, al = hi(n)[:, tau * P:(tau + 1) * P], lo(n)[:, tau * P:(tau + 1) * P]
                        acc = part_of(b, tau)[:]
                        pe.matmul(acc, ah, wh, start=n == 0, stop=False)
                        pe.matmul(acc, ah, wl, start=False, stop=False)
                        mm = pe.matmul(acc, al, wh, start=False, stop=n == k_tiles - 1)
                    if place == UPG - 1:
                        mm.then_inc(w_used, 1)
                    if mid is not None and n in mid:
                        mid[n]()

            def gemm_by_tile(b, hi, lo, mid=None, parts=None):
                k_tiles = _UNIT0[b + 1] - _UNIT0[b]
                pe.wait_ge(pair_free(b), b // 2)
                order = [(n, tau) for n in range(k_tiles - TAIL) for tau in range(NT)]
                order += [(n, tau) for tau in range(NT) for n in range(k_tiles - TAIL, k_tiles)]
                for n, tau in order:
                    group, place = divmod(_UNIT0[b] + n, UPG)
                    cs = slice(place * CB, (place + 1) * CB)
                    if parts is not None and n % 2 == 0:
                        pe.wait_ge(*parts(tau, n // 2))
                    if tau == 0 and (place == 0 or n == 0):
                        pe.wait_ge(w_lo_ready, group + 1)
                    wh, wl = w_hi[:, group % RING, cs], w_lo[:, group % RING, cs]
                    ah, al = hi(n)[:, tau * P:(tau + 1) * P], lo(n)[:, tau * P:(tau + 1) * P]
                    acc = part_of(b, tau)[:]
                    pe.matmul(acc, ah, wh, start=n == 0, stop=False)
                    pe.matmul(acc, ah, wl, start=False, stop=False)
                    mm = pe.matmul(acc, al, wh, start=False, stop=n == k_tiles - 1)
                    if tau == 1 and place == UPG - 1:
                        mm.then_inc(w_used, 1)
                    if tau == 0 and n == k_tiles - 1:
                        mm.then_inc(tile0_done, 1)
                    if mid is not None and (tau, n) in mid:
                        mid[tau, n]()

            def act(n):
                return act_hi[:, n, :]

            def act_l(n):
                return act_lo[:, n, :]

            def ret(n):
                return ret_hi[:, n, :]

            def ret_l(n):
                return ret_lo[:, n, :]

            def ff(n):
                return ff_hi[:, n // 2, (n % 2) * S:(n % 2 + 1) * S]

            def ff_l(n):
                return ff_lo[:, n // 2, (n % 2) * S:(n % 2 + 1) * S]

            def begin(key, off=None):
                n = SIDE[key][1] - 1
                if n or off is not None:
                    pe.wait_ge(side_free(key), plus(n, off))

            def end(ins, key):
                ins.then_inc(side_filled[SIDE[key][0] - 4], 1)

            def turn(key, sources, off=None):
                begin(key, off)
                for n, src in enumerate(sources):
                    mm = pe.transpose(side(key)[:, n * P:(n + 1) * P], src, ident[:])
                end(mm, key)

            def turn_tok(key, j, src):
                turn((key, j), [src(tau, k) for k in (2 * j, 2 * j + 1) for tau in range(NT)])

            def turn_x(key, tau, posts):
                for half in range(2):
                    pe.wait_ge(x_ready, 2 * NT * (posts - 1) + 2 * tau + half + 1)
                    turn((key, tau, half), [x[:, tau, k * P:(k + 1) * P] for k in range(4 * half, 4 * half + 4)])

            def x_parts(key, posts):
                def parts(tau, j):
                    if j % 2 == 0:
                        return x_half_ready, 4 * (posts - 1) + 2 * tau + j // 2 + 1
                    return freed((key, tau, j // 2))
                return parts

            pe.wait_ge(ident_loaded, 16)
            pe.wait_ge(normed, 2)
            for j in range(4):
                turn_tok("pre0", j, lambda tau, k: tmp[:, tau, k * P:(k + 1) * P])
            def mod_sums(r):
                key = ("mod", r)
                pe.wait_ge(ada_loaded[2 * r + 1], 16)
                pe.wait_ge(ada_summed, SUMMED * (r + 1))
                begin(key)
                for q in range(4):
                    o = side(key)[:, q:q + 1]
                    for k in range(SUMMED, KD):
                        pe.matmul(o, ada_w[:, r, k, q * P:(q + 1) * P], cv("c", k), start=k == SUMMED, stop=False)
                    mm = pe.matmul(o, h_T[:, 2 * r + q // 2, (q % 2) * P:(q % 2 + 1) * P], ones[:, 0:1],
                                   start=False, stop=True)
                end(mm, key)

            pe.wait_ge(ones_ready, 1)
            pe.wait_ge(col_loaded, 16)
            mod_sums(0)
            def side_by_side(k, b):
                cs = slice(b * CB, (b + 1) * CB)
                for tau in range(NT):
                    ts_ = slice(tau * P, (tau + 1) * P)
                    acc = part_of(b, tau)[:]
                    pe.matmul(acc, act_hi[:, k, ts_], w_hi[:, k, cs], start=k == 0, stop=False)
                    pe.matmul(acc, act_hi[:, k, ts_], w_lo[:, k, cs], start=False, stop=False)
                    mm = pe.matmul(acc, act_lo[:, k, ts_], w_hi[:, k, cs], start=False, stop=k == KD - 1)
                return mm

            for k in range(KD - 2):
                if k % 2 == 0:
                    pe.wait_ge(act0_ready, k // 2 + 1)
                pe.wait_ge(w_lo_ready, k + 1)
                side_by_side(k, 0)
                side_by_side(k, 1).then_inc(w_used, 1)
                if k % 2 == 0:
                    mod_sums(k // 2 + 1)
            pe.wait_ge(act0_ready, ROUNDS)
            pe.wait_ge(w_lo_ready, KD)
            side_by_side(KD - 2, 0)
            side_by_side(KD - 1, 0).then_inc(block0_done, 1)
            side_by_side(KD - 2, 1).then_inc(w_used, 1)
            side_by_side(KD - 1, 1).then_inc(w_used, 1)
            for b in range(2, 4):
                gemm(b, act, act_l)
            pe.wait_ge(*drained(2))
            pe.wait_ge(*drained(3))
            for j in range(4):
                turn_tok("aT", j, lambda tau, k: tmp[:, tau, k * P:(k + 1) * P])
            with pe.Fori(0, 4) as i:
                for n in range(2):
                    gemm(first("qk") + n, act, act_l, off=i)
            pe.wait_ge(gate_summed, KD)
            for j in range(2):
                begin(("gate", j))
                end(pe.matmul(side(("gate", j))[:], ones, gate_sum[:, j * CB:(j + 1) * CB], start=True, stop=True),
                    ("gate", j))
            with pe.Fori(0, 2) as i:
                for n in range(2):
                    gemm(first("z") + n, act, act_l, off=i)

            def head_turn(h):
                pe.wait_ge(rotated, 2 * NT)
                for w, key in ((0, "qT"), (1, "kT")):
                    turn((key, h), [qkv[:, w, tau, h * 256 + k * P:h * 256 + (k + 1) * P]
                                    for k in range(2) for tau in range(NT)])

            def head_scores(h):
                key = ("rs", h)
                begin(key)
                pe.wait_ge(*freed(("qT", h)))
                pe.wait_ge(*freed(("kT", h)))
                for k in range(2):
                    pe.matmul(side(key)[:, 0:S], qk_T[:, 1, k, 0:P], qk_T[:, 0, k, :], start=k == 0, stop=k == 1)
                for k in range(2):
                    mm = pe.matmul(side(key)[:, S:S + P], qk_T[:, 1, k, P:S], qk_T[:, 0, k, P:S],
                                   start=k == 0, stop=k == 1)
                end(mm, key)

            def head_out(h):
                def v(tau):
                    return qkv[:, 2 + h // 2, tau, (h % 2) * CB:(h % 2 + 1) * CB]

                pe.wait_ge(*freed(("rs", h)))
                begin(("ro", h, 0))
                end(pe.matmul(side(("ro", h, 0))[:], masked[:, h % 2, 0:P], v(0), start=True, stop=True), ("ro", h, 0))
                begin(("ro", h, 1))
                pe.matmul(side(("ro", h, 1))[:], masked[:, h % 2, P:2 * P], v(0), start=True, stop=False)
                end(pe.matmul(side(("ro", h, 1))[:], masked[:, h % 2, 2 * P:3 * P], v(1), start=False, stop=True),
                    ("ro", h, 1))

            for m in range(6):
                if m >= 2:
                    head_out(m - 2)
                mid = {}
                if 1 <= m <= 4:
                    mid[3] = lambda: head_scores(m - 1)
                if m <= 3:
                    mid[6] = lambda: head_turn(m)
                gemm(first("zc") + m, act, act_l, mid=mid)
            pe.wait_ge(ret_ready, 2 * RH)
            for j in range(8):
                turn(("retT", j), [qkv[:, j % 2, tau, (j // 2) * 256 + k * P:(j // 2) * 256 + (k + 1) * P]
                                   for k in range(2) for tau in range(NT)])
            def conv_turn():
                pe.wait_ge(conv_step, KD * (CW + 1) + 1)
                for tau in range(NT):
                    for half in range(2):
                        turn(("cvtok", 2 * tau + half), [tmp_T[:, 4 * half + k, tau * P:(tau + 1) * P] for k in range(4)])

            def conv_turn_back():
                pe.wait_ge(conv_act_ready, NT)
                for j in range(4):
                    turn_tok("cvT", j, lambda tau, k: tmp[:, tau, k * P:(k + 1) * P])

            gemm(first("ret"), ret, ret_l, mid={KD - 1: conv_turn}, parts=lambda j: freed(("retT", j)))
            gemm(first("ret") + 1, ret, ret_l, mid={KD - 1: conv_turn_back})

            def merged_turn(c):
                pe.wait_ge(merged, NT * (c + 1))
                for j in range(2 * c, 2 * c + 2):
                    turn_tok("mgT", j, lambda tau, k: g[:, 0, tau, k * P:(k + 1) * P])

            gemm(first("conv"), act, act_l, parts=lambda j: freed(("cvT", j)))
            gemm(first("conv") + 1, act, act_l, mid={3: lambda: merged_turn(0)})
            gemm(first("wout"), ret, ret_l, mid={1: lambda: merged_turn(1)}, parts=lambda j: freed(("mgT", j)))
            gemm_by_tile(first("wout") + 1, ret, ret_l, mid={(1, 5): lambda: turn_x("pre1", 0, 1)})

            def feed_forward(which, key, posts, stage_in, stage_out, turn_next=None):
                b = first(stage_in)

                def hidden_turn(parity, off):
                    key = ("ffT", which, parity)
                    pe.wait_ge(*drained(b + parity, off))
                    turn(key, [ff_tok[:, parity, tau, k * P:(k + 1) * P] for k in range(2) for tau in range(NT)], off)

                def hidden(j):
                    if j == FB - 2:
                        return freed(("ffT", which, 1), FB // 2 - 1)
                    if j == FB - 1:
                        return freed(("ffT", which, 0), FB // 2)
                    return None

                gemm_by_tile(b, act, act_l, mid={(0, 5): lambda: turn_x(key, 1, posts)}, parts=x_parts(key, posts))
                with pe.Fori(0, (FB - 1) // 2) as i:
                    gemm(b + 1, act, act_l, off=i)
                    hidden_turn(0, i)
                    gemm(b + 2, act, act_l, off=i)
                    hidden_turn(1, i)
                gemm(first(stage_out), ff, ff_l, mid={3: lambda: hidden_turn(0, (FB - 1) // 2)}, parts=hidden)
                gemm_by_tile(first(stage_out) + 1, ff, ff_l, mid={(1, KF - 3): turn_next} if turn_next else None)

            feed_forward(0, "pre1", 1, "f1i", "f1o", turn_next=lambda: turn_x("pre2", 0, 2))

            mix = first("mixi")

            def hgrn_turn(key, c):
                pe.wait_ge(*drained(mix + c))
                for j in range(2):
                    turn((key, j), [tmp[:, tau, c * CB + k * P:c * CB + (k + 1) * P]
                                    for k in (2 * j, 2 * j + 1) for tau in range(NT)])

            def gates_turn():
                pe.wait_ge(*freed("gates"))
                begin("gatesT")
                for w in range(2):
                    for tau in range(NT):
                        mm = pe.matmul(side("gatesT")[0:NH, w * S + tau * P:w * S + (tau + 1) * P],
                                       gt[:, tau, 4 * w:4 * w + 4], ident[:], start=True, stop=True)
                end(mm, "gatesT")

            def um_turn():
                pe.wait_ge(row_step, 7)
                begin("umT")
                for w, r in ((0, 0), (1, 3)):
                    for tau in range(NT):
                        n = 8 * w + 4 * tau
                        mm = pe.matmul(side("umT")[:, n:n + 4], row[:, r, tau * P:(tau + 1) * P], ident[0:NH, 0:NH],
                                       start=True, stop=True)
                end(mm, "umT")

            def m_spread():
                pe.wait_ge(row_step, 6)
                pe.wait_ge(sel_loaded, 16)
                for j in range(2):
                    begin(("mb", j))
                    for n in range(2):
                        mm = pe.matmul(side(("mb", j))[:, n * S:(n + 1) * S], sel[:, 2 * j + n, :], row[:, 2, :],
                                       start=True, stop=True)
                    end(mm, ("mb", j))

            def level_scores(lv):
                if lv == 0:
                    pe.wait_ge(*freed(("hqT", 0)))
                    pe.wait_ge(*freed(("hqT", 1)))
                    pe.wait_ge(hk_T_ready, 1)
                    q_of, k_of = hq_T[:], hk_T[:]
                else:
                    pe.wait_ge(q_scaled, lv)
                    pe.wait_ge(k_scaled, lv)
                    q_of = qs[:, lv % 2, :].rearrange("p (h s) -> p h s", h=NH)
                    k_of = ks[:, lv % 2, :].rearrange("p (h s) -> p h s", h=NH)
                for blk in range(NT if lv < 8 else 1):
                    key = ("lv", lv, blk)
                    begin(key)
                    for h in range(NH):
                        s_at = slice(blk * P, (blk + 1) * P)
                        t_at = s_at if lv < 8 else slice(P, S)
                        mm = pe.matmul(side(key)[:, h * P:(h + 1) * P], k_of[:, h, s_at], q_of[:, h, t_at],
                                       start=True, stop=True)
                    end(mm, key)

            def conv2_turn():
                pe.wait_ge(*drained(mix + 2))
                for j in range(2):
                    turn(("cv2T", j), [mqk[:, tau, k * P:(k + 1) * P] for k in (2 * j, 2 * j + 1) for tau in range(NT)])

            def mlstm_scores(h):
                key = ("ms", h)
                begin(key)
                rows_at = slice((h % 2) * QK, (h % 2 + 1) * QK)
                q_of, k_of = mqk_T[rows_at, h // 2, :], mqk_T[rows_at, 2 + h // 2, :]
                pe.matmul(side(key)[:, 0:S], k_of[:, 0:P], q_of, start=True, stop=True)
                end(pe.matmul(side(key)[:, S:S + P], k_of[:, P:S], q_of[:, P:S], start=True, stop=True), key)

            def gates_product():
                pe.wait_ge(gw_ready, 2)
                begin("gate_rows")
                o = side("gate_rows")[0:8, 0:S]
                for k in range(KD):
                    cs = slice(8 * k, 8 * k + 8)
                    pe.matmul(o, gw_hi[:, cs], act_hi[:, k, :], start=k == 0, stop=False)
                    pe.matmul(o, gw_lo[:, cs], act_hi[:, k, :], start=False, stop=False)
                    mm = pe.matmul(o, gw_hi[:, cs], act_lo[:, k, :], start=False, stop=k == KD - 1)
                end(mm, "gate_rows")

            def gates_to_tokens():
                pe.wait_ge(*freed("gate_rows"))
                begin("gates")
                for tau in range(NT):
                    mm = pe.transpose(side("gates")[:, 8 * tau:8 * tau + 8], gate_rows[:, tau * P:(tau + 1) * P],
                                      ident[0:8, 0:8])
                end(mm, "gates")

            gemm_by_tile(mix, act, act_l, mid={(0, 5): lambda: turn_x("pre2", 1, 2)}, parts=x_parts("pre2", 2))
            gates_product()
            gemm(mix + 1, act, act_l, mid={1: gates_to_tokens, 3: lambda: hgrn_turn("hqT", 0)})
            gemm(mix + 2, act, act_l, mid={1: lambda: hgrn_turn("hfT", 1), 3: gates_turn})
            gemm(mix + 3, act, act_l, mid={0: um_turn, 3: m_spread})
            level_scores(0)
            conv2_turn()
            gemm(mix + 4, act, act_l, mid={3: lambda: level_scores(1)})
            level_scores(2)
            gemm(mix + 5, act, act_l, mid={3: lambda: level_scores(3)})
            pe.wait_ge(mqk_T_ready, 1)
            for h in range(NH):
                mlstm_scores(h)
            level_scores(4)

            def mlstm_out():
                for h in range(NH):
                    pe.wait_ge(*freed(("ms", h)))
                pe.wait_ge(mv_ones, 1)
                pe.wait_ge(*drained(mix + 3))
                for tau in range(NT):
                    for j in range(2):
                        key = ("mn", tau, j)
                        begin(key)
                        for n in range(2):
                            h = 2 * j + n
                            o = side(key)[:, n * (P + 1):(n + 1) * (P + 1)]
                            if tau == 0:
                                mm = pe.matmul(o, mw[:, h, 0:P], mv[:, 0, h, 0:P + 1], start=True, stop=True)
                            else:
                                pe.matmul(o, mw[:, h, P:S], mv[:, 0, h, 0:P + 1], start=True, stop=False)
                                mm = pe.matmul(o, mw[:, h, S:S + P], mv[:, 1, h, 0:P + 1], start=False, stop=True)
                        end(mm, key)

            gemm(mix + 6, act, act_l, mid={3: lambda: level_scores(5), 5: lambda: level_scores(6), 6: mlstm_out})
            for lv in range(7, 9):
                level_scores(lv)
            for tau in range(NT):
                pe.wait_ge(*freed(("lv", 7, tau)))
                if tau == 1:
                    pe.wait_ge(*freed(("lv", 8, 0)))
                key = ("ho", tau)
                begin(key)
                for h in range(NH):
                    o = side(key)[:, h * P:(h + 1) * P]
                    if tau == 1:
                        pe.matmul(o, hoff[:, h, :], hv[:, 0, h * P:(h + 1) * P], start=True, stop=False)
                    mm = pe.matmul(o, hsc[:, tau, h, :], hv[:, tau, h * P:(h + 1) * P], start=tau == 0, stop=True)
                end(mm, key)
            pe.wait_ge(mixed, NT)
            for j in range(2):
                turn_tok("mxT", j, lambda tau, k: tmp[:, tau, k * P:(k + 1) * P])

            def hgrn_mixed_turn():
                pe.wait_ge(mixed, 2 * NT)
                for j in range(2, 4):
                    turn_tok("mxT", j, lambda tau, k: tmp[:, tau, k * P:(k + 1) * P])

            gemm(first("mixo"), act, act_l, mid={3: hgrn_mixed_turn}, parts=lambda j: freed(("mxT", j)))
            gemm_by_tile(first("mixo") + 1, act, act_l, mid={(1, 5): lambda: turn_x("pre3", 0, 3)})
            feed_forward(1, "pre3", 3, "f2i", "f2o")

        @block.scalar
        def _(act):
            def hi_part(n, off=None):
                act.wait_ge(raw_loaded[n % RAW], plus(16 * (n // RAW + 1), off, 16 * LOOP_GROUPS // RAW))
                if n >= RING:
                    act.wait_ge(w_used, plus(n - RING + 1, off, LOOP_GROUPS))
                act.activation(w_hi[:, n % RING, :], raw[:, n % RAW, :], ACT.Copy).then_inc(w_hi_ready, 1)

            def hi_parts(b, off=None):
                for n in range(split_to(b - 1), split_to(b)):
                    hi_part(n, off)

            def squares(name, src):
                for tau in range(NT):
                    if SUMS_BEFORE[name] + tau:
                        act.wait_ge(ss_ready, SUMS_BEFORE[name] + tau)
                    act.activation(junk[:], src(tau), ACT.Square, accum_out=sums(name)[0][:, tau:tau + 1]
                                   ).then_inc(ss_ready, 1)

            def hi_of(key, j, dst, scale=1.0):
                act.wait_ge(*full((key, j)))
                act.activation(dst, side((key, j))[:].rearrange("p (k s) -> p k s", s=S), ACT.Copy,
                               scale=scale).then_inc(act_hi_ready, 1)

            def hi_scaled(key, tau, at):
                for half in range(2):
                    act.wait_ge(*full((key, tau, half)))
                    for n in range(4):
                        k = 4 * half + n
                        act.activation(act_hi[:, k, tau * P:(tau + 1) * P], side((key, tau, half))[:, n * P:(n + 1) * P],
                                       ACT.Copy, scale=cv("pre2", at + k)).then_inc(act_hi_ready, 1)

            def drain(b, dst, func, off=None, scale=1.0):
                act.wait_ge(*done(b, off))
                for tau in range(NT):
                    ins = act.activation(dst(tau), part_of(b, tau)[:], func, scale=scale)
                ins.then_inc(pair_free(b), 1)

            act.wait_ge(x_loaded, 16)
            squares("pre0", lambda tau: x[:, tau, :])
            for j in range(4):
                act.wait_ge(*full(("pre0", j)))
            for j in range(4):
                act.activation(tmp_T[:, 2 * j:2 * j + 2, :], side(("pre0", j))[:].rearrange("p (k s) -> p k s", s=S),
                               ACT.Copy).then_inc(side_free(("pre0", j)), 1)
            for j in range(ROUNDS):
                for n in (2 * j, 2 * j + 1):
                    hi_part(n)
                act.wait_ge(h_T_ready, j + 1)
                act.activation(act_hi[:, 2 * j:2 * j + 2, :], h_T[:, 2 * j:2 * j + 2, :], ACT.Copy
                               ).then_inc(act_hi_ready, 1)
            act.wait_ge(trig_step, 13)
            act.activation(trig, ang[:], ACT.Sin).then_inc(trig_ready, 1)
            for b in range(4):
                if b == 0:
                    hi_parts(1)
                if b >= 2:
                    hi_parts(b)
                act.wait_ge(*done(b))
                if b:
                    act.wait_ge(*drained(b - 1))
                for tau in range(NT):
                    act.activation(tanh_u[:, tau, :], part_of(b, tau)[:, 256:512], ACT.Tanh,
                                   scale=0.5).then_inc(tanh_ready, 1)
            act.wait_ge(pad_ready, 1)
            for j in range(4):
                act.wait_ge(*full(("aT", j)))
                act.activation(a_T[:, 2 * j:2 * j + 2, CW - 1:], side(("aT", j))[:].rearrange("p (k s) -> p k s", s=S),
                               ACT.Copy, scale=0.5).then_inc(side_free(("aT", j)), 1)
            with act.Fori(0, 4) as i:
                for n in range(2):
                    hi_parts(first("qk") + n, i)
                    drain(first("qk") + n, lambda tau: qkv[:, i, tau, n * CB:(n + 1) * CB], ACT.Copy, i)
            with act.Fori(0, 2) as i:
                for n in range(2):
                    hi_parts(first("z") + n, i)
                    drain(first("z") + n, lambda tau: z[:, i, tau, n * CB:(n + 1) * CB], ACT.Silu, i)
            for m in range(6):
                b = first("zc") + m
                hi_parts(b)
                if m <= 3:
                    if m:
                        act.wait_ge(*full(("rs", m - 1)))
                    for w, key in ((0, "qT"), (1, "kT")):
                        act.wait_ge(*full((key, m)))
                        act.activation(qk_T[:, w, :, :], side((key, m))[:].rearrange("p (k s) -> p k s", s=S),
                                       ACT.Copy).then_inc(side_free((key, m)), 1)
                if m < 2:
                    drain(b, lambda tau: x[:, tau, m * CB:(m + 1) * CB], ACT.Silu)
                else:
                    drain(b, lambda tau: g[:, (m - 2) // 2, tau, (m % 2) * CB:(m % 2 + 1) * CB], ACT.Tanh, scale=0.5)
            for j in range(8):
                hi_of("retT", j, ret_hi[:, 2 * j:2 * j + 2, :])
            hi_parts(first("ret"))
            for tau in range(NT):
                act.wait_ge(ln_step, 3 * NT + tau + 1)
                act.activation(tmp[:, tau, :], tmp[:, tau, :], ACT.Silu).then_inc(conv_silu, 1)
            hi_parts(first("ret") + 1)
            for j in range(4):
                hi_of("cvT", j, act_hi[:, 2 * j:2 * j + 2, :])
            hi_parts(first("conv"))
            hi_parts(first("conv") + 1)
            for j in range(4):
                hi_of("mgT", j, ret_hi[:, 2 * j:2 * j + 2, :], scale=0.5)

            def square_part(name, b, c, tau):
                act.wait_ge(ss_ready, SUMS_BEFORE[name] + 2 * c + tau)
                act.activation(junk[:, 0:CB], part_of(b, tau)[:], ACT.Square,
                               accum_out=sums(name)[0][:, 2 * c + tau:2 * c + tau + 1]).then_inc(ss_ready, 1)

            def post(name, stage, before, key=None, at=None):
                b = first(stage)
                hi_parts(b)
                act.wait_ge(*done(b))
                square_part(name, b, 0, 0)
                act.wait_ge(post_bank_read, 2 * before + 1)
                square_part(name, b, 0, 1)
                hi_parts(b + 1)
                act.wait_ge(tile0_done, tiles0[name])
                square_part(name, b + 1, 1, 0)
                if key is not None:
                    hi_scaled(key, 0, at)
                act.wait_ge(*done(b + 1))
                square_part(name, b + 1, 1, 1)
                if key is not None:
                    hi_scaled(key, 1, at)
                    act.wait_ge(x_ready, 2 * NT * (before + 1))
                    squares(key, lambda tau: x[:, tau, :])

            def rstd_of(name, tau):
                return sums(name)[2][:, tau:tau + 1]

            def feed_forward(which, name, stage):
                b0 = first(stage)

                def silu(b, off=None):
                    act.wait_ge(*done(b, off))
                    if b > b0:
                        act.wait_ge(*drained(b - 1, off))
                    for tau in range(NT):
                        act.activation(silu_g[:, tau, :], part_of(b, tau)[:, 0:256], ACT.Silu,
                                       scale=rstd_of(name, tau)).then_inc(silu_ready, 1)

                def hidden_hi(parity, j, off=None):
                    key = ("ffT", which, parity)
                    act.wait_ge(*full(key, off))
                    act.activation(ff_hi[:, j, :], side(key)[:], ACT.Copy).then_inc(act_hi_ready, 1)

                hi_parts(b0)
                act.wait_ge(pre_rstd_ready, 2 + 2 * which)
                silu(b0)
                with act.Fori(0, (FB - 1) // 2) as i:
                    for n in range(2):
                        hi_parts(b0 + 1 + n, i)
                        silu(b0 + 1 + n, i)
                        hidden_hi(n, 2 * i + n, i)
                hidden_hi(0, FB - 1, FB // 2)

            post("post_w", "wout", 0, "pre1", 0)
            feed_forward(0, "pre1", "f1i")
            post("post_f1", "f1o", 1, "pre2", 8)
            act.wait_ge(gw_loaded, 16)
            act.activation(gw_hi[:], gw[:], ACT.Copy).then_inc(gw_hi_ready, 1)
            act.wait_ge(lb_step, 3)
            act.activation(lb[:, 1:3, :], lb[:, 1:3, :], ACT.Exp).then_inc(lb_exp, 1)
            mix = first("mixi")

            def drain_scaled(b, dst, func):
                act.wait_ge(*done(b))
                for tau in range(NT):
                    ins = act.activation(dst(tau), part_of(b, tau)[:], func, scale=rstd_of("pre2", tau))
                ins.then_inc(pair_free(b), 1)

            hi_parts(mix)
            act.wait_ge(pre_rstd_ready, 3)
            drain_scaled(mix, lambda tau: tmp[:, tau, 0:CB], ACT.Silu)
            hi_parts(mix + 1)
            for j in range(2):
                act.wait_ge(*full(("hqT", j)))
                act.activation(hq_T[:, 2 * j:2 * j + 2, :], side(("hqT", j))[:].rearrange("p (h s) -> p h s", s=S),
                               ACT.Copy).then_inc(side_free(("hqT", j)), 1)
            drain_scaled(mix + 1, lambda tau: tmp[:, tau, CB:D], ACT.Sigmoid)
            hi_parts(mix + 2)
            for j in range(2):
                act.wait_ge(*freed(("hfT", j)))
            act.activation(dec[:], hk_T[:], ACT.Ln).then_inc(log_f_ready, 1)
            act.wait_ge(*full("gatesT"))
            f_row = side("gatesT")[0:NH, S:2 * S]
            act.activation(row[:, 2, :], f_row, ACT.Abs).then_inc(row_step, 1)
            act.wait_ge(row_step, 1)
            act.activation(row[:, 2, :], row[:, 2, :], ACT.Exp, scale=-1.0).then_inc(row_step, 1)
            act.wait_ge(row_step, 2)
            act.activation(row[:, 2, :], row[:, 2, :], ACT.Ln, bias=1.0).then_inc(row_step, 1)
            drain_scaled(mix + 2, lambda tau: mqk[:, tau, :], ACT.Copy)
            hi_parts(mix + 3)
            act.wait_ge(*full("umT"))
            act.activation(um[:, 8:16], side("umT")[:, 8:16], ACT.Exp, scale=-1.0)
            act.activation(um[:, 0:8], side("umT")[:, 0:8], ACT.Copy).then_inc(side_free("umT"), 1)

            def level_exp(lv):
                act.wait_ge(diff_ready, lv)
                act.activation(decays(lv), decays(lv), ACT.Exp).then_inc(exp_ready, 1)

            level_exp(1)
            for j in range(2):
                act.wait_ge(*freed(("mb", j)))
            act.activation(mw[:], mw[:], ACT.Exp, scale=-1.0).then_inc(mw_exp, 1)
            level_exp(2)
            act.wait_ge(*done(mix + 3))
            for tau in range(NT):
                ins = act.activation(mv[:, tau, :, 0:P], part_of(mix + 3, tau)[:].rearrange("p (h d) -> p h d", h=NH),
                                     ACT.Copy, scale=rstd_of("pre2", tau))
            ins.then_inc(pair_free(mix + 3), 1)
            hi_parts(mix + 4)
            act.wait_ge(mqk_pad_ready, 1)
            for j in range(2):
                act.wait_ge(*full(("cv2T", j)))
                act.activation(mqk_pad[:, 2 * j:2 * j + 2, CW2 - 1:],
                               side(("cv2T", j))[:].rearrange("p (h s) -> p h s", s=S), ACT.Copy
                               ).then_inc(side_free(("cv2T", j)), 1)
            level_exp(3)
            level_exp(4)
            act.wait_ge(conv2_step, 4 * CW2)
            act.activation(mqk_T[:], mqk_T[:], ACT.Silu).then_inc(mqk_T_ready, 1)
            drain_scaled(mix + 4, lambda tau: hv[:, tau, :], ACT.Copy)
            level_exp(5)
            hi_parts(mix + 5)
            level_exp(6)
            level_exp(7)
            act.wait_ge(*done(mix + 5))
            act.wait_ge(half_rstd_ready, 1)
            for tau in range(NT):
                ins = act.activation(mo[:, tau, :], part_of(mix + 5, tau)[:], ACT.Tanh, scale=half_rstd[:, tau:tau + 1])
            ins.then_inc(pair_free(mix + 5), 1)
            hi_parts(mix + 6)
            level_exp(8)
            for tau in range(NT):
                for j in range(2):
                    act.wait_ge(*freed(("mn", tau, j)))
            act.activation(tmp[:, :, CB:D], tmp[:, :, 0:CB], ACT.Square).then_inc(mix_sq, 1)
            drain_scaled(mix + 6, lambda tau: hgate[:, tau, :], ACT.Silu)
            for tau in range(NT):
                key = ("ho", tau)
                act.wait_ge(*full(key))
                for h in range(NH):
                    ins = act.activation(ks[:, 0, (tau * NH + h) * P:(tau * NH + h + 1) * P],
                                         side(key)[:, h * P:(h + 1) * P], ACT.Square,
                                         accum_out=mstat[:, 2, NH * tau + h:NH * tau + h + 1])
                ins.then_inc(hgrn_squared, 1)
            for j in range(4):
                hi_of("mxT", j, act_hi[:, 2 * j:2 * j + 2, :])
            post("post_m", "mixo", 2, "pre3", 16)
            feed_forward(1, "pre3", "f2i")
            post("post_f2", "f2o", 3)

        @block.gpsimd
        def _(pool):
            def spread_row(dst, name):
                r = ROWS.index(name)
                pool.dma_start(dst, rows[r, :].partition_broadcast(P)).then_inc(row_loaded[name], 16)

            def power(dst, src, ready, count):
                pool.wait_ge(ready, count)
                n = dst.shape[-1]
                return pool.tensor_tensor(dst, src, half_power[:, 0:n], ALU.pow)

            def norm(name):
                ss, var, rstd = sums(name)
                n = PRES.index(name) + 1
                pool.wait_ge(ss_ready, SUMS_BEFORE[name] + 2)
                pool.tensor_scalar(var, ss[:, 0:2], 1.0 / D, 1e-6, ALU.mult, ALU.add).then_inc(pre_var_ready, 1)
                power(rstd, var, pre_var_ready, n).then_inc(pre_rstd_ready, 1)

            spread_row(gate_bc[:], "b_gate")
            pool.memset(half_power[:], -0.5).then_inc(half_ready, 1)
            pool.wait_ge(half_ready, 1)
            norm("pre0")
            pool.memset(ones, 1.0).then_inc(ones_ready, 1)
            pool.wait_ge(pos_loaded, 16)
            pool.wait_ge(freq_loaded, 16)
            pool.tensor_copy(pos_f[:], pos_i[:]).then_inc(trig_step, 1)
            pool.wait_ge(trig_step, 1)
            for tau in range(NT):
                for w in range(2):
                    ins = pool.tensor_scalar(ang[:, tau, w, :], inv_freq[:], pos_f[:, tau:tau + 1], None, ALU.mult)
            ins.then_inc(trig_step, 1)
            pool.wait_ge(trig_step, 2)
            pool.tensor_scalar(turns[:, :, 0, :], ang[:, :, 0, :], 1 / TWO_PI, 0.25, ALU.mult, ALU.add)
            pool.tensor_scalar(turns[:, :, 1, :], ang[:, :, 1, :], 1 / TWO_PI, None, ALU.mult).then_inc(trig_step, 1)
            for n, value in enumerate((ROUND, -ROUND)):
                pool.wait_ge(trig_step, 3 + n)
                pool.tensor_scalar(turns[:], turns[:], value, None, ALU.add).then_inc(trig_step, 1)
            for n, value in enumerate((TWO_PI_1, TWO_PI_2, TWO_PI_3)):
                pool.wait_ge(trig_step, 5 + 2 * n)
                pool.tensor_scalar(part, turns[:], value, None, ALU.mult).then_inc(trig_step, 1)
                pool.wait_ge(trig_step, 6 + 2 * n)
                pool.tensor_tensor(ang[:], ang[:], part, ALU.subtract).then_inc(trig_step, 1)
            pool.wait_ge(trig_step, 11)
            pool.tensor_scalar(ang[:, :, 0, :], ang[:, :, 0, :], TWO_PI / 4, None, ALU.add).then_inc(trig_step, 1)
            pool.wait_ge(trig_step, 12)
            pool.tensor_scalar(ang[:], ang[:], PI_INSIDE, -PI_INSIDE, ALU.min, ALU.max).then_inc(trig_step, 1)
            pool.wait_ge(trig_ready, 1)
            pool.wait_ge(act0_ready, 4)
            pool.memset(a_T[:, :, 0:CW - 1], 0.0).then_inc(pad_ready, 1)
            def post_norm(name, before):
                _, var, rstd = sums(name)
                for tau in range(NT):
                    power(rstd[:, tau:tau + 1], var[:, tau:tau + 1], post_var_ready, 3 * before + tau + 2
                          ).then_inc(post_rstd_ready, 1)

            def gate_w(k):
                return (z, g)[k // 4][:, k % 4 // 2, k % 2, :]

            for k in range(KD + 1):
                if k < KD:
                    pool.wait_ge(w_used, 4 * k + 1)
                    pool.dma_start(gate_w(k), ada_gate[k]).then_inc(gate_w_loaded[k], 16)
                if k == 1:
                    pool.wait_ge(gate_w_loaded[0], 16)
                    pool.tensor_scalar(gate_sum, gate_w(0), cv("c", 0), None, ALU.mult).then_inc(gate_summed, 1)
                elif k:
                    pool.wait_ge(gate_w_loaded[k - 1], 16)
                    pool.tensor_scalar(gate_w(k - 1), gate_w(k - 1), cv("c", k - 1), None, ALU.mult
                                       ).then_inc(gate_scaled, 1)
                    pool.wait_ge(gate_scaled, k - 1)
                    pool.wait_ge(gate_summed, k - 1)
                    pool.tensor_tensor(gate_sum, gate_sum, gate_w(k - 1), ALU.add).then_inc(gate_summed, 1)
            for b in range(first("qk"), first("qk") + 4):
                pool.wait_ge(*drained(b))
            n = 0
            for w in range(2):
                for tau in range(NT):
                    t = qkv[:, w, tau, :].rearrange("p (h u f) -> p u h f", h=RH, u=2)
                    cos = trig[:, tau, 0, :].unsqueeze(1).to_broadcast([P, RH, P])
                    sin = trig[:, tau, 1, :].unsqueeze(1).to_broadcast([P, RH, P])
                    if n:
                        pool.wait_ge(rotated, n)
                    pool.tensor_tensor(rot[:, 0], t[:, 0], sin, ALU.mult)
                    pool.tensor_tensor(rot[:, 1], t[:, 1], sin, ALU.mult).then_inc(rot_step, 1)
                    pool.wait_ge(rot_step, 2 * n + 1)
                    pool.tensor_tensor(t[:, 0], t[:, 0], cos, ALU.mult)
                    pool.tensor_tensor(t[:, 1], t[:, 1], cos, ALU.mult).then_inc(rot_step, 1)
                    pool.wait_ge(rot_step, 2 * n + 2)
                    pool.tensor_tensor(t[:, 0], t[:, 0], rot[:, 1], ALU.subtract)
                    pool.tensor_tensor(t[:, 1], t[:, 1], rot[:, 0], ALU.add).then_inc(rotated, 1)
                    n += 1
            for h in range(RH):
                for tau in range(NT):
                    n = NT * h + tau
                    pool.wait_ge(head_var, n + 1)
                    pool.tensor_scalar(head_stat[:, n, 8:9], head_stat[:, n, 7:8], 1e-5, None, ALU.add
                                       ).then_inc(head_eps, 1)
                    power(head_stat[:, n, 9:10], head_stat[:, n, 8:9], head_eps, n + 1
                          ).then_inc(head_rstd, 1)
                for tau in range(NT):
                    pool.wait_ge(*freed(("ro", h, tau)))
                    y = qkv[:, 0:2, tau, h * 256:(h + 1) * 256]
                    zh = z[:, h // 2, tau, (h % 2) * CB:(h % 2 + 1) * CB].rearrange("p (a c) -> p a c", a=2)
                    pool.tensor_tensor(y, y, zh, ALU.mult).then_inc(ret_ready, 1)
            pool.wait_ge(*freed(("rs", RH - 1)))
            spread_row(spread[:, 0, :], "ln_g")
            spread_row(spread[:, 1, :], "ln_b")
            for tau in range(NT):
                pool.wait_ge(ln_var, tau + 1)
                pool.tensor_scalar(ln_stat[:, tau, 14:15], ln_stat[:, tau, 13:14], 1e-5, None, ALU.add
                                   ).then_inc(ln_eps, 1)
                power(ln_stat[:, tau, 15:16], ln_stat[:, tau, 14:15], ln_eps, tau + 1).then_inc(ln_rstd, 1)
            pool.wait_ge(ln_step, 4 * NT)
            spread_row(spread[:, 0, :], "post_g")
            spread_row(spread[:, 1, :], "post0")
            pool.wait_ge(conv_act_ready, NT)
            pool.dma_start(x[:], x_in.rearrange("(t p) d -> p t d", p=P)).then_inc(x_again, 16)
            pool.wait_ge(row_loaded["post_g"], 16)
            pool.wait_ge(*freed(("gate", 1)))
            pool.tensor_tensor(gate_bc[:], gate_bc[:], spread[:, 0, :], ALU.mult).then_inc(factor_ready, 1)
            pool.wait_ge(row_loaded["post0"], 16)
            pool.tensor_scalar(spread[:, 1, :], spread[:, 1, :], 0.5, None, ALU.mult).then_inc(factor_ready, 1)
            pool.wait_ge(factor_ready, 1)
            spread_row(spread[:, 0, :], "mix_norm")
            post_norm("post_w", 0)
            norm("pre1")
            post_norm("post_f1", 1)
            pool.wait_ge(ss_ready, SUMS_BEFORE["post_f1"] + 4)
            for dst, src, loaded in ((gw[:], gates_w, gw_loaded), (gbias[:], gate_bias.partition_broadcast(P), gbias_loaded),
                                   (qs[:, 0, :], level_in, level_loaded),
                                   (causal[:], causal_in, causal_loaded), (sel[:], sel_in, sel_loaded)):
                pool.dma_start(dst, src).then_inc(loaded, 16)
            pool.memset(hsc[:], 0.0).then_inc(hsc_clear, 1)
            pool.memset(mqk_pad[:, :, 0:CW2 - 1], 0.0).then_inc(mqk_pad_ready, 1)
            pool.memset(mv[:, :, :, P:P + 1], 1.0).then_inc(mv_ones, 1)
            norm("pre2")
            pool.wait_ge(pre_rstd_ready, 3)
            pool.tensor_scalar(half_rstd[:], sums("pre2")[2], 0.5, None, ALU.mult).then_inc(half_rstd_ready, 1)
            pool.wait_ge(level_loaded, 16)
            pool.tensor_copy(level[:], qs[:, 0, :].rearrange("p (l t) -> p l t", l=8)).then_inc(level_ready, 1)
            pool.memset(keep, 1.0).then_inc(keep_step, 1)
            pool.wait_ge(keep_step, 1)
            pool.memset(keep[:, :, 0:S:CHUNK], 0.0).then_inc(keep_step, 1)
            pool.wait_ge(log_f_ready, 1)
            pool.tensor_scalar(hk_T[:], hk_T[:], -1.0, 1.0, ALU.mult, ALU.add).then_inc(hk_T_ready, 1)
            pool.wait_ge(exp_ready, 1)
            pool.wait_ge(hk_T_ready, 1)
            pool.tensor_tensor(ks[:, 1, :], hk_T[:].rearrange("p h s -> p (h s)"),
                               decays(1).rearrange("p h s -> p (h s)"), ALU.mult).then_inc(k_scaled, 1)
            pool.wait_ge(mw_exp, 1)
            pool.wait_ge(causal_loaded, 16)
            mask = causal[:].unsqueeze(1).to_broadcast([P, NH, P])
            pool.tensor_tensor(mw[:, :, 0:P], mw[:, :, 0:P], mask, ALU.mult)
            pool.tensor_tensor(mw[:, :, S:S + P], mw[:, :, S:S + P], mask, ALU.mult).then_inc(mw_masked, 1)
            mix = first("mixi")

            def level_scale_k(lv):
                pool.wait_ge(exp_ready, lv)
                if lv >= 3:
                    pool.wait_ge(*full(("lv", lv - 2, 1)))
                pool.tensor_tensor(ks[:, lv % 2, :], hk_T[:].rearrange("p h s -> p (h s)"),
                                   decays(lv).rearrange("p h s -> p (h s)"), ALU.mult).then_inc(k_scaled, 1)

            def mix_rsqrt(n, cs, ready, count):
                slot = 2 * (n > 0)
                pool.wait_ge(ready, count)
                pool.tensor_scalar(mstat[:, slot + 1, cs], mstat[:, slot, cs], 1.0 / P, 1e-6, ALU.mult, ALU.add
                                   ).then_inc(mix_var, 1)
                power(mstat[:, 4 + slot // 2, cs], mstat[:, slot + 1, cs], mix_var, n + 1).then_inc(mix_rstd, 1)

            hg_n = spread[:, 0, 0:CB].unsqueeze(1).to_broadcast([P, NT, CB])
            ml_n = spread[:, 0, CB:D].unsqueeze(1).to_broadcast([P, NT, CB])
            pool.wait_ge(hk_T_ready, 1)
            for lv in range(2, 7):
                level_scale_k(lv)
            pool.wait_ge(row_loaded["mix_norm"], 16)
            pool.wait_ge(*drained(mix + 5))
            pool.tensor_scalar(mo[:], mo[:], 0.5, 0.5, ALU.mult, ALU.add).then_inc(mo_step, 1)
            pool.wait_ge(mo_step, 1)
            pool.tensor_tensor(mo[:], mo[:], ml_n, ALU.mult).then_inc(gates_scaled, 1)
            level_scale_k(7)
            level_scale_k(8)
            mix_rsqrt(0, slice(0, NT * NH), mix_ss, 1)
            pool.wait_ge(*drained(mix + 6))
            pool.tensor_tensor(hgate[:], hgate[:], hg_n, ALU.mult).then_inc(gates_scaled, 1)
            for tau in range(NT):
                mix_rsqrt(1 + tau, slice(NH * tau, NH * (tau + 1)), hgrn_squared, tau + 1)
            pool.wait_ge(gates_scaled, 2)
            spread_row(spread[:, 1, :], "post1")
            spread_row(spread[:, 0, :], "post2")
            pool.wait_ge(row_loaded["post2"], 16)
            pool.tensor_scalar(spread[:, 0, :], spread[:, 0, :], 0.5, None, ALU.mult).then_inc(factor_ready, 1)
            post_norm("post_m", 2)
            norm("pre3")
            post_norm("post_f2", 3)

        @block.vector
        def _(dve):
            def lo_part(n, off=None):
                dve.wait_ge(w_hi_ready, plus(n + 1, off, LOOP_GROUPS))
                dve.tensor_tensor(w_lo[:, n % RING, :], raw[:, n % RAW, :], w_hi[:, n % RING, :].bitcast(F32),
                                  ALU.subtract).then_inc(w_lo_ready, 1)

            def lo_parts(b, off=None):
                for n in range(split_to(b - 1), split_to(b)):
                    lo_part(n, off)

            def lo_of(key, j, dst, hi, count, scale=1.0):
                dve.wait_ge(act_hi_ready, count)
                src = side((key, j))[:].rearrange("p (k s) -> p k s", s=S)
                if scale == 1.0:
                    ins = dve.tensor_tensor(dst, src, hi.bitcast(F32), ALU.subtract)
                else:
                    ins = dve.scalar_tensor_tensor(dst, src, scale, hi.bitcast(F32), ALU.mult, ALU.subtract)
                ins.then_inc(side_free((key, j)), 1)

            def lo_scaled(key, tau, at):
                before = HI_BEFORE[key] + 8 * tau
                for k in range(8):
                    half, n = divmod(k, 4)
                    ts_ = slice(tau * P, (tau + 1) * P)
                    dve.wait_ge(act_hi_ready, before + 4 * half + 4)
                    ins = dve.scalar_tensor_tensor(act_lo[:, k, ts_], side((key, tau, half))[:, n * P:(n + 1) * P],
                                                   cv("pre2", at + k), act_hi[:, k, ts_].bitcast(F32),
                                                   ALU.mult, ALU.subtract)
                    if n == 1:
                        ins.then_inc(x_half_ready, 1)
                    if n == 3:
                        ins.then_inc(side_free((key, tau, half)), 1)

            dve.wait_ge(pre_rstd_ready, 1)
            for tau in range(NT):
                dve.tensor_scalar(tmp[:, tau, :], x[:, tau, :], sums("pre0")[2][:, tau:tau + 1], None,
                                  ALU.mult).then_inc(normed, 1)
            dve.wait_ge(col_loaded, 16)
            for r in range(ROUNDS):
                ada_sum = h_T[:, 2 * r:2 * r + 2, :].rearrange("p k s -> p (k s)")
                for k in range(SUMMED):
                    if k % (KD // 2) == 0:
                        dve.wait_ge(ada_loaded[2 * r + k // (KD // 2)], 16)
                    if k == 0:
                        ins = dve.tensor_scalar(ada_sum, ada_w[:, r, 0, :], cv("c", 0), None, ALU.mult)
                    else:
                        dve.wait_ge(ada_summed, SUMMED * r + k)
                        ins = dve.scalar_tensor_tensor(ada_sum, ada_w[:, r, k, :], cv("c", k), ada_sum, ALU.mult, ALU.add)
                    ins.then_inc(ada_summed, 1)
                lo_part(2 * r)
                shift, scale = slice(4 * r, 4 * r + 2), slice(4 * r + 2, 4 * r + 4)
                dve.wait_ge(*full(("mod", r)))
                dve.tensor_tensor(mod_T[:, 4 * r:4 * r + 4], side(("mod", r))[:, 0:4], cv("b_mod", 4 * r, 4), ALU.add
                                  ).then_inc(side_free(("mod", r)), 1)
                dve.wait_ge(*freed(("mod", r)))
                dve.scalar_tensor_tensor(mod_T[:, scale], mod_T[:, scale], 1.0, cv("pre_g", 2 * r, 2), ALU.add, ALU.mult
                                         ).then_inc(mod_ready, 1)
                dve.wait_ge(*freed(("pre0", r)))
                dve.wait_ge(mod_ready, r + 1)
                for n in range(2):
                    k = 2 * r + n
                    ins = dve.tensor_scalar(h_T[:, k, :], tmp_T[:, k, :], mod_T[:, 4 * r + 2 + n:4 * r + 3 + n],
                                            mod_T[:, 4 * r + n:4 * r + n + 1], ALU.mult, ALU.add)
                ins.then_inc(h_T_ready, 1)
                lo_part(2 * r + 1)
                dve.wait_ge(act_hi_ready, r + 1)
                dve.wait_ge(h_T_ready, r + 1)
                dve.tensor_tensor(act_lo[:, 2 * r:2 * r + 2, :], h_T[:, 2 * r:2 * r + 2, :],
                                  act_hi[:, 2 * r:2 * r + 2, :].bitcast(F32), ALU.subtract).then_inc(act0_ready, 1)
            for b in range(4):
                if b == 0:
                    lo_parts(1)
                if b >= 2:
                    lo_parts(b)
                for tau in range(NT):
                    dve.wait_ge(tanh_ready, 2 * b + tau + 1)
                    ins = dve.scalar_tensor_tensor(tmp[:, tau, b * 256:(b + 1) * 256], tanh_u[:, tau, :], 1.0,
                                                   part_of(b, tau)[:, 0:256], ALU.add, ALU.mult)
                ins.then_inc(pair_free(b), 1)

            def conv_taps(tile, taps, before):
                acc = (tmp_T[:, tile, :], odd_taps)
                for t in taps:
                    src = a_T[:, tile, t:t + S]
                    w = conv_w[:, bass.ds(tile, 1), t:t + 1]
                    if t >= 2:
                        dve.wait_ge(conv_step, before + (t - 1))
                    else:
                        dve.wait_ge(conv_step, before)
                    if t == 0:
                        ins = dve.tensor_scalar(acc[0], src, w, conv_b[:, bass.ds(tile, 1)], ALU.mult, ALU.add)
                    elif t == 1:
                        ins = dve.tensor_scalar(acc[1], src, w, None, ALU.mult)
                    else:
                        ins = dve.scalar_tensor_tensor(acc[t % 2], src, w, acc[t % 2], ALU.mult, ALU.add)
                    ins.then_inc(conv_step, 1)
                if taps[-1] == CW - 1:
                    dve.wait_ge(conv_step, before + CW)
                    dve.tensor_tensor(acc[0], acc[0], acc[1], ALU.add).then_inc(conv_step, 1)

            conv_w = cv("conv_w", 0, KD * CW).rearrange("p (k t) -> p k t", t=CW)
            conv_b = cv("conv_b", 0, KD)
            dve.memset(odd_taps, 0.0).then_inc(conv_step, 1)
            first_taps, last_taps = list(range(16)), list(range(16, CW))
            for j in range(4):
                dve.wait_ge(*freed(("aT", j)))
            with dve.Fori(0, 4) as i:
                for n, taps in enumerate((first_taps, last_taps)):
                    lo_parts(first("qk") + n, i)
                    conv_taps(i, taps, i * (CW + 1) + 1)
            dve.wait_ge(row_loaded["b_gate"], 16)
            for j in range(2):
                dve.wait_ge(*full(("gate", j)))
                cs = slice(j * CB, (j + 1) * CB)
                dve.tensor_tensor(gate_bc[:, cs], gate_bc[:, cs], side(("gate", j))[:], ALU.add
                                  ).then_inc(side_free(("gate", j)), 1)
            with dve.Fori(0, 2) as i:
                for n, taps in enumerate((first_taps, last_taps)):
                    lo_parts(first("z") + n, i)
                    conv_taps(i + 4, taps, (i + 4) * (CW + 1) + 1)

            def head_mask(h):
                dve.wait_ge(*full(("rs", h)))
                dve.tensor_tensor(masked[:, h % 2, :], side(("rs", h))[:, 0:3 * P], decay[:, h, :], ALU.mult
                                  ).then_inc(side_free(("rs", h)), 1)

            def head_stats(h):
                for tau in range(NT):
                    n = NT * h + tau
                    dve.wait_ge(*full(("ro", h, tau)))
                    dve.bn_stats(head_stat[:, n, 0:6], side(("ro", h, tau))[:]).then_inc(head_bn, 1)
                for tau in range(NT):
                    n = NT * h + tau
                    dve.wait_ge(head_bn, n + 1)
                    dve.bn_aggr(head_stat[:, n, 6:8], head_stat[:, n, 0:6]).then_inc(head_var, 1)

            def head_norm(h):
                for tau in range(NT):
                    n = NT * h + tau
                    dve.wait_ge(head_rstd, n + 1)
                    dve.tensor_scalar(qkv[:, 0:2, tau, h * 256:(h + 1) * 256],
                                      side(("ro", h, tau))[:].rearrange("p (a c) -> p a c", a=2),
                                      head_stat[:, n, 6:7], head_stat[:, n, 9:10], ALU.subtract, ALU.mult
                                      ).then_inc(side_free(("ro", h, tau)), 1)

            dve.wait_ge(decay_loaded, 16)
            for m in range(6):
                b = first("zc") + m
                half = (split_to(b - 1) + split_to(b)) // 2
                if m >= 2:
                    head_stats(m - 2)
                for n in range(split_to(b - 1), half):
                    lo_part(n)
                if m >= 2:
                    head_norm(m - 2)
                for n in range(half, split_to(b)):
                    lo_part(n)
                if 1 <= m <= 4:
                    head_mask(m - 1)
                if m < 4:
                    conv_taps(6 + m // 2, last_taps if m % 2 else first_taps, (6 + m // 2) * (CW + 1) + 1)
            for j in range(8):
                lo_of("retT", j, ret_lo[:, 2 * j:2 * j + 2, :], ret_hi[:, 2 * j:2 * j + 2, :], HI_BEFORE["retT"] + j + 1)
            lo_parts(first("ret"))
            for tau in range(NT):
                for half in range(2):
                    key = ("cvtok", 2 * tau + half)
                    dve.wait_ge(*full(key))
                    dve.bn_stats(ln_stat[:, tau, 6 * half:6 * half + 6], side(key)[:]).then_inc(ln_bn, 1)
            for tau in range(NT):
                dve.wait_ge(ln_bn, 2 * tau + 2)
                dve.bn_aggr(ln_stat[:, tau, 12:14], ln_stat[:, tau, 0:12]).then_inc(ln_var, 1)
            for tau in range(NT):
                dve.wait_ge(ln_rstd, tau + 1)
                for half in range(2):
                    key = ("cvtok", 2 * tau + half)
                    dve.tensor_scalar(tmp[:, tau, half * CB:(half + 1) * CB], side(key)[:], ln_stat[:, tau, 12:13],
                                      ln_stat[:, tau, 15:16], ALU.subtract, ALU.mult).then_inc(side_free(key), 1)
            dve.wait_ge(row_loaded["ln_g"], 16)
            dve.wait_ge(row_loaded["ln_b"], 16)
            for tau in range(NT):
                dve.wait_ge(*freed(("cvtok", 2 * tau + 1)))
                dve.tensor_tensor(tmp[:, tau, :], tmp[:, tau, :], spread[:, 0, :], ALU.mult).then_inc(ln_step, 3)
            for tau in range(NT):
                dve.wait_ge(ln_step, 3 * (tau + 1))
                dve.tensor_tensor(tmp[:, tau, :], tmp[:, tau, :], spread[:, 1, :], ALU.add).then_inc(ln_step, 1)

            def branch(b, which, c):
                dve.wait_ge(*done(b))
                for tau in range(NT):
                    dst = g[:, which, tau, c * CB:(c + 1) * CB]
                    ins = dve.scalar_tensor_tensor(dst, dst, 1.0, part_of(b, tau)[:], ALU.add, ALU.mult)
                ins.then_inc(pair_free(b), 1)

            def merge(c):
                dve.wait_ge(*drained(first("conv") + c))
                for tau in range(NT):
                    cs = slice(c * CB, (c + 1) * CB)
                    dve.tensor_tensor(g[:, 0, tau, cs], g[:, 0, tau, cs], g[:, 1, tau, cs], ALU.add
                                      ).then_inc(merged, 1)

            for tau in range(NT):
                dve.wait_ge(conv_silu, tau + 1)
                dve.tensor_tensor(tmp[:, tau, :], tmp[:, tau, :], x[:, tau, :], ALU.mult).then_inc(conv_act_ready, 1)
            branch(first("ret"), 0, 0)
            lo_parts(first("ret") + 1)
            for j in range(4):
                lo_of("cvT", j, act_lo[:, 2 * j:2 * j + 2, :], act_hi[:, 2 * j:2 * j + 2, :], HI_BEFORE["cvT"] + j + 1)
            branch(first("ret") + 1, 0, 1)
            lo_parts(first("conv"))
            branch(first("conv"), 1, 0)
            merge(0)
            lo_parts(first("conv") + 1)
            for j in range(4):
                if j == 2:
                    branch(first("conv") + 1, 1, 1)
                    merge(1)
                lo_of("mgT", j, ret_lo[:, 2 * j:2 * j + 2, :], ret_hi[:, 2 * j:2 * j + 2, :],
                      HI_BEFORE["mgT"] + j + 1, scale=0.5)

            def post(name, stage, factor, before, key=None, at=None):
                ss, var, rstd = sums(name)
                b = first(stage)
                left, right = slice(0, CB), slice(CB, D)
                lo_parts(b)
                dve.wait_ge(*done(b))
                dve.tensor_tensor(tmp[:, 1, left], part_of(b, 1)[:], factor[:, left], ALU.mult).then_inc(post_bank_read, 1)
                dve.wait_ge(ss_ready, SUMS_BEFORE[name] + 1)
                dve.tensor_tensor(tmp[:, 0, left], part_of(b, 0)[:], factor[:, left], ALU.mult).then_inc(pair_free(b), 1)
                dve.wait_ge(ss_ready, SUMS_BEFORE[name] + 2)
                dve.tensor_scalar(var, ss[:, 0:2], 1.0 / D, 1e-6, ALU.mult, ALU.add).then_inc(post_var_ready, 1)
                lo_parts(b + 1)
                dve.wait_ge(post_var_ready, 3 * before + 1)
                for tau in range(NT):
                    one = slice(tau, tau + 1)
                    dve.wait_ge(ss_ready, SUMS_BEFORE[name] + 3 + tau)
                    dve.scalar_tensor_tensor(var[:, one], ss[:, 2 + tau:3 + tau], 1.0 / D, var[:, one],
                                             ALU.mult, ALU.add).then_inc(post_var_ready, 1)
                    ins = dve.tensor_tensor(tmp[:, tau, right], part_of(b + 1, tau)[:], factor[:, right], ALU.mult)
                    ins.then_inc(pair_free(b + 1) if tau == 1 else post_bank_read, 1)
                    dve.wait_ge(post_rstd_ready, NT * before + tau + 1)
                    for c, cs in ((0, left), (1, right)):
                        if c == 0:
                            dve.wait_ge(*drained(b))
                        elif tau == 0:
                            dve.wait_ge(post_bank_read, 2 * before + 2)
                        else:
                            dve.wait_ge(*drained(b + 1))
                        dve.scalar_tensor_tensor(x[:, tau, cs], tmp[:, tau, cs], rstd[:, one], x[:, tau, cs],
                                                 ALU.mult, ALU.add).then_inc(x_ready, 1)
                    if key is not None:
                        lo_scaled(key, tau, at)

            def feed_forward(which, name, stage):
                b0 = first(stage)
                hi_before = HI_BEFORE[("ffT", which)]
                silu_before = which * 2 * FB

                def gate(b, parity, off=None):
                    for tau in range(NT):
                        dve.wait_ge(silu_ready, plus(silu_before + 2 * (b - b0) + tau + 1, off, 4))
                        ins = dve.scalar_tensor_tensor(ff_tok[:, parity, tau, :], part_of(b, tau)[:, 256:512],
                                                       sums(name)[2][:, tau:tau + 1], silu_g[:, tau, :],
                                                       ALU.mult, ALU.mult)
                    ins.then_inc(pair_free(b), 1)

                def hidden_lo(parity, j, count, off=None):
                    key = ("ffT", which, parity)
                    dve.wait_ge(act_hi_ready, count)
                    dve.tensor_tensor(ff_lo[:, j, :], side(key)[:], ff_hi[:, j, :].bitcast(F32), ALU.subtract
                                      ).then_inc(side_free(key), 1)

                lo_parts(b0)
                dve.wait_ge(pre_rstd_ready, 2 + 2 * which)
                gate(b0, 0)
                with dve.Fori(0, (FB - 1) // 2) as i:
                    for n in range(2):
                        lo_parts(b0 + 1 + n, i)
                        gate(b0 + 1 + n, 1 - n, i)
                        hidden_lo(n, 2 * i + n, plus(hi_before + n + 1, i, 2), i)
                hidden_lo(0, FB - 1, hi_before + FB)

            dve.wait_ge(x_again, 16)
            dve.wait_ge(factor_ready, 1)
            post("post_w", "wout", gate_bc[:], 0, "pre1", 0)
            feed_forward(0, "pre1", "f1i")
            dve.wait_ge(factor_ready, 2)
            post("post_f1", "f1o", spread[:, 1, :], 1, "pre2", 8)
            l0, l1 = cv("lb", 0, NH), cv("lb", NH, NH)
            dve.tensor_tensor(lb[:, 0, :], l0, l1, ALU.max).then_inc(lb_step, 1)
            dve.wait_ge(lb_step, 1)
            dve.tensor_tensor(lb[:, 1, :], l0, lb[:, 0, :], ALU.subtract).then_inc(lb_step, 1)
            dve.tensor_tensor(lb[:, 2, :], l1, lb[:, 0, :], ALU.subtract).then_inc(lb_step, 1)
            dve.wait_ge(gw_hi_ready, 1)
            dve.tensor_tensor(gw_lo[:], gw[:], gw_hi[:].bitcast(F32), ALU.subtract).then_inc(gw_ready, 2)
            dve.wait_ge(lb_exp, 1)
            dve.tensor_tensor(lb[:, 3, :], lb[:, 1, :], lb[:, 2, :], ALU.add).then_inc(lb_step, 1)
            dve.wait_ge(lb_step, 4)
            dve.reciprocal(lb[:, 3, :], lb[:, 3, :]).then_inc(lb_step, 1)
            dve.wait_ge(lb_step, 5)
            dve.tensor_tensor(lb[:, 4, :], lb[:, 1, :], lb[:, 3, :], ALU.mult).then_inc(lb_step, 1)
            dve.tensor_tensor(lb[:, 5, :], lb[:, 2, :], lb[:, 3, :], ALU.mult).then_inc(lb_step, 1)
            mix = first("mixi")
            lo_parts(mix)
            dve.wait_ge(*full("gate_rows"))
            dve.tensor_copy(gate_rows, side("gate_rows")[0:8, 0:S]).then_inc(side_free("gate_rows"), 1)
            dve.wait_ge(*full("gates"))
            dve.wait_ge(gbias_loaded, 16)
            dve.wait_ge(pre_rstd_ready, 3)
            for tau in range(NT):
                ins = dve.scalar_tensor_tensor(gt[:, tau, :], side("gates")[:, 8 * tau:8 * tau + 8],
                                               sums("pre2")[2][:, tau:tau + 1], gbias[:], ALU.mult, ALU.add)
            ins.then_inc(side_free("gates"), 1)
            lo_parts(mix + 1)
            dve.wait_ge(lb_step, 7)
            for j in range(2):
                dve.wait_ge(*full(("hfT", j)))
                for h in (2 * j, 2 * j + 1):
                    ins = dve.tensor_scalar(hk_T[:, h, :], side(("hfT", j))[:, (h % 2) * S:(h % 2 + 1) * S],
                                            lb[:, 5, h:h + 1], lb[:, 4, h:h + 1], ALU.mult, ALU.add)
                ins.then_inc(side_free(("hfT", j)), 1)
            lo_parts(mix + 2)
            dve.wait_ge(log_f_ready, 1)
            dve.wait_ge(keep_step, 2)
            dve.tensor_tensor_scan(cum[:].rearrange("p h s -> p (h s)"), keep.rearrange("p h s -> p (h s)"),
                                   dec[:].rearrange("p h s -> p (h s)"), 0.0, ALU.mult, ALU.add
                                   ).then_inc(cum_ready, 1)

            def level_diff(lv):
                n = 2 ** (lv - 1)
                if lv <= 2:
                    dve.wait_ge(cum_ready, 1)
                else:
                    dve.wait_ge(q_scaled, lv - 2)
                    dve.wait_ge(k_scaled, lv - 2)
                if lv <= 6:
                    c = cum[:].rearrange("p h (b a n) -> p (h b) a n", a=2, n=n)
                    d = decays(lv).rearrange("p h (b a n) -> p (h b) a n", a=2, n=n)
                    middle = c[:, :, 0, n - 1:n].to_broadcast([P, NH * S // (2 * n), n])
                    dve.tensor_tensor(d[:, :, 1, :], c[:, :, 1, :], middle, ALU.subtract)
                    ins = dve.tensor_tensor(d[:, :, 0, :], middle, c[:, :, 0, :], ALU.subtract)
                else:
                    c = cum[:].rearrange("p h (b n) -> p h b n", n=CHUNK)
                    d = decays(lv).rearrange("p h (b n) -> p h b n", n=CHUNK)

                    def chunk_sum(b):
                        return c[:, :, b, CHUNK - 1:CHUNK].to_broadcast([P, NH, CHUNK])

                    if lv == 7:
                        for b in (0, 2):
                            dve.tensor_tensor(d[:, :, b, :], chunk_sum(b), c[:, :, b, :], ALU.subtract)
                            ins = dve.tensor_copy(d[:, :, b + 1, :], c[:, :, b + 1, :])
                    else:
                        dve.tensor_tensor(d[:, :, 0, :], chunk_sum(0), c[:, :, 0, :], ALU.subtract)
                        dve.tensor_tensor(d[:, :, 1, :], chunk_sum(1), c[:, :, 1, :], ALU.subtract)
                        dve.tensor_copy(d[:, :, 2, :], c[:, :, 2, :])
                        dve.tensor_tensor(d[:, :, 3, :], c[:, :, 3, :], chunk_sum(2), ALU.add
                                          ).then_inc(diff_part, 1)
                        dve.wait_ge(diff_part, 1)
                        ins = dve.tensor_tensor(d[:, :, 0, :], d[:, :, 0, :], chunk_sum(1), ALU.add)
                ins.then_inc(diff_ready, 1)

            def level_scale_q(lv):
                dve.wait_ge(exp_ready, lv)
                dve.tensor_tensor(qs[:, lv % 2, :], hq_T[:].rearrange("p h s -> p (h s)"),
                                  decays(lv).rearrange("p h s -> p (h s)"), ALU.mult).then_inc(q_scaled, 1)

            def level_take(lv):
                for blk in range(NT):
                    key = ("lv", lv, blk)
                    dve.wait_ge(*full(key))
                    if lv:
                        dve.wait_ge(*freed(("lv", lv - 1, blk)))
                    dve.copy_predicated(hsc[:, blk, :, :], level[:, lv, :].unsqueeze(1).to_broadcast([P, NH, P]),
                                        side(key)[:].rearrange("p (h t) -> p h t", h=NH)).then_inc(side_free(key), 1)

            level_diff(1)
            dve.wait_ge(row_step, 3)
            i_row, f_row = side("gatesT")[0:NH, 0:S], side("gatesT")[0:NH, S:2 * S]
            dve.scalar_tensor_tensor(row[:, 0, :], f_row, 0.0, row[:, 2, :], ALU.min, ALU.subtract
                                     ).then_inc(row_step, 1)
            dve.wait_ge(row_step, 4)
            dve.tensor_tensor_scan(row[:, 1, :], row[:, 0, :], row[:, 0, :], 0.0, ALU.add, ALU.min
                                   ).then_inc(row_step, 1)
            dve.wait_ge(row_step, 5)
            dve.tensor_tensor(row[:, 0, :], i_row, row[:, 1, :], ALU.subtract).then_inc(side_free("gatesT"), 1)
            dve.wait_ge(*freed("gatesT"))
            dve.tensor_tensor_scan(row[:, 2, :], row[:, 0, :], row[:, 0, :], 0.0, ALU.max, ALU.max
                                   ).then_inc(row_step, 1)
            dve.wait_ge(row_step, 6)
            dve.tensor_tensor(row[:, 3, :], row[:, 1, :], row[:, 2, :], ALU.add).then_inc(row_step, 1)
            level_diff(2)
            lo_parts(mix + 3)
            dve.wait_ge(*freed("umT"))
            for j in range(2):
                dve.wait_ge(*full(("mb", j)))
                for n in range(2):
                    h = 2 * j + n
                    m_all = side(("mb", j))[:, n * S:(n + 1) * S]
                    dve.tensor_scalar(mw[:, h, 0:S], m_all, um[:, h:h + 1], 0.0, ALU.subtract, ALU.max)
                    ins = dve.tensor_scalar(mw[:, h, S:S + P], m_all[:, P:S], um[:, 4 + h:5 + h], 0.0,
                                            ALU.subtract, ALU.max)
                ins.then_inc(side_free(("mb", j)), 1)
            dve.wait_ge(hsc_clear, 1)
            dve.wait_ge(level_ready, 1)
            level_scale_q(1)
            level_diff(3)
            lo_parts(mix + 4)
            level_take(0)
            level_scale_q(2)
            level_diff(4)
            for j in range(2):
                dve.wait_ge(*freed(("cv2T", j)))
            for t in range(CW2):
                for k in range(4):
                    w = cv("conv_w2", k * CW2 + t)
                    if t:
                        dve.wait_ge(conv2_step, 4 * (t - 1) + k + 1)
                        ins = dve.scalar_tensor_tensor(mqk_T[:, k, :], mqk_pad[:, k, t:t + S], w, mqk_T[:, k, :],
                                                       ALU.mult, ALU.add)
                    else:
                        ins = dve.tensor_scalar(mqk_T[:, k, :], mqk_pad[:, k, 0:S], w, cv("conv_b2", k),
                                                ALU.mult, ALU.add)
                    ins.then_inc(conv2_step, 1)
            level_take(1)
            level_scale_q(3)
            level_diff(5)
            lo_parts(mix + 5)
            level_take(2)
            level_take(3)
            level_scale_q(4)
            level_diff(6)
            dve.wait_ge(mw_masked, 1)
            for h in range(NH):
                dve.wait_ge(*full(("ms", h)))
                dve.scalar_tensor_tensor(mw[:, h, :], side(("ms", h))[:, 0:3 * P], QK ** -0.5, mw[:, h, :],
                                         ALU.mult, ALU.mult).then_inc(side_free(("ms", h)), 1)
            level_scale_q(5)
            level_diff(7)
            level_take(4)
            level_scale_q(6)
            lo_parts(mix + 6)
            level_diff(8)
            level_take(5)
            level_scale_q(7)
            level_take(6)
            level_scale_q(8)
            for tau in range(NT):
                for j in range(2):
                    key = ("mn", tau, j)
                    dve.wait_ge(*full(key))
                    n = 4 * tau + 2 * j
                    den = side(key)[:, 0:2 * (P + 1)].rearrange("p (h d) -> p h d", h=2)[:, :, P]
                    dve.scalar_tensor_tensor(mden[:, 0, n:n + 2], den, -1.0, um[:, 8 + n:10 + n], ALU.mult, ALU.max
                                             ).then_inc(mden_step, 1)
                    dve.wait_ge(mden_step, n + 1)
                    dve.tensor_tensor(mden[:, 0, n:n + 2], den, mden[:, 0, n:n + 2], ALU.max
                                      ).then_inc(mden_step, 1)
            dve.wait_ge(mden_step, 8)
            dve.reciprocal(mden[:, 1, :], mden[:, 0, :]).then_inc(mden_step, 1)
            dve.wait_ge(mden_step, 9)
            for tau in range(NT):
                for j in range(2):
                    key = ("mn", tau, j)
                    n = 4 * tau + 2 * j
                    num = side(key)[:, 0:2 * (P + 1)].rearrange("p (h d) -> p h d", h=2)[:, :, 0:P]
                    dst = tmp[:, tau, 2 * j * P:2 * (j + 1) * P].rearrange("p (h d) -> p h d", h=2)
                    dve.tensor_tensor(dst, num, mden[:, 1, n:n + 2].unsqueeze(2).to_broadcast([P, 2, P]), ALU.mult
                                      ).then_inc(side_free(key), 1)
            dve.wait_ge(mix_sq, 1)
            dve.tensor_reduce(mstat[:, 0, :].rearrange("p (t h) -> p t h", t=NT),
                              tmp[:, :, CB:D].rearrange("p t (h d) -> p t h d", d=P), AX.X, ALU.add).then_inc(mix_ss, 1)
            level_take(7)
            dve.wait_ge(*full(("lv", 8, 0)))
            dve.tensor_copy(hoff[:], side(("lv", 8, 0))[:].rearrange("p (h t) -> p h t", h=NH)
                            ).then_inc(side_free(("lv", 8, 0)), 1)
            dve.wait_ge(mix_rstd, 1)
            for tau in range(NT):
                o = tmp[:, tau, 0:CB].rearrange("p (h d) -> p h d", d=P)
                dve.tensor_tensor(o, o, mstat[:, 4, NH * tau:NH * (tau + 1)].unsqueeze(2).to_broadcast([P, NH, P]),
                                  ALU.mult).then_inc(mix_scaled, 1)
            dve.wait_ge(gates_scaled, 1)
            for tau in range(NT):
                dve.wait_ge(mix_scaled, tau + 1)
                dve.tensor_tensor(tmp[:, tau, 0:CB], tmp[:, tau, 0:CB], mo[:, tau, :], ALU.mult).then_inc(mixed, 1)
            dve.wait_ge(gates_scaled, 2)
            for tau in range(NT):
                dve.wait_ge(hgrn_squared, tau + 1)
                dve.tensor_tensor(qs[:, 0, tau * CB:(tau + 1) * CB], side(("ho", tau))[:], hgate[:, tau, :], ALU.mult
                                  ).then_inc(side_free(("ho", tau)), 1)
            for j in range(2):
                lo_of("mxT", j, act_lo[:, 2 * j:2 * j + 2, :], act_hi[:, 2 * j:2 * j + 2, :], HI_BEFORE["mxT"] + j + 1)
            for tau in range(NT):
                dve.wait_ge(mix_rstd, 2 + tau)
                dve.wait_ge(*freed(("ho", tau)))
                dve.tensor_tensor(tmp[:, tau, CB:D].rearrange("p (h d) -> p h d", d=P),
                                  qs[:, 0, tau * CB:(tau + 1) * CB].rearrange("p (h d) -> p h d", d=P),
                                  mstat[:, 5, NH * tau:NH * (tau + 1)].unsqueeze(2).to_broadcast([P, NH, P]),
                                  ALU.mult).then_inc(mixed, 1)
            for j in range(2, 4):
                lo_of("mxT", j, act_lo[:, 2 * j:2 * j + 2, :], act_hi[:, 2 * j:2 * j + 2, :], HI_BEFORE["mxT"] + j + 1)
            dve.wait_ge(row_loaded["post1"], 16)
            post("post_m", "mixo", spread[:, 1, :], 2, "pre3", 16)
            feed_forward(1, "pre3", "f2i")
            dve.wait_ge(factor_ready, 3)
            post("post_f2", "f2o", spread[:, 0, :], 3)


def kernel(**inputs):
    from concourse import bacc
    from concourse.bass_utils import run_bass_kernel_spmd

    a = {k: np.asarray(v) for k, v in inputs.items()}

    def units(w):
        k, n = w.shape
        return w.reshape(k // P, P, n // CB, CB).transpose(2, 0, 1, 3).reshape(-1, P, CB)

    def pairs(left, right):
        k, n = left.shape
        return np.stack([left.reshape(k, n // 256, 256), right.reshape(k, n // 256, 256)], axis=2).reshape(k, 2 * n)

    w_in = a["w_in"][0]
    q, k, v, z_ret, u_val, u_gate, z_conv, g_a, g_b = np.split(
        w_in, [1024, 2048, 4096, 6144, 7168, 8192, 9216, 10240], axis=1)
    mix_in = a["w_mix_in_2"][0]
    hq, hf, hi, hgate, mqk, mv, mo, gates = np.split(mix_in, [512, 1024, 1536, 2048, 2560, 3072, 3584], axis=1)
    u = units(pairs(u_val, u_gate))
    start = u[:2 * KD].reshape(2, KD, P, CB).transpose(1, 0, 2, 3).reshape(2 * KD, P, CB)
    all_units = np.concatenate([
        start, u[2 * KD:], units(q), units(k), units(v), units(z_ret), units(z_conv), units(g_a), units(g_b),
        units(a["w_ret_out"][0]), units(a["w_conv_out"][0]), units(a["w_out"][0]),
        units(pairs(a["ffn1_w_in_2"][0][:, :FF], a["ffn1_w_in_2"][0][:, FF:])), units(a["ffn1_w_out_2"][0]),
        units(hq), units(hf), units(mqk), units(mv), units(hi), units(mo), units(hgate),
        units(np.roll(a["w_mix_out_2"][0], CB, axis=0)),
        units(pairs(a["ffn2_w_in_2"][0][:, :FF], a["ffn2_w_in_2"][0][:, FF:])), units(a["ffn2_w_out_2"][0])])
    stream = np.ascontiguousarray(all_units.reshape(GROUPS, UPG, P, CB).transpose(0, 2, 1, 3)).reshape(
        GROUPS, P, UPG * CB)

    def columns(vec):
        return vec.reshape(-1, P).T

    def taps(w):
        return w.reshape(w.shape[0], -1, P).transpose(2, 1, 0).reshape(P, -1)

    b_ada = a["b_ada"][0]
    cols = np.ascontiguousarray(np.concatenate([
        columns(a["c"][0]), columns(a["pre_norm_g"][0]),
        columns(b_ada[:2 * D]).reshape(P, 2, ROUNDS, 2).transpose(0, 2, 1, 3).reshape(P, 2 * KD),
        columns(a["conv_b"][0]),
        taps(a["conv_w"][0]), columns(a["norm_pre_2"][0]), columns(a["hgrn_lb_logits_2"][:2]), taps(a["conv_w_2"][0]),
        columns(a["conv_b_2"][0])], axis=1))
    rows = np.ascontiguousarray(np.stack([
        b_ada[2 * D:], a["conv_ln_g"][0], a["conv_ln_b"][0], a["post_norm_g"][0], a["norm_post_2"][0, 0],
        np.concatenate([a["hgrn_norm_2"][0], a["mlstm_norm_2"][0]]), a["norm_post_2"][0, 1], a["norm_post_2"][0, 2]]))

    idx = np.arange(P)
    log_gamma = np.log1p(-np.exp2(-5.0 - np.arange(RH)))
    gap = idx[None, :] - idx[:, None]
    decay = np.zeros((P, RH, 3 * P))
    for h in range(RH):
        same = np.where(gap >= 0, np.exp(log_gamma[h] * np.maximum(gap, 0)), 0.0)
        decay[:, h] = np.concatenate([same, np.exp(log_gamma[h] * (gap + P)), same], axis=1) / 16.0
    levels = np.zeros((P, 8, P), np.float32)
    levels[:, 0] = gap == 0
    for lv in range(1, 8):
        size = 2 ** lv
        s_, t_ = idx[:, None], idx[None, :]
        levels[:, lv] = (s_ // size == t_ // size) & (s_ % size < size // 2) & (t_ % size >= size // 2)
    sel = np.zeros((NH, NH, P), np.float32)
    for h in range(NH):
        sel[h, h] = 1.0
    inv_freq = np.float32(10000.0) ** (-np.arange(P, dtype=np.float32) / np.float32(P))
    arrays = {
        "stream": stream,
        "ada": np.ascontiguousarray(a["w_ada"][0][:, :2 * D].reshape(KD, P, 2, ROUNDS, 2 * P).transpose(3, 1, 0, 2, 4)
                                    ).reshape(ROUNDS, P, KD * CB),
        "ada_gate": np.ascontiguousarray(a["w_ada"][0][:, 2 * D:].reshape(KD, P, D)),
        "gates_w": np.ascontiguousarray(gates.reshape(KD, P, 8).transpose(1, 0, 2).reshape(P, KD * 8)),
        "cols": cols, "rows": rows, "gate_bias": np.ascontiguousarray(a["mlstm_gate_bias_2"][0]),
        "x": np.ascontiguousarray(a["x"][0]),
        "pos": np.ascontiguousarray(a["positions"][0].reshape(NT, P).T),
        "ident": np.eye(P, dtype=np.float32),
        "inv_freq": np.ascontiguousarray(np.broadcast_to(inv_freq, (P, P))),
        "decay": decay.reshape(P, -1).astype(np.float32),
        "level": levels.reshape(P, -1),
        "causal": (gap >= 0).astype(np.float32),
        "sel": sel,
    }
    nc = bacc.Bacc("TRN2", target_bir_lowering=False, num_devices=1)
    args = [nc.dram_tensor(f"in_{n}", v.shape, mybir.dt.from_np(v.dtype), kind="ExternalInput").ap()
            for n, v in arrays.items()]
    args.append(nc.dram_tensor("out_x", (S, D), F32, kind="ExternalOutput").ap())
    build_program(nc, *args)
    r = run_bass_kernel_spmd(nc, [{f"in_{n}": v for n, v in arrays.items()}], core_ids=[0])
    return r.results[0]["out_x"].reshape(1, S, D)
```
